# Optimizing a Trainium2 kernel written in Bass

```python
import math
import jax
import jax.numpy as jnp
from jax import lax
import numpy as np
import jax, jax.numpy as jnp

D_MODEL = 1024
BATCH = 1
SEQ = 512
DEPTH = 1

CTX_LEN = 256
GRID_W = 64
HEAD_DIM = 128
N_HEADS_GDN = 4
N_HEADS_RET = 4
W_GDN = N_HEADS_GDN * HEAD_DIM
W_RET = N_HEADS_RET * HEAD_DIM
MIX_WIDTH = W_GDN + W_RET
IN_COLS = 4 * W_GDN + 4 * N_HEADS_GDN + 4 * W_RET
CONV_K = 5
CHUNK = 64
D_FF = ((8 * D_MODEL + 3 * 256 - 1) // (3 * 256)) * 256
ROPE_THETA = 10000.0
ROPE_SEQ_PAIRS = 16
ROPE_ROW_PAIRS = 24
ROPE_COL_PAIRS = 24
HALF = HEAD_DIM // 2
NORM_EPS = 1e-6


def rms_norm(x, g):
    xf = x.astype(jnp.float32)
    y = xf * lax.rsqrt(jnp.mean(xf * xf, axis=-1, keepdims=True) + NORM_EPS)
    return (y * g.astype(jnp.float32)).astype(x.dtype)

def head_group_norm(t, g):
    mu = jnp.mean(t, axis=-1, keepdims=True)
    var = jnp.mean(jnp.square(t - mu), axis=-1, keepdims=True)
    return (t - mu) * lax.rsqrt(var + NORM_EPS) * g.astype(jnp.float32)

def l2_normalize(t):
    return t * lax.rsqrt(jnp.sum(t * t, axis=-1, keepdims=True) + NORM_EPS)

def modulate(h, shift, scale):
    return h * (1.0 + scale) + shift

def adaln(cond, w, b):
    mod = (jax.nn.silu(cond) @ w + b)[:, None, :]
    return jnp.split(mod, 6, axis=-1)

def swiglu(h, w_in, w_out):
    gate, up = jnp.split(h @ w_in, 2, axis=-1)
    return (jax.nn.silu(gate) * up) @ w_out

def axis_angles(pos, n_pairs):
    inv_freq = ROPE_THETA ** (-jnp.arange(n_pairs, dtype=jnp.float32) / n_pairs)
    return pos[:, None] * inv_freq[None, :]

def rope_tables(rows):
    n_lat = rows * GRID_W
    row = jnp.repeat(jnp.arange(rows, dtype=jnp.float32), GRID_W)
    col = jnp.tile(jnp.arange(GRID_W, dtype=jnp.float32), rows)
    zeros_ctx = jnp.zeros((CTX_LEN,), jnp.float32)
    p_seq = jnp.concatenate([jnp.arange(CTX_LEN, dtype=jnp.float32),
                             jnp.full((n_lat,), float(CTX_LEN), jnp.float32)])
    p_row = jnp.concatenate([zeros_ctx, row])
    p_col = jnp.concatenate([zeros_ctx, col])
    ang = jnp.concatenate([axis_angles(p_seq, ROPE_SEQ_PAIRS),
                           axis_angles(p_row, ROPE_ROW_PAIRS),
                           axis_angles(p_col, ROPE_COL_PAIRS)], axis=-1)
    return jnp.cos(ang), jnp.sin(ang)

def apply_rope(t, cos, sin):
    c = cos[None, :, None, :]
    s = sin[None, :, None, :]
    t1, t2 = t[..., :HALF], t[..., HALF:]
    return jnp.concatenate([t1 * c - t2 * s, t1 * s + t2 * c], axis=-1)

def to_bwd(t):
    return jnp.concatenate([jnp.flip(t[:, :CTX_LEN], axis=1), jnp.flip(t[:, CTX_LEN:], axis=1)], axis=1)

def short_conv(u, w):
    n = u.shape[1]
    pad = (CONV_K - 1) // 2
    up = jnp.pad(u, ((0, 0), (pad, pad), (0, 0)))
    y = up[:, 0:n] * w[0]
    for i in range(1, CONV_K):
        y = y + up[:, i:i + n] * w[i]
    return jax.nn.silu(y)

def to_chunks(t):
    b, tl, h = t.shape[:3]
    t = t.reshape((b, tl // CHUNK, CHUNK, h) + t.shape[3:])
    return t.transpose((1, 0, 3, 2) + tuple(range(4, t.ndim)))

def from_chunks(o):
    nc, b, h, cl, d = o.shape
    return o.transpose(1, 0, 3, 2, 4).reshape(b, nc * cl, h, d)

def gated_delta_rule(q, k, v, g, beta):
    b, tl, h, dk = q.shape
    dv = v.shape[-1]
    qc, kc, vc = to_chunks(q), to_chunks(k), to_chunks(v)
    gc, bc = to_chunks(g), to_chunks(beta)
    G = jnp.cumsum(gc, axis=-1)
    idx = jnp.arange(CHUNK)
    incl = idx[:, None] >= idx[None, :]
    strict = idx[:, None] > idx[None, :]
    diff = G[..., :, None] - G[..., None, :]
    decay = jnp.where(incl, jnp.exp(jnp.where(incl, diff, 0.0)), 0.0)
    kb = kc * bc[..., None]
    A = jnp.where(strict, jnp.einsum('nbhid,nbhjd->nbhij', kb, kc) * decay, 0.0)
    rhs = jnp.concatenate([vc * bc[..., None], kb * jnp.exp(G)[..., None]], axis=-1)
    sol = lax.linalg.triangular_solve(A + jnp.eye(CHUNK, dtype=A.dtype), rhs,
                                      left_side=True, lower=True, unit_diagonal=True)
    u, w = sol[..., :dv], sol[..., dv:]
    qk = jnp.einsum('nbhid,nbhjd->nbhij', qc, kc) * decay
    q_dec = qc * jnp.exp(G)[..., None]
    k_dec = kc * jnp.exp(G[..., -1:] - G)[..., None]
    g_last = jnp.exp(G[..., -1])[..., None, None]

    def step(S, xs):
        u_c, w_c, q_c, qk_c, k_c, gl = xs
        v_new = u_c - jnp.einsum('bhck,bhkv->bhcv', w_c, S)
        o = jnp.einsum('bhck,bhkv->bhcv', q_c, S) + jnp.einsum('bhij,bhjv->bhiv', qk_c, v_new)
        S = gl * S + jnp.einsum('bhck,bhcv->bhkv', k_c, v_new)
        return S, o

    S0 = jnp.zeros((b, h, dk, dv), q.dtype)
    _, o = lax.scan(step, S0, (u, w, q_dec, qk, k_dec, g_last))
    return from_chunks(o)

def retention_chunkwise(q, k, v, log_gamma):
    b, tl, h, dk = q.shape
    dv = v.shape[-1]
    qc, kc, vc = to_chunks(q), to_chunks(k), to_chunks(v)
    pos = jnp.arange(CHUNK, dtype=jnp.float32)
    lg = log_gamma.astype(jnp.float32)[:, None]
    diff = pos[:, None] - pos[None, :]
    decay = jnp.where(diff >= 0, jnp.exp(lg[:, :, None] * jnp.maximum(diff, 0.0)), 0.0)
    xi = jnp.exp(lg * (pos + 1.0))
    zeta = jnp.exp(lg * (CHUNK - 1.0 - pos))
    g_chunk = jnp.exp(lg * CHUNK)[..., None]
    inner = jnp.einsum('nbhij,nbhjv->nbhiv', jnp.einsum('nbhid,nbhjd->nbhij', qc, kc) * decay, vc)

    def step(R, xs):
        q_c, k_c, v_c = xs
        o = jnp.einsum('bhik,bhkv->bhiv', q_c * xi[..., None], R)
        R = g_chunk * R + jnp.einsum('bhjk,bhjv->bhkv', k_c * zeta[..., None], v_c)
        return R, o

    R0 = jnp.zeros((b, h, dk, dv), q.dtype)
    _, cross = lax.scan(step, R0, (qc, kc, vc))
    return from_chunks(inner + cross)

def hybrid_mixer(h_ctx, h_lat, w_in, conv_w, gdn_a_log, gdn_dt_bias, gdn_norm_g,
                 ret_decay_logit, ret_norm_g, cos, sin):
    out_dtype = h_lat.dtype
    f32 = jnp.float32
    h = jnp.concatenate([h_ctx, h_lat], axis=1)
    p = (h @ w_in).astype(f32)
    b, tl, _ = p.shape
    splits = [3 * W_GDN, 4 * W_GDN, 4 * W_GDN + 4 * N_HEADS_GDN,
              4 * W_GDN + 4 * N_HEADS_GDN + W_RET,
              4 * W_GDN + 4 * N_HEADS_GDN + 2 * W_RET,
              4 * W_GDN + 4 * N_HEADS_GDN + 3 * W_RET]
    qkv_a, z, ab, rq, rk, rv, rg = jnp.split(p, splits, axis=-1)

    cw = conv_w.astype(f32)
    qkv_a = jnp.concatenate([short_conv(qkv_a[:, :CTX_LEN], cw), short_conv(qkv_a[:, CTX_LEN:], cw)], axis=1)
    q, k, v = [t.reshape(b, tl, N_HEADS_GDN, HEAD_DIM) for t in jnp.split(qkv_a, 3, axis=-1)]
    q = l2_normalize(q) * (HEAD_DIM ** -0.5)
    k = l2_normalize(k)
    a_f, a_b, b_f, b_b = jnp.split(ab, 4, axis=-1)
    A = jnp.exp(gdn_a_log.astype(f32))
    dtb = gdn_dt_bias.astype(f32)
    g_f = -A[0] * jax.nn.softplus(a_f + dtb[0])
    g_b = -A[1] * jax.nn.softplus(a_b + dtb[1])
    o_f = gated_delta_rule(q, k, v, g_f, jax.nn.sigmoid(b_f))
    o_b = to_bwd(gated_delta_rule(to_bwd(q), to_bwd(k), to_bwd(v), to_bwd(g_b), to_bwd(jax.nn.sigmoid(b_b))))
    o_gdn = rms_norm(o_f + o_b, gdn_norm_g) * jax.nn.silu(z.reshape(b, tl, N_HEADS_GDN, HEAD_DIM))

    rq = apply_rope(rq.reshape(b, tl, N_HEADS_RET, HEAD_DIM), cos, sin)
    rk = apply_rope(rk.reshape(b, tl, N_HEADS_RET, HEAD_DIM), cos, sin) * (HEAD_DIM ** -0.5)
    rv = rv.reshape(b, tl, N_HEADS_RET, HEAD_DIM)
    lg = jax.nn.log_sigmoid(ret_decay_logit.astype(f32))
    r_f = retention_chunkwise(rq, rk, rv, lg[0])
    r_b = to_bwd(retention_chunkwise(to_bwd(rq), to_bwd(rk), to_bwd(rv), lg[1]))
    o_ret = head_group_norm(r_f + r_b, ret_norm_g) * jax.nn.silu(rg.reshape(b, tl, N_HEADS_RET, HEAD_DIM))

    y = jnp.concatenate([o_gdn.reshape(b, tl, W_GDN), o_ret.reshape(b, tl, W_RET)], axis=-1)
    return y.astype(out_dtype)

def first_inputs(seed: int = 0) -> dict:
    key = jax.random.key(seed)
    ks = jax.random.split(key, 19)
    f32 = jnp.float32

    def nrm(k, shape, scale):
        return scale * jax.random.normal(k, shape, f32)

    x = nrm(ks[0], (BATCH, SEQ, D_MODEL), 1.0)
    c = nrm(ks[1], (BATCH, D_MODEL), 1.0)
    ctx = nrm(ks[2], (BATCH, CTX_LEN, D_MODEL), 1.0)
    c_ctx = nrm(ks[3], (D_MODEL,), 1.0)
    ada_w = nrm(ks[4], (DEPTH, D_MODEL, 6 * D_MODEL), D_MODEL ** -0.5)
    ada_b = nrm(ks[5], (DEPTH, 6 * D_MODEL), 0.02)
    norm_mix_g = 1.0 + nrm(ks[6], (DEPTH, D_MODEL), 0.05)
    norm_ffn_g = 1.0 + nrm(ks[7], (DEPTH, D_MODEL), 0.05)
    w_in = nrm(ks[8], (DEPTH, D_MODEL, IN_COLS), D_MODEL ** -0.5)
    conv_w = nrm(ks[9], (DEPTH, CONV_K, 3 * W_GDN), CONV_K ** -0.5)
    gdn_a_log = jnp.log(jax.random.uniform(ks[10], (DEPTH, 2, N_HEADS_GDN), f32, 1.0, 16.0))
    dt = jnp.exp(jax.random.uniform(ks[11], (DEPTH, 2, N_HEADS_GDN), f32, math.log(1e-3), math.log(1e-1)))
    gdn_dt_bias = dt + jnp.log(-jnp.expm1(-dt))
    gdn_norm_g = 1.0 + nrm(ks[12], (DEPTH, HEAD_DIM), 0.05)
    heads = jnp.arange(N_HEADS_RET, dtype=f32)
    ret_decay_logit = jnp.log(2.0 ** (5.0 + heads) - 1.0) + nrm(ks[13], (DEPTH, 2, N_HEADS_RET), 0.01)
    ret_norm_g = 1.0 + nrm(ks[14], (DEPTH, HEAD_DIM), 0.05)
    w_out = nrm(ks[15], (DEPTH, MIX_WIDTH, D_MODEL), MIX_WIDTH ** -0.5)
    w_ffn_in = nrm(ks[16], (DEPTH, D_MODEL, 2 * D_FF), D_MODEL ** -0.5)
    w_ffn_out = nrm(ks[17], (DEPTH, D_FF, D_MODEL), D_FF ** -0.5)
    final_g = 1.0 + nrm(ks[18], (D_MODEL,), 0.05)
    return {"x": x, "c": c, "ctx": ctx, "c_ctx": c_ctx, "ada_w": ada_w, "ada_b": ada_b,
            "norm_mix_g": norm_mix_g, "norm_ffn_g": norm_ffn_g, "w_in": w_in, "conv_w": conv_w,
            "gdn_a_log": gdn_a_log, "gdn_dt_bias": gdn_dt_bias, "gdn_norm_g": gdn_norm_g,
            "ret_decay_logit": ret_decay_logit, "ret_norm_g": ret_norm_g, "w_out": w_out,
            "w_ffn_in": w_ffn_in, "w_ffn_out": w_ffn_out, "final_g": final_g}

def first_block(x, c, ctx, c_ctx, ada_w, ada_b, norm_mix_g, norm_ffn_g, w_in, conv_w,
              gdn_a_log, gdn_dt_bias, gdn_norm_g, ret_decay_logit, ret_norm_g, w_out,
              w_ffn_in, w_ffn_out, final_g):
    n_lat = x.shape[1]
    rows = n_lat // GRID_W
    cos, sin = rope_tables(rows)
    x_ctx = ctx
    for layer in range(DEPTH):
        sh1, sc1, g1, sh2, sc2, g2 = adaln(c, ada_w[layer], ada_b[layer])
        csh1, csc1, cg1, csh2, csc2, cg2 = adaln(c_ctx[None, :], ada_w[layer], ada_b[layer])
        h_lat = modulate(rms_norm(x, norm_mix_g[layer]), sh1, sc1)
        h_ctx = modulate(rms_norm(x_ctx, norm_mix_g[layer]), csh1, csc1)
        y = hybrid_mixer(h_ctx, h_lat, w_in[layer], conv_w[layer], gdn_a_log[layer],
                         gdn_dt_bias[layer], gdn_norm_g[layer], ret_decay_logit[layer],
                         ret_norm_g[layer], cos, sin)
        x = x + g1 * (y[:, CTX_LEN:] @ w_out[layer])
        x = x + g2 * swiglu(modulate(rms_norm(x, norm_ffn_g[layer]), sh2, sc2),
                            w_ffn_in[layer], w_ffn_out[layer])
        if layer < DEPTH - 1:
            x_ctx = x_ctx + cg1 * (y[:, :CTX_LEN] @ w_out[layer])
            x_ctx = x_ctx + cg2 * swiglu(modulate(rms_norm(x_ctx, norm_ffn_g[layer]), csh2, csc2),
                                         w_ffn_in[layer], w_ffn_out[layer])
    return rms_norm(x, final_g)


DEPTH_2 = 2

D_CONV = D_MODEL
CONV_GROUPS = 8
SHORT_CONV_K = 3
D_RNN = D_MODEL
RNN_HEADS = 4
RNN_HEAD_DIM = D_RNN // RNN_HEADS
RNN_CONV_K = 4
LRU_C = 8.0
N_BRANCH = 2
D_FF_2 = 2816
D_IN = 3 * D_CONV + 2 * D_RNN + N_BRANCH * D_MODEL
SPLITS = (D_CONV, 2 * D_CONV, 3 * D_CONV, 3 * D_CONV + D_RNN, 3 * D_CONV + 2 * D_RNN)
ALPHA = (2.0 * DEPTH_2) ** 0.25
BETA = (8.0 * DEPTH_2) ** -0.25
LN_EPS = 1e-5


def layer_norm(x, g, b):
    xf = x.astype(jnp.float32)
    mu = jnp.mean(xf, axis=-1, keepdims=True)
    var = jnp.mean(jnp.square(xf - mu), axis=-1, keepdims=True)
    y = (xf - mu) * lax.rsqrt(var + LN_EPS)
    return (y * g.astype(jnp.float32) + b.astype(jnp.float32)).astype(x.dtype)

def causal_depthwise_conv(x, w, k):
    s = x.shape[1]
    xp = jnp.pad(x, ((0, 0), (k - 1, 0), (0, 0)))
    out = xp[:, 0:s, :] * w[0]
    for i in range(1, k):
        out = out + xp[:, i:i + s, :] * w[i]
    return out

def swiglu_2(x, w1, w2):
    g, u = jnp.split(x @ w1, 2, axis=-1)
    return (jax.nn.silu(g) * u) @ w2

def rg_lru(x, gate_in, gate_rec, a_param):
    s = x.shape[1]
    log_a = -LRU_C * gate_rec * jax.nn.softplus(-a_param)
    a = jnp.exp(log_a)
    mult = jnp.sqrt(-jnp.expm1(2.0 * log_a))
    is_start = (jnp.arange(s) == 0)[None, :, None]
    mult = jnp.where(is_start, 1.0, mult)
    b = x * gate_in * mult

    def combine(left, right):
        a1, b1 = left
        a2, b2 = right
        return a1 * a2, a2 * b1 + b2

    _, h = lax.associative_scan(combine, (a, b), axis=1)
    return h

def hybrid_mixer_2(x, w_in, b_merge, sc_w, rc_w, rc_b, rg_w, rg_b, a_param,
                 w_out_conv, w_out_rnn, w_o):
    bsz, s, _ = x.shape
    proj = x @ w_in
    b_gate, c_gate, v, x_r, y_r, g_logits = jnp.split(proj, SPLITS, axis=-1)

    y_a = (b_gate * causal_depthwise_conv(c_gate * v, sc_w, SHORT_CONV_K)) @ w_out_conv

    xc = causal_depthwise_conv(x_r, rc_w, RNN_CONV_K) + rc_b
    xh = xc.reshape(bsz, s, RNN_HEADS, RNN_HEAD_DIM)
    gates = jnp.einsum('bshi,ghij->gbshj', xh, rg_w).reshape(2, bsz, s, D_RNN)
    gates = jax.nn.sigmoid((gates + rg_b[:, None, None, :]).astype(jnp.float32))
    h = rg_lru(xc.astype(jnp.float32), gates[0], gates[1],
               a_param.astype(jnp.float32)).astype(x.dtype)
    y_b = (h * jax.nn.gelu(y_r)) @ w_out_rnn

    g_a, g_b = jnp.split(jax.nn.sigmoid(g_logits + b_merge), 2, axis=-1)
    return (g_a * y_a + g_b * y_b) @ w_o

def second_inputs(seed: int = 0) -> dict:
    key = jax.random.key(seed)
    ks = jax.random.split(key, 20)
    f32 = jnp.float32
    nrm = lambda k, shape, scale: jax.random.normal(k, shape, f32) * scale

    x = jax.random.normal(ks[0], (BATCH, SEQ, D_MODEL), f32)
    w_in = nrm(ks[1], (DEPTH_2, D_MODEL, D_IN), D_MODEL ** -0.5)
    b_merge = nrm(ks[2], (DEPTH_2, N_BRANCH * D_MODEL), 0.1)
    sc_w = nrm(ks[3], (DEPTH_2, SHORT_CONV_K, D_CONV), SHORT_CONV_K ** -0.5)
    rc_w = nrm(ks[4], (DEPTH_2, RNN_CONV_K, D_RNN), RNN_CONV_K ** -0.5)
    rc_b = nrm(ks[5], (DEPTH_2, D_RNN), 0.02)
    rg_w = nrm(ks[6], (DEPTH_2, 2, RNN_HEADS, RNN_HEAD_DIM, RNN_HEAD_DIM), RNN_HEAD_DIM ** -0.5)
    rg_b = nrm(ks[7], (DEPTH_2, 2, D_RNN), 0.1)
    u = jax.random.uniform(ks[8], (DEPTH_2, D_RNN), f32, 0.9, 0.999)
    s_a = u ** (1.0 / LRU_C)
    a_param = jnp.log(s_a) - jnp.log1p(-s_a)
    w_out_conv = nrm(ks[9], (DEPTH_2, D_CONV, D_MODEL), D_CONV ** -0.5)
    w_out_rnn = nrm(ks[10], (DEPTH_2, D_RNN, D_MODEL), D_RNN ** -0.5)
    w_o = nrm(ks[11], (DEPTH_2, D_MODEL, D_MODEL), BETA * D_MODEL ** -0.5)
    ffn_w1 = nrm(ks[12], (DEPTH_2, 2, D_MODEL, 2 * D_FF_2), D_MODEL ** -0.5)
    ffn_w2 = nrm(ks[13], (DEPTH_2, 2, D_FF_2, D_MODEL), BETA * D_FF_2 ** -0.5)
    ln_g = 1.0 + nrm(ks[14], (DEPTH_2, 3, D_MODEL), 0.02)
    ln_b = nrm(ks[15], (DEPTH_2, 3, D_MODEL), 0.02)
    return {"x": x, "w_in": w_in, "b_merge": b_merge, "sc_w": sc_w, "rc_w": rc_w,
            "rc_b": rc_b, "rg_w": rg_w, "rg_b": rg_b, "a_param": a_param,
            "w_out_conv": w_out_conv, "w_out_rnn": w_out_rnn, "w_o": w_o,
            "ffn_w1": ffn_w1, "ffn_w2": ffn_w2, "ln_g": ln_g, "ln_b": ln_b}

def second_block(x, w_in, b_merge, sc_w, rc_w, rc_b, rg_w, rg_b, a_param,
              w_out_conv, w_out_rnn, w_o, ffn_w1, ffn_w2, ln_g, ln_b):
    for l in range(DEPTH_2):
        x = layer_norm(ALPHA * x + 0.5 * swiglu_2(x, ffn_w1[l, 0], ffn_w2[l, 0]),
                       ln_g[l, 0], ln_b[l, 0])
        mix = hybrid_mixer_2(x, w_in[l], b_merge[l], sc_w[l], rc_w[l], rc_b[l], rg_w[l],
                           rg_b[l], a_param[l], w_out_conv[l], w_out_rnn[l], w_o[l])
        x = layer_norm(ALPHA * x + mix, ln_g[l, 1], ln_b[l, 1])
        x = layer_norm(ALPHA * x + 0.5 * swiglu_2(x, ffn_w1[l, 1], ffn_w2[l, 1]),
                       ln_g[l, 2], ln_b[l, 2])
    return x


def setup_inputs(seed=0):
    out = dict(first_inputs(seed))
    for name, value in second_inputs(seed + 1).items():
        if name != "x":
            out[name + "_2"] = value
    return out


def reference(
    x, c, ctx, c_ctx, ada_w, ada_b, norm_mix_g, norm_ffn_g, w_in, conv_w, gdn_a_log,
    gdn_dt_bias, gdn_norm_g, ret_decay_logit, ret_norm_g, w_out, w_ffn_in, w_ffn_out, final_g,
    w_in_2, b_merge_2, sc_w_2, rc_w_2, rc_b_2, rg_w_2, rg_b_2, a_param_2, w_out_conv_2,
    w_out_rnn_2, w_o_2, ffn_w1_2, ffn_w2_2, ln_g_2, ln_b_2,
):
    x = first_block(
        x, c, ctx, c_ctx, ada_w, ada_b, norm_mix_g, norm_ffn_g, w_in, conv_w, gdn_a_log,
        gdn_dt_bias, gdn_norm_g, ret_decay_logit, ret_norm_g, w_out, w_ffn_in, w_ffn_out,
        final_g,
    )
    return second_block(
        x, w_in_2, b_merge_2, sc_w_2, rc_w_2, rc_b_2, rg_w_2, rg_b_2, a_param_2, w_out_conv_2,
        w_out_rnn_2, w_o_2, ffn_w1_2, ffn_w2_2, ln_g_2, ln_b_2,
    )


_drawn_inputs = setup_inputs


def setup_inputs(seed=0):
    import zlib

    import numpy as np

    out = dict(_drawn_inputs(seed))
    spreads = {}
    factors = {'gdn_norm_g': 3.252,
     'ret_norm_g': 2.932,
     'b_merge_2': 4.31,
     'rc_b_2': 3.503,
     'rg_b_2': 6.706}
    for name, (base, spread) in spreads.items():
        noise = np.random.default_rng([zlib.crc32(name.encode()), seed]).standard_normal(out[name].shape)
        drawn = base * np.exp(spread * noise) if base else spread * noise
        out[name] = jnp.asarray(drawn.astype(out[name].dtype))
    for name, factor in factors.items():
        out[name] = (out[name] * factor).astype(out[name].dtype)
    return out
```

```python
from contextlib import ExitStack, contextmanager

import numpy as np

import concourse.bass as bass
from concourse import mybir

F32 = mybir.dt.float32
F32R = mybir.dt.float32r
U8 = mybir.dt.uint8
ALU = mybir.AluOpType
ACT = mybir.ActivationFunctionType

P = 128
D = 1024
KT = D // P
CTX, LAT = 256, 512
TOK = CTX + LAT
H = 4
NC = TOK // P
NCC = CTX // P
FF = 2816
FT = FF // P
LAYERS = 2
GRID_W, ROPE_THETA = 64, 10000.0
SEQ_PAIRS, ROW_PAIRS, COL_PAIRS = 16, 24, 24
EPS, LN_EPS = 1e-6, 1e-5
ALPHA = (2.0 * LAYERS) ** 0.25
LRU_C = 8.0
HSCALE = float(P) ** -0.5

TILES = 8
SLOTS, RAW = 4, 2
N_PROJ = 7 * H + 1 + H
N_B1 = N_PROJ + KT + 2 * FT + FT
N_LAYER = 2 * 3 * FT + 3 * KT + 5 * H + 4 * KT + KT
N_CHUNKS = N_B1 + LAYERS * N_LAYER
N_STREAM = N_CHUNKS + SLOTS
assert N_LAYER % SLOTS == 0
ADA_M = 6 * KT
ADA_GROUP, ADA_GROUPS = 4, 3

_o = 0


def _cols(n):
    global _o
    _o += n
    return _o - n


C_COND, C_ADAB, C_GMIX, C_GFFN = _cols(2 * KT), _cols(ADA_M), _cols(KT), _cols(KT)
C_CONV, C_GDNG, C_RETG, C_FING = _cols(12 * 5), _cols(1), _cols(1), _cols(KT)
C_DTB, C_ALOG, C_RETL = _cols(8), _cols(8), _cols(8)
C_UP, C_DOWN = _cols(1), _cols(1)
C_LAY = _o
L_SC, L_RC, L_RCB, L_RGB, L_BM, L_LNG, L_LNB, L_AP, L_C8, L_N8 = 0, 24, 56, 64, 80, 96, 120, 144, 152, 160
L_W = 168
C_W = C_LAY + LAYERS * L_W
LAYER_STEPS = 157
N_SP = NC * 8 + 8 + LAYERS * KT


class Tally:

    def __init__(self):
        self.base, self.k = 0, 0

    def up(self, n=1):
        self.k += n
        return self.base + self.k

    @property
    def now(self):
        return self.base + self.k


@contextmanager
def rounds(engine, count, *pers):
    starts = [(t.base, t.k) for t, _ in pers]
    with engine.Fori(0, count) as i:
        for t, n in pers:
            t.base, t.k = i * n + (t.base + t.k), 0
        yield i
        for t, n in pers:
            assert t.k == n, (t.k, n)
    for (t, n), (base, k) in zip(pers, starts):
        t.base, t.k = base, k + count * n


def f32(ap):
    return ap.bitcast(F32)


def build(nc, x_in, stream, ada, params, consts, masks, rope, out):
    ctx = ExitStack()
    with ctx:
        base = 16512
        KB = 1024

        def at(name, off, shape, dt=F32):
            return nc.alloc_sbuf_tensor_at(name, shape, dt, offset=base + off)

        h1 = at("h1", 0, [P, KT, 2, TOK], F32R)
        acts = at("acts", 0, [P, 34, 2, LAT], F32R)
        ktok = at("ktok", 0, [P, NC, H, P])
        vtok = at("vtok", 12 * KB, [P, NC, H, P])
        rktok = at("rktok", 24 * KB, [P, NC, H, P])
        oret = at("oret", 36 * KB, [P, H, LAT])
        retS = [at(f"retS{d}", (44 + 2 * d) * KB, [P, H, P]) for d in range(2)]
        xin = at("xin", 48 * KB, [P, KT, TOK])
        adaw = at("adaw", 72 * KB, [P, ADA_GROUPS * ADA_GROUP, KT, P])
        kT = at("kT", 48 * KB, [P, H, TOK])
        qT = at("qT", 60 * KB, [P, H, LAT])
        vfm = at("vfm", 68 * KB, [P, H, TOK])
        ogdn = at("ogdn", 68 * KB, [P, H, LAT])
        rqT = at("rqT", 80 * KB, [P, H, LAT])
        rkT = at("rkT", 88 * KB, [P, H, TOK])
        rvtok = at("rvtok", 100 * KB, [P, NC, H * P])
        zs = at("zs", 112 * KB, [P, H, LAT])
        rgs = at("rgs", 120 * KB, [P, H, LAT])
        rope_sb = at("rope_sb", 112 * KB, [P, 2 * TOK + 2 * LAT])
        lmask = at("lmask", 128 * KB, [P, 14, P], U8)
        masks_in = at("masks_in", 40 * KB, [P, 14 * P])
        cst1 = at("cst1", 130 * KB, [P, 3, P])
        Dsum = at("Dsum", 132 * KB, [P, H, P])
        tok = at("tok", 134 * KB, [P, 10, NC * 8])
        XO = 136 * KB
        X = at("X", XO, [P, KT, LAT])
        big = [at(f"big{i}", XO + i * 3104, [P, 776]) for i in range(5)]
        WO = XO + 16 * KB
        w_hi = at("w_hi", WO, [P, SLOTS, TILES, P], F32R)
        w_lo = at("w_lo", WO + 16 * KB, [P, SLOTS, TILES, P], F32R)
        raw = at("raw", WO + 32 * KB, [P, RAW, TILES, P])
        MO = WO + 40 * KB
        ident = at("ident", MO, [P, P])
        ones = at("ones", MO + 512, [P, P])
        prm = at("prm", MO + 1024, [P, C_W])
        lay = at("lay", MO + 1024 + 4 * C_W, [P, L_W])
        so = MO + 1024 + 4 * C_W + 4 * L_W
        csil = at("csil", so, [P, 2 * KT])
        mod = at("mod", so + 64, [P, ADA_M, 2])
        coef = at("coef", so + 64 + 8 * ADA_M, [P, 3, KT])
        lgc = at("lgc", so + 64 + 8 * ADA_M + 96, [P, 8])
        gch = at("gch", so + 64 + 8 * ADA_M + 128, [P, 8])
        zeta = at("zeta", so + 64 + 8 * ADA_M + 160, [P, 8])
        epsc = at("epsc", so + 64 + 8 * ADA_M + 192, [P, 8])
        to = (so + 64 + 8 * ADA_M + 224 + 31) // 32 * 32
        tmp = [at(f"tmp{i}", to + i * 2 * KB, [P, LAT]) for i in range(4)]
        spw = at("spw", to + 8 * KB, [P, 6, N_SP])
        assert base + to + 8 * KB + 24 * N_SP <= 229344
        rt = [at(f"rt{i}", XO + i * 2 * KB, [P, H, P]) for i in range(8)]
        gt = [[rt[4 * d + i] for i in range(4)]
              + [at(f"gt{d}{i}", (80 + 16 * d + 2 * i) * KB, [P, H, P]) for i in range(8)] for d in range(2)]
        MT = 96 * KB
        mt = [at(f"mt{i}", MT + i * 2080, [P, LAT + 3]) for i in range(15)]

        ps = [ctx.enter_context(nc.psum_tensor(f"ps{i}", [P, 512], F32)) for i in range(8)]
        pair = lambda j: (acts[:, j, 0, :], acts[:, j, 1, :])

        def sem(name):
            return ctx.enter_context(nc.semaphore(name))


        s_Gc = sem("Gc")
        s_abt = sem("abt")
        s_acc = sem("acc")
        s_act = sem("act")
        s_ada = [sem(f"ada{i}") for i in range(ADA_GROUPS)]
        s_ada_done = sem("ada_done")
        s_ath = sem("ath")
        s_aux_done = sem("aux_done")
        s_aux_in = sem("aux_in")
        s_aux_read = sem("aux_read")
        s_beta = sem("beta")
        s_cdone = sem("cdone")
        s_cs = sem("cs")
        s_csil = sem("csil")
        s_cst = sem("cst")
        s_cum = sem("cum")
        s_dec = sem("dec")
        s_dexp = sem("dexp")
        s_dm = [sem(f"dm{d}") for d in range(2)]
        s_done = sem("done")
        s_dve = sem("dve")
        s_e = [sem(f"e{d}") for d in range(2)]
        s_eG = sem("eG")
        s_eg = [sem(f"eg{d}") for d in range(2)]
        s_eps = sem("eps")
        s_fin = sem("fin")
        s_g = sem("g")
        s_gS = [sem(f"gS{d}") for d in range(2)]
        s_gelu = sem("gelu")
        s_go = [sem(f"go{d}") for d in range(2)]
        s_god = [sem(f"god{d}") for d in range(2)]
        s_gp = [sem(f"gp{d}") for d in range(2)]
        s_gt = [sem(f"gt{d}") for d in range(2)]
        s_gx = [sem(f"gx{d}") for d in range(2)]
        s_gxt = [sem(f"gxt{d}") for d in range(2)]
        s_gy = [sem(f"gy{d}") for d in range(2)]
        s_gyc = [sem(f"gyc{d}") for d in range(2)]
        s_h1 = sem("h1")
        s_hg = sem("hg")
        s_hh = sem("hh")
        s_hhi = sem("hhi")
        s_hi = sem("hi")
        s_hid = sem("hid")
        s_hm2 = sem("hm2")
        s_hread = sem("hread")
        s_hsq = sem("hsq")
        s_hss = sem("hss")
        s_hstd = sem("hstd")
        s_hval = sem("hval")
        s_hvar = sem("hvar")
        s_kg = [sem(f"kg{d}") for d in range(2)]
        s_kv = [sem(f"kv{d}") for d in range(2)]
        s_lg = sem("lg")
        s_lo = sem("lo")
        s_m2 = sem("m2")
        s_merge = sem("merge")
        s_mg = sem("mg")
        s_mh = sem("mh")
        s_mlo = sem("mlo")
        s_mod = sem("mod")
        s_msq = sem("msq")
        s_na = [sem(f"na{d}") for d in range(2)]
        s_nwT = [sem(f"nwT{d}") for d in range(2)]
        s_out = sem("out")
        s_pre = sem("pre")
        s_pread = sem("pread")
        s_prm = sem("prm")
        s_prod = sem("prod")
        s_qadd = sem("qadd")
        s_rS = [sem(f"rS{d}") for d in range(2)]
        s_raw = [sem(f"raw{i}") for i in range(RAW)]
        s_res = sem("res")
        s_rkv = [sem(f"rkv{d}") for d in range(2)]
        s_rkz = [sem(f"rkz{d}") for d in range(2)]
        s_rm = sem("rm")
        s_rm4 = sem("rm4")
        s_ro = [sem(f"ro{d}") for d in range(2)]
        s_rod = [sem(f"rod{d}") for d in range(2)]
        s_root = sem("root")
        s_rope = sem("rope")
        s_rows = [sem(f"rows{d}") for d in range(2)]
        s_rqk = sem("rqk")
        s_rqx = [sem(f"rqx{d}") for d in range(2)]
        s_rv = sem("rv")
        s_sig = sem("sig")
        s_sil = sem("sil")
        s_silu = sem("silu")
        s_spa = sem("spa")
        s_sq = sem("sq")
        s_sqadd = sem("sqadd")
        s_sqx = sem("sqx")
        s_ss = sem("ss")
        s_stat = sem("stat")
        s_std = sem("std")
        s_std0 = sem("std0")
        s_turn = sem("turn")
        s_turned = sem("turned")
        s_var = sem("var")
        s_vn = [sem(f"vn{d}") for d in range(2)]
        s_vp = [sem(f"vp{d}") for d in range(2)]
        s_wT = [sem(f"wT{d}") for d in range(2)]
        s_xc = sem("xc")
        s_xcf = sem("xcf")
        s_xch = sem("xch")
        s_xhi = sem("xhi")
        s_xin = sem("xin")
        s_xlo = sem("xlo")
        s_xn = sem("xn")
        s_xr = sem("xr")
        s_xres = sem("xres")
        s_y = sem("y")
        s_ya = sem("ya")
        s_yaf = sem("yaf")
        s_yah = sem("yah")
        s_yb = sem("yb")
        s_ybh = sem("ybh")
        s_yf = sem("yf")
        s_yh = sem("yh")

        items = [(kind, h) for kind in ("k", "v", "rk", "rq", "q", "z", "rg") for h in range(H)] + [("ab", 0)]
        WHOLE, CONV, NORMED, ROPED = ("k", "v", "rk", "ab"), ("k", "v", "q"), ("k", "q"), ("rk", "rq")
        count = lambda kinds: [sum(k in kinds for k, _ in items[:i + 1]) for i in range(len(items))]
        n_aux, n_c, n_conv = count(NORMED + ROPED), count(CONV + ROPED), count(CONV)
        n_last_rope = max(i for i, (k, _) in enumerate(items) if k in ROPED)
        pbuf = lambda j: big[j % 2]
        cbuf = lambda j: big[2 + j % 2]
        turned = [(kind, c) for kind in ("k", "v", "rk") for c in range(NC)]
        order = (list(range(NC)), list(range(NCC))[::-1] + list(range(NCC, NC))[::-1])
        DOWN = (4, 5, 6, 7, 0, 1, 2, 3)
        mats = tmp[3][:, :].rearrange("p (a n) -> p a n", a=4)

        block = ctx.enter_context(nc.Block())

        @block.sync
        def _(sp):
            sp.dma_start(prm[:, :], params).then_inc(s_prm, 16)
            sp.dma_start(xin[:, :, :], x_in).then_inc(s_xin, 16)

            def load_ada(g):
                if g >= ADA_GROUPS:
                    sp.wait_ge(s_ada_done, ADA_GROUP * (g - ADA_GROUPS + 1))
                r = g % ADA_GROUPS
                sp.dma_start(adaw[:, ADA_GROUP * r:ADA_GROUP * (r + 1)].rearrange("p m k n -> p m (k n)"),
                             ada[ADA_GROUP * g:ADA_GROUP * (g + 1)].rearrange("m p n -> p m n")
                             ).then_inc(s_ada[r], 16)

            for g in range(ADA_GROUPS):
                load_ada(g)
            sp.dma_start(tmp[3][:, :], consts[:, 5 * P:9 * P]).then_inc(s_rm4, 16)
            sp.dma_start(ident[:, :], consts[:, 0:P]).then_inc(s_cst, 16)
            sp.dma_start(ones[:, :], consts[:, P:2 * P]).then_inc(s_cst, 16)
            sp.dma_start(cst1[:, :, :].rearrange("p a n -> p (a n)"), consts[:, 2 * P:5 * P]).then_inc(s_cst, 16)
            sp.dma_start(masks_in[:, :], masks).then_inc(s_cst, 16)
            for g in range(ADA_GROUPS, ADA_M // ADA_GROUP):
                load_ada(g)

            def load_chunk(n, slot):
                sp.dma_start(raw[:, slot, :, :].rearrange("p k n -> p (k n)"),
                             stream[bass.ds(n, 1), :, :].rearrange("a p n -> (a p) n")).then_inc(s_raw[slot], 16)

            load_chunk(0, 0)
            load_chunk(1, 1)
            sp.wait_ge(s_ada_done, ADA_M)
            sp.dma_start(rope_sb[:, :], rope).then_inc(s_rope, 16)
            split = Tally()
            body = (N_STREAM - RAW) // RAW
            with rounds(sp, body, (split, RAW)) as i:
                for s in range(RAW):
                    sp.wait_ge(s_lo, split.up())
                    load_chunk(i * RAW + RAW + s, s)
            for n in range(RAW + body * RAW, N_STREAM):
                sp.wait_ge(s_lo, split.up())
                load_chunk(n, n % RAW)

        @block.gpsimd
        def _(pool):
            hi = Tally()

            def low_part(slot):
                pool.wait_ge(s_hi, hi.up())
                nc.gpsimd.tensor_tensor(w_lo[:, slot, :, :], raw[:, slot % RAW, :, :],
                                        f32(w_hi[:, slot, :, :]), ALU.subtract).then_inc(s_lo, 1)

            with rounds(pool, N_STREAM // SLOTS, (hi, SLOTS)):
                for slot in range(SLOTS):
                    low_part(slot)
            for slot in range(N_STREAM % SLOTS):
                low_part(slot)

        @block.tensor
        def _(pe):
            mm = nc.tensor.matmul
            slot = [0]
            n_hi, n_lo = Tally(), Tally()

            def chunk(outs):
                s = slot[0] % SLOTS
                slot[0] += 1
                pe.wait_ge(s_hi, n_hi.up())
                for k in range(TILES):
                    for o, xh, xl, start, stop in outs(k):
                        mm(o, w_hi[:, s, k, :], xh, start=start, stop=False, skip_group_check=True)
                        mm(o, w_hi[:, s, k, :], xl, start=False, stop=False, skip_group_check=True)
                pe.wait_ge(s_lo, n_lo.up())
                for k in range(TILES):
                    for o, xh, xl, start, stop in outs(k):
                        last = mm(o, w_lo[:, s, k, :], xh, start=False, stop=stop, skip_group_check=True)
                last.then_inc(s_done, 1)

            pe.wait_ge(s_csil, 1)
            for m in range(ADA_M):
                g = m // ADA_GROUP
                if m % ADA_GROUP == 0:
                    pe.wait_ge(s_ada[g % ADA_GROUPS], 16 * (g // ADA_GROUPS + 1))
                for k in range(KT):
                    last = mm(ps[0][:, 2 * m:2 * m + 2], adaw[:, m % (ADA_GROUP * ADA_GROUPS), k, :],
                              csil[:, 2 * k:2 * k + 2], start=(k == 0), stop=(k == KT - 1))
                last.then_inc(s_ada_done, 1)

            pe.wait_ge(s_cst, 64)
            pe.wait_ge(s_acc, 1)
            mm(ps[2][:, 0:CTX], ones[:, :], big[2][:, 0:CTX], start=True, stop=True)
            mm(ps[1][:, :], ones[:, :], big[2][:, CTX:TOK], start=True, stop=True).then_inc(s_ss, 1)

            pe.wait_ge(s_mod, 1)
            for i, (kind, h) in enumerate(items + [(None, 0)] * 2):
                if kind:
                    if i >= 2:
                        pe.wait_ge(s_pread, i - 1)
                    if i == 0:
                        pe.wait_ge(s_h1, KT)
                    L, C = ps[2 * (i % 2)], ps[2 * (i % 2) + 1]
                    s = slice(CTX, TOK)

                    def outs(k, whole=kind in WHOLE):
                        r = [(L[:, :], h1[:, k, 0, CTX:TOK], h1[:, k, 1, CTX:TOK], k == 0, k == KT - 1)]
                        if whole:
                            r.append((C[:, 0:CTX], h1[:, k, 0, 0:CTX], h1[:, k, 1, 0:CTX], k == 0, k == KT - 1))
                        return r

                    chunk(outs)
                if i >= 2:
                    kind, h = items[i - 2]
                    j = i - 2
                    if kind in NORMED + ROPED:
                        pe.wait_ge(s_aux_in, n_aux[j])
                        if n_aux[j] >= 2:
                            pe.wait_ge(s_aux_read, n_aux[j] - 1)
                        w = ones[:, :] if kind in NORMED else cst1[:, 2, :]
                        src = cbuf(j) if kind in NORMED else pbuf(j)
                        if kind == "k":
                            mm(ps[5][:, 0:CTX], w, src[:, 0:CTX], start=True, stop=True)
                            last = mm(ps[4][:, :], w, src[:, CTX + 4:TOK + 4], start=True, stop=True)
                        elif kind == "rk":
                            mm(ps[5][:, 0:CTX], w, src[:, 0:CTX], start=True, stop=True)
                            last = mm(ps[4][:, :], w, src[:, CTX:TOK], start=True, stop=True)
                        else:
                            last = mm(ps[4][:, :], w, src[:, 0:LAT], start=True, stop=True)
                        last.then_inc(s_aux_done, 1)
                    if kind == "ab":
                        pe.wait_ge(s_pread, j + 1)
                        for c in range(NC):
                            last = nc.tensor.transpose(ps[6][:, 16 * c:16 * c + 16],
                                                       pbuf(j)[0:16, c * P:(c + 1) * P], ident[0:16, 0:16])
                        last.then_inc(s_abt, 1)

            pe.wait_ge(s_pread, len(items))
            pe.wait_ge(s_aux_read, n_aux[len(items) - 1])
            for q in range(H):
                sl = slot[0] % SLOTS
                slot[0] += 1
                pe.wait_ge(s_hi, n_hi.up())
                pe.wait_ge(s_lo, n_lo.up())
                for t in range(NC):
                    for kk in range(2):
                        k = 2 * q + kk
                        wh = w_hi[:, sl, 4 * kk:4 * kk + 4, :].rearrange("p a n -> p (a n)")
                        wl = w_lo[:, sl, 4 * kk:4 * kk + 4, :].rearrange("p a n -> p (a n)")
                        xh, xl = (h1[:, k, a, t * P:(t + 1) * P] for a in range(2))
                        mm(ps[t][:, :], xh, wh, start=(k == 0), stop=False, skip_group_check=True)
                        mm(ps[t][:, :], xh, wl, start=False, stop=False, skip_group_check=True)
                        last = mm(ps[t][:, :], xl, wh, start=False, stop=(k == KT - 1), skip_group_check=True)
                last.then_inc(s_done, 1)

            pe.wait_ge(s_g, 1)
            g = tok[:, 0, :]
            mm(ps[7][:, 128:152], cst1[:, 0, :], g[:, 0:24], start=True, stop=True)
            mm(ps[7][:, 152:176], cst1[:, 1, :], g[:, 24:48], start=True, stop=True)
            mm(ps[7][:, 192:240], ones[:, :], g, start=True, stop=True).then_inc(s_cum, 1)

            pe.wait_ge(s_fin, n_aux[-1])
            pe.wait_ge(s_sil, 12)
            for j, (src, c) in enumerate(turned):
                if j >= 2:
                    pe.wait_ge(s_turned, j - 1)
                else:
                    pe.wait_ge(s_rv, 6)
                src = {"k": kT, "v": vfm, "rk": rkT}[src]
                for h in range(H):
                    last = nc.tensor.transpose(ps[j % 2][:, h * P:(h + 1) * P], src[:, h, c * P:(c + 1) * P],
                                               ident[:, :])
                last.then_inc(s_turn, 1)
            pe.wait_ge(s_turned, len(turned))

            for s in range(NC):
                for d in range(2):
                    c, b, n = order[d][s], 4 * d, 2 * s + d
                    cs = slice(c * P, (c + 1) * P)
                    lat = slice(c * P - CTX, (c + 1) * P - CTX)
                    if c >= NCC:
                        if d == 0:
                            if s > NCC:
                                pe.wait_ge(s_rm, s - NCC)
                            for h in range(H):
                                last = mm(ps[b][:, h * P:(h + 1) * P], rkT[:, h, cs], rqT[:, h, lat],
                                          start=True, stop=True)
                            last.then_inc(s_rqk, 1)
                            pe.wait_ge(s_rm, s - NCC + 1)
                        pe.wait_ge(s_rqx[d], s - NCC + 1)
                        if s > NCC:
                            pe.wait_ge(s_ro[d], s - NCC)
                        pe.wait_ge(s_rS[d], s)
                        for h in range(H):
                            o = ps[b + 1][:, h * P:(h + 1) * P]
                            last = mm(o, retS[d][:, h, :], rt[3 + d][:, h, :], start=True, stop=(d == 1))
                            if d == 0:
                                last = mm(o, rvtok[:, c, h * P:(h + 1) * P], rt[2][:, h, :], start=False, stop=True)
                        last.then_inc(s_rod[d], 1)
                    if s < NC - 1:
                        pe.wait_ge(s_rkz[d], s + 1)
                        if s:
                            pe.wait_ge(s_rS[d], s)
                        for h in range(H):
                            last = mm(ps[b + 2][:, h * P:(h + 1) * P], rt[d][:, h, :],
                                      rvtok[:, c, h * P:(h + 1) * P], start=True, stop=True)
                        last.then_inc(s_rkv[d], 1)
            pe.wait_ge(s_ro[1], 4)
            pe.wait_ge(s_ro[0], 4)
            pe.wait_ge(s_rS[0], NC - 1)
            pe.wait_ge(s_rS[1], NC - 1)

            for s in range(NC):
                both = [(d, order[d][s], 4 * d, gt[d]) for d in range(2)]
                for d, c, b, t in both:
                    cs = slice(c * P, (c + 1) * P)
                    U = cst1[:, d, :]
                    if s:
                        pe.wait_ge(s_nwT[d], s)
                        pe.wait_ge(s_gx[d], 7 * s)
                    if s > NCC:
                        pe.wait_ge(s_go[d], s - NCC)
                    for h in range(H):
                        col = 24 * d + 4 * c + h
                        mm(ps[b][:, h * P:(h + 1) * P], tok[:, 0, col:col + 1].to_broadcast([P, P]), U,
                           start=True, stop=True)
                    for h in range(H):
                        last = mm(ps[b + 1][:, h * P:(h + 1) * P], kT[:, h, cs], kT[:, h, cs],
                                  start=True, stop=True)
                    if c >= NCC:
                        for h in range(H):
                            last = mm(ps[b + 2][:, h * P:(h + 1) * P], kT[:, h, cs],
                                      qT[:, h, c * P - CTX:(c + 1) * P - CTX], start=True, stop=True)
                    last.then_inc(s_rows[d], 1)
                for lev in range(7):
                    for d, c, b, t in both:
                        E, NA, Xi, XT, Y = t[0:5]
                        if lev == 0:
                            pe.wait_ge(s_na[d], s + 1)
                            for h in range(H):
                                last = nc.tensor.transpose(ps[b + 1][:, h * P:(h + 1) * P], NA[:, h, :], ident[:, :])
                            last.then_inc(s_gp[d], 1)
                        else:
                            pe.wait_ge(s_gx[d], 7 * s + lev)
                            for h in range(H):
                                last = mm(ps[b][:, h * P:(h + 1) * P], NA[:, h, :], Xi[:, h, :],
                                          start=True, stop=True)
                            last.then_inc(s_gy[d], 1)
                    for d, c, b, t in both:
                        E, NA, Xi, XT, Y = t[0:5]
                        if 0 < lev:
                            pe.wait_ge(s_gyc[d], 6 * s + lev)
                            if lev > 1:
                                pe.wait_ge(s_gxt[d], 5 * s + lev - 1)
                            for h in range(H):
                                if lev < 6:
                                    last = mm(ps[b + 1][:, h * P:(h + 1) * P], XT[:, h, :], Y[:, h, :],
                                              start=True, stop=True)
                                else:
                                    last = mm(ps[b + 1][:, h * P:(h + 1) * P], Y[:, h, :], XT[:, h, :],
                                              start=True, stop=True)
                            last.then_inc(s_gp[d], 1)
                    for d, c, b, t in both:
                        E, NA, Xi, XT, Y = t[0:5]
                        if 0 < lev < 6:
                            pe.wait_ge(s_gx[d], 7 * s + lev + 1)
                            for h in range(H):
                                last = nc.tensor.transpose(ps[b + 2][:, h * P:(h + 1) * P], Xi[:, h, :], ident[:, :])
                            last.then_inc(s_gt[d], 1)
                for d, c, b, t in both:
                    XT, kG = t[3], t[8]
                    pe.wait_ge(s_gx[d], 7 * s + 7)
                    pe.wait_ge(s_kg[d], s + 1)
                    for h in range(H):
                        last = mm(ps[b][:, h * P:(h + 1) * P], kG[:, h, :], XT[:, h, :], start=True, stop=True)
                    last.then_inc(s_wT[d], 1)
                for d, c, b, t in both:
                    XT, nwT, S = t[3], t[7], t[11]
                    if s:
                        pe.wait_ge(s_nwT[d], s + 1)
                        pe.wait_ge(s_gS[d], s)
                    for h in range(H):
                        o = ps[b + 3][:, h * P:(h + 1) * P]
                        last = mm(o, XT[:, h, :], vtok[:, c, h, :], start=True, stop=(s == 0))
                        if s:
                            last = mm(o, nwT[:, h, :], S[:, h, :], start=False, stop=True)
                    last.then_inc(s_vp[d], 1)
                for d, c, b, t in both:
                    QK, qd, kd, vn, S = t[5], t[6], t[9], t[10], t[11]
                    pe.wait_ge(s_vn[d], s + 1)
                    if c >= NCC:
                        for h in range(H):
                            o = ps[b + 2][:, h * P:(h + 1) * P]
                            mm(o, S[:, h, :], qd[:, h, :], start=True, stop=False)
                            last = mm(o, vn[:, h, :], QK[:, h, :], start=False, stop=True)
                        last.then_inc(s_god[d], 1)
                    if s < NC - 1:
                        for h in range(H):
                            last = mm(ps[b + 3][:, h * P:(h + 1) * P], kd[:, h, :], vn[:, h, :],
                                      start=True, stop=True)
                        last.then_inc(s_kv[d], 1)

            for j in range(2 * H):
                if j == 0:
                    pe.wait_ge(s_go[0], 4)
                    pe.wait_ge(s_go[1], 4)
                if j >= 2:
                    pe.wait_ge(s_hread, j - 1)
                pe.wait_ge(s_hsq, j + 1)
                src = ogdn if j < H else oret
                mm(ps[2 * (j % 2)][:, :], ones[:, :], tmp[j % 2][:, :], start=True, stop=True)
                mm(ps[2 * (j % 2) + 1][:, :], ones[:, :], src[:, j % H, :], start=True, stop=True).then_inc(s_hss, 1)

            n_pre, n_q, n_x, n_prod, n_hid = Tally(), Tally(), Tally(), Tally(), Tally()

            def x_outs(bank, wait=None):
                return lambda k: [(bank[:, :], *pair(k), k == 0, k == KT - 1)]

            def norm_sums(seq, mean=True):
                for i, k in enumerate(seq):
                    pe.wait_ge(s_pre, n_pre.up())
                    if mean:
                        mm(ps[seq[0]][:, :], ones[:, :], X[:, k, :], start=(i == 0), stop=(i == KT - 1),
                           skip_group_check=True)
                pe.wait_ge(s_qadd, n_q.up(KT))
                mm(ps[seq[1]][:, :], ones[:, :], tmp[2][:, :], start=True, stop=True).then_inc(s_stat, 1)

            def ffn(mean=True):
                ready = n_x.up(KT)
                with rounds(pe, FT // 2, (n_hi, 4), (n_lo, 4), (n_prod, 2)):
                    for j in range(2):
                        if j == 0:
                            pe.wait_ge(s_xlo, ready)
                        pe.wait_ge(s_prod, n_prod.up())
                        chunk(x_outs(ps[2 * j]))
                        chunk(x_outs(ps[2 * j + 1]))
                first = [True]

                def down(k, seq, a, b, tiles=False):
                    s = slot[0] % SLOTS
                    slot[0] += 1
                    hh, hl = acts[:, 8 + k, 0, :] if isinstance(k, int) else acts[:, bass.ds(k + 8, 1), 0, :], \
                        acts[:, 8 + k, 1, :] if isinstance(k, int) else acts[:, bass.ds(k + 8, 1), 1, :]
                    pe.wait_ge(s_hid, n_hid.up())
                    pe.wait_ge(s_hi, n_hi.up())
                    for i, m in enumerate(seq):
                        if a and i == 4:
                            pe.wait_ge(s_prod, n_prod.now + 2)
                        mm(ps[m][:, :], w_hi[:, s, m, :], hh, start=a, stop=False, skip_group_check=True)
                        mm(ps[m][:, :], w_hi[:, s, m, :], hl, start=False, stop=False, skip_group_check=True)
                    pe.wait_ge(s_lo, n_lo.up())
                    for i, m in enumerate(seq):
                        last = mm(ps[m][:, :], w_lo[:, s, m, :], hh, start=False, stop=b, skip_group_check=True)
                        if b and i < KT - 1:
                            last.then_inc(s_out, 1)
                    last.then_inc(s_done, 1)

                seq = DOWN
                down(0, seq, True, False)
                down(1, seq, False, False)
                with rounds(pe, 4, (n_hi, 4), (n_lo, 4), (n_hid, 4)) as i:
                    for j in range(4):
                        down(i * 4 + (2 + j), seq, False, False)
                for k in range(18, FT):
                    down(k, seq, False, k == FT - 1)
                norm_sums(seq, mean)

            pe.wait_ge(s_y, KT)
            for m in range(KT):
                chunk(x_outs(ps[m]))
            norm_sums(range(KT), mean=False)
            ffn(mean=False)

            n_mix = {q: Tally() for q in ("ya", "xc", "yb", "merge", "half", "gate")}
            tallies = [(n_hi, N_LAYER), (n_lo, N_LAYER), (n_pre, 24), (n_q, 24), (n_x, 24), (n_prod, 44),
                       (n_hid, 44), (n_mix["ya"], KT), (n_mix["xc"], KT), (n_mix["yb"], KT),
                       (n_mix["merge"], KT), (n_mix["half"], H), (n_mix["gate"], KT)]
            with rounds(pe, LAYERS, *tallies):
                ffn()
                pe.wait_ge(s_xlo, n_x.up(KT))
                for f in range(KT):
                    b = 3 * (f % 2)
                    if f >= 2:
                        pe.wait_ge(s_ya, n_mix["ya"].up())
                    for j in range(3):
                        chunk(x_outs(ps[b + j]))
                n_mix["ya"].up(2)
                for h in range(H):
                    if h == 0:
                        pe.wait_ge(s_ya, n_mix["ya"].now)
                    if h:
                        pe.wait_ge(s_gelu, n_mix["gate"].up(2))
                    for j in range(4):
                        chunk(x_outs(ps[j]))
                    if h:
                        pe.wait_ge(s_sig, n_mix["half"].up())
                    pe.wait_ge(s_xc, n_mix["xc"].up(2))

                    def gates(t):
                        g, m, k = t // 4, (t // 2) % 2, t % 2
                        return [(ps[4 + 2 * g + m][:, :], *pair(32 + k), k == 0, k == 1)]

                    chunk(gates)
                n_mix["gate"].up(2)
                n_mix["half"].up(1)
                banks_read = (n_mix["gate"].now, n_mix["half"].now)
                ready = n_mix["yb"].up(KT)
                with rounds(pe, 4, (n_hi, 8), (n_lo, 8), (n_mix["merge"], 2)):
                    for j in range(2):
                        if j == 0:
                            pe.wait_ge(s_ya, n_mix["ya"].now)
                            pe.wait_ge(s_yb, ready)
                            pe.wait_ge(s_gelu, banks_read[0])
                            pe.wait_ge(s_sig, banks_read[1])
                        pe.wait_ge(s_merge, n_mix["merge"].up())
                        b = 4 * j
                        chunk(lambda k: [(ps[b][:, :], *pair(8 + k), k == 0, k == KT - 1)])
                        chunk(x_outs(ps[b + 1]))
                        chunk(lambda k: [(ps[b + 2][:, :], *pair(16 + k), k == 0, k == KT - 1)])
                        chunk(x_outs(ps[b + 3]))
                pe.wait_ge(s_merge, n_mix["merge"].now + 2)
                pe.wait_ge(s_mlo, n_mix["merge"].now)
                for m in range(KT):
                    chunk(lambda k: [(ps[m][:, :], *pair(24 + k), k == 0, k == KT - 1)])
                norm_sums(range(KT))
                ffn()

        @block.scalar
        def _(act):
            A = nc.scalar.activation
            step = Tally()

            def link(ins):
                ins.then_inc(s_act, 1)
                act.wait_ge(s_act, step.up())

            slot = [0]
            loaded, used = [Tally(), Tally()], Tally()

            def hi_part():
                s = slot[0] % SLOTS
                slot[0] += 1
                act.wait_ge(s_raw[s % RAW], loaded[s % RAW].up(16))
                A(w_hi[:, s, :, :], raw[:, s % RAW, :, :], ACT.Copy).then_inc(s_hi, 1)

            def done():
                act.wait_ge(s_done, used.up())
                hi_part()

            chunks = lambda n: ((used, n), (loaded[0], 8 * n), (loaded[1], 8 * n))

            act.wait_ge(s_prm, 16)
            A(csil[:, :], prm[:, C_COND:C_COND + 2 * KT], ACT.Silu).then_inc(s_csil, 1)
            act.wait_ge(s_xin, 16)
            for k in range(KT):
                if k >= 2:
                    act.wait_ge(s_sqadd, k - 1)
                A(big[k % 2][:, 0:TOK], xin[:, k, :], ACT.Square).then_inc(s_sq, 1)
            act.wait_ge(s_ss, 1)
            act.wait_ge(s_eps, 1)
            A(big[3][:, 0:CTX], ps[2][:, 0:CTX], ACT.Sqrt, scale=1.0 / D, bias=epsc[:, 0:1])
            A(big[3][:, CTX:TOK], ps[1][:, :], ACT.Sqrt, scale=1.0 / D, bias=epsc[:, 0:1]).then_inc(s_std0, 1)
            for _ in range(SLOTS):
                hi_part()
            for k in range(KT):
                act.wait_ge(s_hval, k + 1)
                A(h1[:, k, 0, :], big[k % 2][:, 0:TOK], ACT.Copy).then_inc(s_hhi, 1)

            n = len(items)
            for i in range(n + 2):
                if i < n:
                    kind, h = items[i]
                    L, C = ps[2 * (i % 2)], ps[2 * (i % 2) + 1]
                    done()
                    if kind in CONV + ROPED + ("ab",):
                        b = pbuf(i)
                        if i >= 2:
                            act.wait_ge(s_cdone, n_c[i - 2])
                        if i >= 2 and items[i - 2][0] in ROPED:
                            act.wait_ge(s_aux_done, n_aux[i - 2])
                    if kind in CONV:
                        off, o2 = (2, CTX + 6) if kind != "q" else (2, 2)
                        if i < 2 or (kind == "q" and h < 2):
                            z = epsc[:, 2:4]
                            A(b[:, 0:2], z, ACT.Copy)
                            if kind != "q":
                                A(b[:, CTX + 2:CTX + 4], z, ACT.Copy)
                                A(b[:, CTX + 4:CTX + 6], z, ACT.Copy)
                                A(b[:, TOK + 6:TOK + 8], z, ACT.Copy)
                            else:
                                A(b[:, LAT + 2:LAT + 4], z, ACT.Copy)
                        if kind != "q":
                            A(b[:, 2:CTX + 2], C[:, 0:CTX], ACT.Copy)
                        A(b[:, o2:o2 + LAT], L[:, :], ACT.Copy).then_inc(s_pread, 1)
                    elif kind in ROPED:
                        if kind == "rk":
                            A(b[:, 0:CTX], C[:, 0:CTX], ACT.Copy)
                            link(A(b[:, CTX:TOK], L[:, :], ACT.Copy))
                        else:
                            link(A(b[:, 0:LAT], L[:, :], ACT.Copy))
                        act.sem_inc(s_pread, 1)
                        act.sem_inc(s_aux_in, 1)
                    elif kind == "ab":
                        A(b[0:16, 0:CTX], C[0:16, 0:CTX], ACT.Copy)
                        A(b[0:16, CTX:TOK], L[0:16, :], ACT.Copy).then_inc(s_pread, 1)
                    else:
                        if kind == "z" and h == 0:
                            act.wait_ge(s_fin, n_aux[n_last_rope])
                        A((zs if kind == "z" else rgs)[:, h, :], L[:, :], ACT.Silu).then_inc(s_pread, 1)
                j = i - 1
                if 0 <= j < n and items[j][0] in CONV:
                    kind, h = items[j]
                    act.wait_ge(s_cdone, n_c[j])
                    dst, c = {"k": kT, "q": qT, "v": vfm}[kind], cbuf(j)
                    segs = [(slice(0, LAT), slice(0, LAT))] if kind == "q" else \
                        [(slice(0, CTX), slice(0, CTX)), (slice(CTX, TOK), slice(CTX + 4, TOK + 4))]
                    for a, b in segs:
                        last = A(dst[:, h, a], c[:, b], ACT.Silu)
                    last.then_inc(s_sil, 1)
                    if kind in NORMED:
                        act.wait_ge(s_sil, n_conv[j])
                        for a, b in segs:
                            last = A(c[:, b], dst[:, h, a], ACT.Square)
                        last.then_inc(s_aux_in, 1)
                j = i - 2
                if 0 <= j < n and items[j][0] in NORMED:
                    kind, h = items[j]
                    act.wait_ge(s_aux_done, n_aux[j])
                    if n_aux[j] > 1:
                        act.wait_ge(s_fin, n_aux[j] - 1)
                    r = big[4]
                    if kind == "k":
                        A(r[:, 0:CTX], ps[5][:, 0:CTX], ACT.Sqrt, bias=epsc[:, 0:1])
                        last = A(r[:, CTX:TOK], ps[4][:, :], ACT.Sqrt, bias=epsc[:, 0:1])
                    else:
                        last = A(r[:, 0:LAT], ps[4][:, :], ACT.Sqrt, scale=float(P), bias=epsc[:, 1:2])
                    last.then_inc(s_aux_read, 1)
            for _ in range(H):
                done()
            for t in range(NC):
                A(rvtok[:, t, :], ps[t][:, :], ACT.Copy).then_inc(s_rv, 1)

            act.wait_ge(s_spa, 1)
            link(A(spw[:, 2, :], spw[:, 1, :], ACT.Exp, scale=-1.0))
            link(A(gch[:, :], prm[:, C_ALOG:C_ALOG + 8], ACT.Exp))
            act.wait_ge(s_abt, 1)
            for d in range(2):
                A(tok[:, 1, 24 * d:24 * d + 24].rearrange("p (c h) -> p c h", h=H),
                  ps[6][:, 0:96].rearrange("p (c h) -> p c h", h=16)[:, :, 8 + 4 * d:12 + 4 * d],
                  ACT.Sigmoid).then_inc(s_beta, 1)
            act.wait_ge(s_lg, 1)
            A(gch[:, :], lgc[:, :], ACT.Exp, scale=float(P))
            A(zeta[:, 0:H], lgc[:, 0:H], ACT.Exp, scale=prm[:, C_DOWN:C_DOWN + 1])
            A(zeta[:, H:2 * H], lgc[:, H:2 * H], ACT.Exp, scale=prm[:, C_UP:C_UP + 1])
            act.wait_ge(s_rm4, 16)
            for d in range(2):
                for h in range(H):
                    A(rt[5 + d][:, h, :], mats[:, d, :], ACT.Exp, scale=lgc[:, 4 * d + h:4 * d + h + 1])
            for d in range(2):
                if d:
                    act.wait_ge(s_dec, 1)
                for h in range(H):
                    last = A(rt[7][:, h, :], mats[:, 2 + d, :], ACT.Exp, scale=lgc[:, 4 * d + h:4 * d + h + 1])
                last.then_inc(s_dexp, 1)
            act.wait_ge(s_Gc, 1)
            A(tok[:, 4, :], tok[:, 3, :], ACT.Exp)
            A(tok[:, 5, :], tok[:, 7, :], ACT.Exp)
            A(tok[:, 6, :], ps[7][:, 192:240], ACT.Exp).then_inc(s_eG, 1)
            act.wait_ge(s_turned, len(turned))

            for s in range(NC - 1):
                for d in range(2):
                    c = order[d][s]
                    if s:
                        act.wait_ge(s_rkv[d], s)
                    for h in range(H):
                        last = A(rt[d][:, h, :], rktok[:, c, h, :], ACT.Copy, scale=zeta[:, 4 * d + h:4 * d + h + 1])
                    last.then_inc(s_rkz[d], 1)

            for s in range(NC):
                both = [(d, order[d][s], 4 * d, gt[d]) for d in range(2)]
                for d, c, b, t in both:
                    act.wait_ge(s_dm[d], s + 1)
                    A(t[0][:, :, :], t[0][:, :, :], ACT.Exp).then_inc(s_e[d], 1)
                    if c >= NCC:
                        if s > NCC:
                            act.wait_ge(s_god[d], s - NCC)
                        A(t[6][:, :, :].rearrange("p h n -> p (h n)"), ps[b][:, :], ACT.Exp).then_inc(s_eg[d], 1)
                    if s:
                        act.wait_ge(s_kv[d], s)
                    for h in range(H):
                        col = 24 * d + 4 * c + h
                        A(t[8][:, h, :], ktok[:, c, h, :], ACT.Copy, scale=tok[:, 4, col:col + 1])
                        last = A(t[9][:, h, :], ktok[:, c, h, :], ACT.Copy, scale=tok[:, 5, col:col + 1])
                    last.then_inc(s_kg[d], 1)
                for lev in range(1, 7):
                    for d, c, b, t in both:
                        act.wait_ge(s_gy[d], 6 * s + lev)
                        A(t[4][:, :, :].rearrange("p h n -> p (h n)"), ps[b][:, :], ACT.Copy).then_inc(s_gyc[d], 1)
                    if lev < 6:
                        for d, c, b, t in both:
                            act.wait_ge(s_gt[d], 5 * s + lev)
                            A(t[3][:, :, :].rearrange("p h n -> p (h n)"), ps[b + 2][:, :],
                              ACT.Copy).then_inc(s_gxt[d], 1)
                for d, c, b, t in both:
                    act.wait_ge(s_wT[d], s + 1)
                    A(t[7][:, :, :].rearrange("p h n -> p (h n)"), ps[b][:, :], ACT.Copy,
                      scale=-1.0).then_inc(s_nwT[d], 1)
            for d in range(2):
                act.wait_ge(s_go[d], 4)

            act.dma_start(X[:, :, :], x_in[:, :, CTX:TOK]).then_inc(s_xres, 16)

            for j in range(2 * H):
                src = (ogdn if j < H else oret)[:, j % H, :]
                if j >= 2:
                    act.wait_ge(s_hss, j - 1)
                A(tmp[j % 2][:, :], src, ACT.Square).then_inc(s_hsq, 1)
                act.wait_ge(s_hss, j + 1)
                a, b = ps[2 * (j % 2)], ps[2 * (j % 2) + 1]
                if j:
                    act.wait_ge(s_hread, j)
                if j < H:
                    A(tmp[2][:, :], a[:, :], ACT.Sqrt, scale=1.0 / P, bias=epsc[:, 0:1]).then_inc(s_hstd, 1)
                else:
                    A(tmp[2][:, :], b[:, :], ACT.Square, scale=1.0 / P).then_inc(s_hm2, 1)
                    act.wait_ge(s_hvar, j - H + 1)
                    A(tmp[2][:, :], tmp[2][:, :], ACT.Sqrt, bias=epsc[:, 0:1]).then_inc(s_hstd, 1)
                act.wait_ge(s_yf, j + 1)
                A(acts[:, j, 0, :], tmp[3][:, :], ACT.Copy).then_inc(s_yh, 1)

            pre, qadd, xn = Tally(), Tally(), Tally()
            stat, var, prod = Tally(), Tally(), Tally()

            def norm(seq, mean=True, keep=False):
                for i, k in enumerate(seq):
                    act.wait_ge(s_pre, pre.up())
                    if i >= 2:
                        act.wait_ge(s_qadd, qadd.up())
                    A(tmp[i % 2][:, :], X[:, k, :], ACT.Square).then_inc(s_sqx, 1)
                qadd.up(2)
                act.wait_ge(s_stat, stat.up())
                if mean:
                    A(tmp[0][:, :], ps[seq[0]][:, :], ACT.Square, scale=1.0 / D).then_inc(s_msq, 1)
                    act.wait_ge(s_var, var.up())
                    A(tmp[1][:, :], tmp[1][:, :], ACT.Sqrt, bias=epsc[:, 4:5]).then_inc(s_std, 1)
                else:
                    A(tmp[1][:, :], ps[seq[1]][:, :], ACT.Sqrt, scale=1.0 / D, bias=epsc[:, 0:1]).then_inc(s_std, 1)
                for k in range(KT):
                    act.wait_ge(s_xn, xn.up())
                    A(acts[:, k, 0, :], (tmp[2 + k % 2][:, :] if keep else X[:, k, :]),
                      ACT.Copy).then_inc(s_xhi, 1)

            def ffn():
                with rounds(act, FT // 2, *chunks(4), (prod, 2)) as i:
                    for j in range(2):
                        done()
                        A(tmp[0][:, :], ps[2 * j][:, :], ACT.Silu).then_inc(s_silu, 1)
                        done()
                        act.wait_ge(s_prod, 2 + prod.up())
                        A(acts[:, bass.ds(i * 2 + (8 + j), 1), 0, :], tmp[1][:, :], ACT.Copy).then_inc(s_hh, 1)
                with rounds(act, FT // SLOTS, *chunks(SLOTS)):
                    for _ in range(SLOTS):
                        done()
                for _ in range(FT % SLOTS):
                    done()

            for m in range(KT):
                done()
            norm(range(KT), mean=False, keep=True)
            ffn()
            norm(DOWN, mean=False)

            yaf, xcf, sig, m2, hg, yb, merge = (Tally() for _ in range(7))
            tallies = [*chunks(N_LAYER), (pre, 24), (qadd, 24), (xn, 24), (stat, 3), (var, 3), (prod, 44),
                       (yaf, KT), (xcf, KT), (sig, H), (m2, H), (hg, KT), (yb, KT), (merge, KT)]
            with rounds(act, LAYERS, *tallies):
                ffn()
                norm(DOWN)
                for f in range(KT):
                    b = 3 * (f % 2)
                    done()
                    A(mt[0][:, 0:LAT], ps[b][:, :], ACT.Copy).then_inc(s_cs, 1)
                    done()
                    done()
                    act.wait_ge(s_yaf, yaf.up())
                    A(acts[:, 8 + f, 0, :], mt[3][:, 0:LAT], ACT.Copy).then_inc(s_yah, 1)

                def rows(h, j):
                    done()
                    A(mt[j][:, 3:LAT + 3], ps[j][:, :], ACT.Copy).then_inc(s_xr, 1)

                def split_rows():
                    for j in range(2):
                        act.wait_ge(s_xcf, xcf.up())
                        A(acts[:, 32 + j, 0, :], mt[2 + j][:, 0:LAT], ACT.Copy).then_inc(s_xch, 1)

                def split_h(h):
                    for j in range(2):
                        act.wait_ge(s_hg, hg.up())
                        A(acts[:, 16 + 2 * h + j, 0, :], mt[4 + j][:, 0:LAT], ACT.Copy).then_inc(s_ybh, 1)

                def roots():
                    act.wait_ge(s_m2, m2.up())
                    for j in range(2):
                        A(mt[8 + j][:, 0:LAT], mt[8 + j][:, 0:LAT], ACT.Sqrt).then_inc(s_root, 1)

                for h in range(H):
                    rows(h, 0)
                    if h:
                        roots()
                    rows(h, 1)
                    split_rows()
                    for j in range(2):
                        done()
                        if h and j == 0:
                            split_h(h - 1)
                        if h:
                            act.wait_ge(s_yb, yb.up())
                        A(mt[4 + j][:, 0:LAT], ps[2 + j][:, :], ACT.Gelu_apprx_tanh).then_inc(s_gelu, 1)
                    done()
                    for j in range(2):
                        f = 2 * h + j
                        A(mt[6 + j][:, 0:LAT], ps[4 + j][:, :], ACT.Sigmoid, bias=lay[:, L_RGB + f:L_RGB + f + 1])
                        last = A(mt[8 + j][:, 0:LAT], ps[6 + j][:, :], ACT.Sigmoid,
                                 bias=lay[:, L_RGB + KT + f:L_RGB + KT + f + 1])
                    last.then_inc(s_sig, 1)
                    act.wait_ge(s_sig, sig.up())
                    for j in range(2):
                        f = 2 * h + j
                        A(mt[10 + j][:, 0:LAT], mt[8 + j][:, 0:LAT], ACT.Exp, scale=lay[:, L_C8 + f:L_C8 + f + 1])
                        A(mt[12 + j][:, 0:LAT], mt[8 + j][:, 0:LAT], ACT.Tanh,
                          scale=lay[:, L_N8 + f:L_N8 + f + 1]).then_inc(s_ath, 1)
                roots()
                split_h(H - 1)
                yb.up(2)
                with rounds(act, 4, *chunks(8), (merge, 2)) as i:
                    for j in range(2):
                        b, m = 4 * j, i * 2 + j
                        done()
                        done()
                        A(tmp[0][:, :], ps[b + 1][:, :], ACT.Sigmoid,
                          bias=lay[:, bass.ds(m + L_BM, 1)]).then_inc(s_mg, 1)
                        done()
                        done()
                        A(tmp[1][:, :], ps[b + 3][:, :], ACT.Sigmoid,
                          bias=lay[:, bass.ds(m + (L_BM + KT), 1)]).then_inc(s_mg, 1)
                        act.wait_ge(s_merge, 2 + merge.up())
                        A(acts[:, bass.ds(m + 24, 1), 0, :], tmp[2][:, :], ACT.Copy).then_inc(s_mh, 1)
                for _ in range(KT):
                    done()
                norm(range(KT))
                ffn()
                norm(DOWN)
            act.dma_start(out, X[:, :, :]).then_inc(s_res, 16)
            act.wait_ge(s_res, 16)

        @block.vector
        def _(dve):
            V = nc.vector
            TT, TS, STT, CP = V.tensor_tensor, V.tensor_scalar, V.scalar_tensor_tensor, V.tensor_copy
            step = Tally()

            def link(ins):
                ins.then_inc(s_dve, 1)
                dve.wait_ge(s_dve, step.up())

            flat = lambda t: t[:, :, :].rearrange("p h n -> p (h n)")

            for j, v in ((0, EPS), (1, P * EPS), (2, 0.0), (3, 0.0), (4, LN_EPS)):
                last = V.memset(epsc[:, j:j + 1], v)
            last.then_inc(s_eps, 1)
            dve.sem_inc(s_prod, 2)
            dve.sem_inc(s_merge, 2)

            dve.wait_ge(s_cst, 64)
            link(CP(lmask[:, :, :].rearrange("p a n -> p (a n)"), masks_in[:, :]))

            acc = big[2]
            for k in range(KT):
                dve.wait_ge(s_sq, k + 1)
                if k == 0:
                    CP(acc[:, 0:TOK], big[0][:, 0:TOK]).then_inc(s_sqadd, 1)
                else:
                    dve.wait_ge(s_sqadd, k)
                    TT(acc[:, 0:TOK], acc[:, 0:TOK], big[k % 2][:, 0:TOK], ALU.add).then_inc(s_sqadd, 1)
            dve.wait_ge(s_sqadd, KT)
            dve.sem_inc(s_acc, 1)
            dve.wait_ge(s_prm, 16)
            dve.wait_ge(s_ada_done, ADA_M)
            link(TT(mod[:, :, :], ps[0][:, 0:2 * ADA_M].rearrange("p (m v) -> p m v", v=2),
                    prm[:, C_ADAB:C_ADAB + ADA_M].unsqueeze(2).to_broadcast([P, ADA_M, 2]), ALU.add))
            for j, part, v, g in ((0, 1, 0, C_GMIX), (1, 1, 1, C_GMIX), (2, 4, 0, C_GFFN)):
                last = STT(coef[:, j, :], mod[:, KT * part:KT * (part + 1), v], 1.0, prm[:, g:g + KT], ALU.add, ALU.mult)
            link(last)
            dve.wait_ge(s_std0, 1)
            link(V.reciprocal(big[3][:, 0:TOK], big[3][:, 0:TOK]))
            dve.sem_inc(s_mod, 1)
            for k in range(KT):
                b = big[k % 2]
                link(TT(xin[:, k, :], xin[:, k, :], big[3][:, 0:TOK], ALU.mult))
                TS(b[:, 0:CTX], xin[:, k, 0:CTX], coef[:, 1, k:k + 1], mod[:, k, 1:2], ALU.mult, ALU.add)
                TS(b[:, CTX:TOK], xin[:, k, CTX:TOK], coef[:, 0, k:k + 1], mod[:, k, 0:1], ALU.mult,
                   ALU.add).then_inc(s_hval, 1)
                dve.wait_ge(s_hhi, k + 1)
                TT(h1[:, k, 1, :], b[:, 0:TOK], f32(h1[:, k, 0, :]), ALU.subtract).then_inc(s_h1, 1)

            n = len(items)
            for i in range(n + 2):
                if i < n and items[i][0] in CONV + ROPED:
                    kind, h = items[i]
                    dve.wait_ge(s_pread, i + 1)
                    b, c = pbuf(i), cbuf(i)
                    if i >= 2 and items[i - 2][0] in NORMED + ROPED:
                        dve.wait_ge(s_aux_done, n_aux[i - 2])
                    if kind in CONV:
                        if i >= 2 and items[i - 2][0] in CONV:
                            dve.wait_ge(s_sil, n_conv[i - 2])
                        ct = {"q": 0, "k": 1, "v": 2}[kind] * H + h
                        w = [prm[:, C_CONV + 5 * ct + a:C_CONV + 5 * ct + a + 1] for a in range(5)]
                        m = LAT if kind == "q" else TOK + 4
                        link(TS(c[:, 0:m], b[:, 0:m], w[0], None, ALU.mult))
                        for a in range(1, 5):
                            last = STT(c[:, 0:m], b[:, a:m + a], w[a], c[:, 0:m], ALU.mult, ALU.add)
                            if a < 4:
                                link(last)
                        last.then_inc(s_cdone, 1)
                    else:
                        if n_c[i] == 2 * H + 1:
                            dve.wait_ge(s_rope, 16)
                        dst, o, m = (rkT, 0, TOK) if kind == "rk" else (rqT, 2 * TOK, LAT)
                        TT(dst[:, h, :], b[:, 0:m], rope_sb[:, o:o + m], ALU.mult).then_inc(s_cdone, 1)
                j = i - 2
                if j >= 0 and n_aux[j] > 1 and items[j][0] in NORMED + ROPED:
                    dve.wait_ge(s_fin, n_aux[j] - 1)
                if j >= 0 and items[j][0] in NORMED:
                    kind, h = items[j]
                    dst, m = (kT, TOK) if kind == "k" else (qT, LAT)
                    dve.wait_ge(s_aux_read, n_aux[j])
                    link(V.reciprocal(big[4][:, 0:m], big[4][:, 0:m]))
                    TT(dst[:, h, :], dst[:, h, :], big[4][:, 0:m], ALU.mult).then_inc(s_fin, 1)
                if j >= 0 and items[j][0] in ROPED:
                    kind, h = items[j]
                    c = big[4]
                    dve.wait_ge(s_aux_done, n_aux[j])
                    if kind == "rk":
                        TT(c[:, 0:CTX], ps[5][:, 0:CTX], rope_sb[:, TOK:TOK + CTX], ALU.mult)
                        TT(c[:, CTX:TOK], ps[4][:, :], rope_sb[:, TOK + CTX:2 * TOK], ALU.mult).then_inc(s_aux_read, 1)
                        dst, m = rkT, TOK
                    else:
                        TT(c[:, 0:LAT], ps[4][:, :], rope_sb[:, 2 * TOK + LAT:], ALU.mult).then_inc(s_aux_read, 1)
                        dst, m = rqT, LAT
                    dve.wait_ge(s_aux_read, n_aux[j])
                    TT(dst[:, h, :], dst[:, h, :], c[:, 0:m], ALU.add).then_inc(s_fin, 1)

            dve.wait_ge(s_abt, 1)
            v = [spw[:, j, :] for j in range(6)]
            ab = ps[6][:, 0:96].rearrange("p (c h) -> p c h", h=16)
            for d in range(2):
                TT(v[0][:, 24 * d:24 * d + 24].rearrange("p (c h) -> p c h", h=H), ab[:, :, 4 * d:4 * d + 4],
                   prm[:, C_DTB + 4 * d:C_DTB + 4 * d + 4].unsqueeze(1).to_broadcast([P, NC, H]), ALU.add)
            TS(v[0][:, 48:56], prm[:, C_RETL:C_RETL + 8], -1.0, None, ALU.mult)
            for l in range(LAYERS):
                a = C_LAY + l * L_W + L_AP
                last = TS(v[0][:, 56 + KT * l:56 + KT * (l + 1)], prm[:, a:a + KT], -1.0, None, ALU.mult)
            link(last)
            STT(v[1], v[0], -1.0, v[0], ALU.mult, ALU.max).then_inc(s_spa, 1)
            dve.wait_ge(s_spa, 1)
            dve.wait_ge(s_act, 8 + 2)
            link(TS(v[3], v[2], 2.0, None, ALU.add))
            link(V.reciprocal(v[3], v[3]))
            link(TT(v[3], v[3], v[2], ALU.mult))
            link(TT(v[4], v[3], v[3], ALU.mult))
            link(TS(v[5], v[4], 1.0 / 17, None, ALU.mult))
            for a in range(15, 1, -2):
                link(STT(v[5], v[5], 1.0 / a, v[4], ALU.add, ALU.mult))
            TS(v[1], v[0], 0.0, None, ALU.max)
            link(STT(v[5], v[5], 1.0, v[3], ALU.add, ALU.mult))
            link(STT(v[5], v[5], 2.0, v[1], ALU.mult, ALU.add))
            for d in range(2):
                last = STT(tok[:, 0, 24 * d:24 * d + 24].rearrange("p (c h) -> p c h", h=H),
                           v[5][:, 24 * d:24 * d + 24].rearrange("p (c h) -> p c h", h=H), -1.0,
                           gch[:, 4 * d:4 * d + 4].unsqueeze(1).to_broadcast([P, NC, H]), ALU.mult, ALU.mult)
            last.then_inc(s_g, 1)
            for l in range(LAYERS):
                a, b = C_LAY + l * L_W, v[5][:, 56 + KT * l:56 + KT * (l + 1)]
                TS(prm[:, a + L_C8:a + L_C8 + KT], b, -LRU_C, None, ALU.mult)
                TS(prm[:, a + L_N8:a + L_N8 + KT], b, LRU_C, None, ALU.mult)
            TS(lgc[:, :], v[5][:, 48:56], -1.0, None, ALU.mult).then_inc(s_lg, 1)
            dve.wait_ge(s_beta, 2)
            TS(tok[:, 2, :], tok[:, 1, :], -1.0, None, ALU.mult)
            for d in range(2):
                dve.wait_ge(s_dexp, d + 1)
                U = cst1[:, d, :].unsqueeze(1).to_broadcast([P, H, P])
                if d == 0:
                    TT(Dsum[:, :, :], rt[7][:, :, :], U, ALU.mult).then_inc(s_dec, 1)
                else:
                    link(TT(rt[7][:, :, :], rt[7][:, :, :], U, ALU.mult))
                    link(TT(Dsum[:, :, :], Dsum[:, :, :], rt[7][:, :, :], ALU.add))
            dve.wait_ge(s_cum, 1)
            link(CP(tok[:, 3, :], ps[7][:, 128:176]))
            TT(tok[:, 7, :], ps[7][:, 192:240], tok[:, 3, :], ALU.subtract).then_inc(s_Gc, 1)

            for j, (src, c) in enumerate(turned):
                dve.wait_ge(s_turn, j + 1)
                dst = {"k": ktok, "v": vtok, "rk": rktok}[src]
                CP(dst[:, c, :, :].rearrange("p h n -> p (h n)"), ps[j % 2][:, :]).then_inc(s_turned, 1)

            def add_rows(s, d, c, dst, bank):
                o = dst[:, :, c * P - CTX:(c + 1) * P - CTX]
                p = bank[:, :].rearrange("p (h n) -> p h n", h=H)
                return CP(o, p) if s < NCC + (NC - NCC) // 2 else TT(o, o, p, ALU.add)

            for s in range(NC):
                for d in range(2):
                    c, b = order[d][s], 4 * d
                    lat = slice(c * P - CTX, (c + 1) * P - CTX)
                    if c >= NCC:
                        if s > NCC:
                            dve.wait_ge(s_rod[d], s - NCC)
                        TT(rt[3 + d][:, :, :], rqT[:, :, lat], rt[5 + d][:, :, :], ALU.mult).then_inc(s_rqx[d], 1)
                        if d == 0:
                            dve.wait_ge(s_rqk, s - NCC + 1)
                            TT(rt[2][:, :, :], ps[b][:, :].rearrange("p (h n) -> p h n", h=H), Dsum[:, :, :],
                               ALU.mult).then_inc(s_rm, 1)
                        dve.wait_ge(s_rod[d], s - NCC + 1)
                        add_rows(s, d, c, oret, ps[b + 1]).then_inc(s_ro[d], 1)
                    if s < NC - 1:
                        dve.wait_ge(s_rkv[d], s + 1)
                        if s == 0:
                            CP(flat(retS[d]), ps[b + 2][:, :]).then_inc(s_rS[d], 1)
                        else:
                            for h in range(H):
                                last = STT(retS[d][:, h, :], retS[d][:, h, :], gch[:, 4 * d + h:4 * d + h + 1],
                                           ps[b + 2][:, h * P:(h + 1) * P], ALU.mult, ALU.add)
                            last.then_inc(s_rS[d], 1)

            I = ident[:, :].unsqueeze(1).to_broadcast([P, H, P])
            bank = lambda b: ps[b][:, :].rearrange("p (h n) -> p h n", h=H)

            def merge(dst, d, rows, lev, src):
                m = lmask[:, lev + 7 * (d ^ rows), :].unsqueeze(1).to_broadcast([P, H, P])
                return V.copy_predicated(dst[:, :, :], m, src)

            for s in range(NC):
                both = [(d, order[d][s], 4 * d, gt[d]) for d in range(2)]
                for d, c, b, t in both:
                    dve.wait_ge(s_rows[d], s + 1)
                    for h in range(H):
                        col = 24 * d + 4 * c + h
                        last = TS(t[0][:, h, :], ps[b][:, h * P:(h + 1) * P], tok[:, 3, col:col + 1], 0.0,
                                  ALU.subtract, ALU.min)
                    last.then_inc(s_dm[d], 1)
                    CP(t[2][:, :, :], I)
                    CP(t[3][:, :, :], I)
                for d, c, b, t in both:
                    dve.wait_ge(s_e[d], s + 1)
                    for h in range(H):
                        col = 24 * d + 4 * c + h
                        last = STT(t[1][:, h, :], ps[b + 1][:, h * P:(h + 1) * P], tok[:, 2, col:col + 1],
                                   t[0][:, h, :], ALU.mult, ALU.mult)
                    last.then_inc(s_na[d], 1)
                    if c >= NCC:
                        dve.wait_ge(s_na[d], s + 1)
                        link(TT(t[0][:, :, :], t[0][:, :, :], cst1[:, d, :].unsqueeze(1).to_broadcast([P, H, P]),
                                ALU.mult))
                        TT(t[5][:, :, :], bank(b + 2), t[0][:, :, :], ALU.mult)
                        dve.wait_ge(s_eg[d], s - NCC + 1)
                        TT(t[6][:, :, :], t[6][:, :, :], qT[:, :, c * P - CTX:(c + 1) * P - CTX], ALU.mult)
                for lev in range(7):
                    for d, c, b, t in both:
                        dve.wait_ge(s_gp[d], 7 * s + lev + 1)
                        if lev == 0:
                            dve.wait_ge(s_na[d], s + 1)
                            merge(t[3], d, 1, 0, t[1][:, :, :])
                        last = merge(t[2], d, 0, lev, bank(b + 1)) if lev < 6 else merge(t[3], d, 1, lev, bank(b + 1))
                        last.then_inc(s_gx[d], 1)
                for d, c, b, t in both:
                    dve.wait_ge(s_vp[d], s + 1)
                    for h in range(H):
                        col = 24 * d + 4 * c + h
                        last = TS(t[10][:, h, :], ps[b + 3][:, h * P:(h + 1) * P], tok[:, 1, col:col + 1], None,
                                  ALU.mult)
                    last.then_inc(s_vn[d], 1)
                for d, c, b, t in both:
                    if c >= NCC:
                        dve.wait_ge(s_god[d], s - NCC + 1)
                        add_rows(s, d, c, ogdn, ps[b + 2]).then_inc(s_go[d], 1)
                    if s < NC - 1:
                        dve.wait_ge(s_kv[d], s + 1)
                        for h in range(H):
                            col = 24 * d + 4 * c + h
                            if s == 0:
                                last = CP(t[11][:, h, :], ps[b + 3][:, h * P:(h + 1) * P])
                            else:
                                last = STT(t[11][:, h, :], t[11][:, h, :], tok[:, 6, col:col + 1],
                                           ps[b + 3][:, h * P:(h + 1) * P], ALU.mult, ALU.add)
                        last.then_inc(s_gS[d], 1)

            for j in range(2 * H):
                src = (ogdn if j < H else oret)[:, j % H, :]
                z = (zs if j < H else rgs)[:, j % H, :]
                gn = prm[:, C_GDNG:C_GDNG + 1] if j < H else prm[:, C_RETG:C_RETG + 1]
                a, b = ps[2 * (j % 2)], ps[2 * (j % 2) + 1]
                if j >= H:
                    dve.wait_ge(s_hm2, j - H + 1)
                    STT(tmp[2][:, :], a[:, :], 1.0 / P, tmp[2][:, :], ALU.mult, ALU.subtract).then_inc(s_hvar, 1)
                    dve.wait_ge(s_hvar, j - H + 1)
                    link(STT(src, b[:, :], -1.0 / P, src, ALU.mult, ALU.add))
                dve.wait_ge(s_hstd, j + 1)
                link(V.reciprocal(tmp[2][:, :], tmp[2][:, :]))
                link(TT(src, src, tmp[2][:, :], ALU.mult))
                dve.sem_inc(s_hread, 1)
                STT(tmp[3][:, :], src, gn, z, ALU.mult, ALU.mult).then_inc(s_yf, 1)
                dve.wait_ge(s_yf, j + 1)
                dve.wait_ge(s_yh, j + 1)
                TT(acts[:, j, 1, :], tmp[3][:, :], f32(acts[:, j, 0, :]), ALU.subtract).then_inc(s_y, 1)

            done, sqx, stat, msq = Tally(), Tally(), Tally(), Tally()
            std, xhi, silu, hh, out_t, prod, pre, qadd, xn, var, hid, xlo = (Tally() for _ in range(12))

            def norm(seq, residual, ready, mean=True, g=None, b=None, keep=False):
                q = tmp[2][:, :]
                dve.wait_ge(s_dve, step.now)
                for i, k in enumerate([*seq, None]):
                    if k is not None:
                        ready(i)
                        residual(k).then_inc(s_pre, 1)
                        pre.up()
                    if i == 1:
                        dve.wait_ge(s_sqx, sqx.up())
                        CP(q, tmp[0][:, :]).then_inc(s_qadd, 1)
                        qadd.up()
                    elif i > 1:
                        dve.wait_ge(s_sqx, sqx.up())
                        dve.wait_ge(s_qadd, qadd.now)
                        TT(q, q, tmp[(i - 1) % 2][:, :], ALU.add).then_inc(s_qadd, 1)
                        qadd.up()
                dve.wait_ge(s_stat, stat.up())
                mb = ps[seq[0]][:, :]
                if mean:
                    dve.wait_ge(s_msq, msq.up())
                    STT(tmp[1][:, :], ps[seq[1]][:, :], 1.0 / D, tmp[0][:, :], ALU.mult, ALU.subtract).then_inc(s_var, 1)
                    var.up()
                dve.wait_ge(s_std, std.up())
                if mean:
                    dve.wait_ge(s_var, var.now)
                link(V.reciprocal(tmp[1][:, :], tmp[1][:, :]))
                dve.wait_ge(s_pre, pre.now)
                for k in range(KT):
                    if keep and k:
                        dve.wait_ge(s_xlo, xlo.now)
                    dst = tmp[2 + k % 2][:, :] if keep else X[:, k, :]
                    src = X[:, k, :]
                    if mean:
                        link(STT(X[:, k, :], mb, -1.0 / D, X[:, k, :], ALU.mult, ALU.add))
                    link(TT(dst, src, tmp[1][:, :], ALU.mult))
                    TS(dst, dst, g(k), b(k) if b else None, ALU.mult, *([ALU.add] if b else [])).then_inc(s_xn, 1)
                    dve.wait_ge(s_xn, xn.up())
                    dve.wait_ge(s_xhi, xhi.up())
                    TT(acts[:, k, 1, :], dst, f32(acts[:, k, 0, :]), ALU.subtract).then_inc(s_xlo, 1)
                    xlo.up()

            def chunk_ready(_):
                dve.wait_ge(s_done, done.up())

            def down_ready(i):
                if i < KT - 1:
                    dve.wait_ge(s_out, out_t.up())
                else:
                    dve.wait_ge(s_done, done.up())

            def hidden():
                with rounds(dve, FT // 2, (done, 4), (silu, 2), (prod, 2), (hh, 2), (hid, 2)) as i:
                    for j in range(2):
                        dve.wait_ge(s_hid, hid.now)
                        dve.wait_ge(s_silu, silu.up())
                        dve.wait_ge(s_done, done.up(2))
                        TT(tmp[1][:, :], tmp[0][:, :], ps[2 * j + 1][:, :], ALU.mult).then_inc(s_prod, 1)
                        dve.wait_ge(s_prod, 2 + prod.up())
                        dve.wait_ge(s_hh, hh.up())
                        TT(acts[:, bass.ds(i * 2 + (8 + j), 1), 1, :], tmp[1][:, :],
                           f32(acts[:, bass.ds(i * 2 + (8 + j), 1), 0, :]), ALU.subtract).then_inc(s_hid, 1)
                        hid.up()
                done.up(FT - 1)

            def modulated(part):
                return lambda k: STT(X[:, k, :], ps[k][:, :], mod[:, KT * part + k, 0:1], X[:, k, :],
                                     ALU.mult, ALU.add)

            done.up(N_PROJ)
            dve.wait_ge(s_xres, 16)
            norm(range(KT), modulated(2), chunk_ready, mean=False, keep=True,
                 g=lambda k: coef[:, 2, k:k + 1], b=lambda k: mod[:, 3 * KT + k, 0:1])
            hidden()
            norm(DOWN, modulated(5), down_ready, mean=False, g=lambda k: prm[:, C_FING + k:C_FING + k + 1])

            cs, yah, xr, xch, ybh, sig, ath, root, mg, mh, gelu = (Tally() for _ in range(11))
            yaf, xcf, m2, hg, merged, ya, mlo = (Tally() for _ in range(7))
            tallies = [(done, N_LAYER), (sqx, 24), (stat, 3), (msq, 3), (std, 3), (xhi, 24), (silu, 44), (hh, 44),
                       (out_t, 14), (prod, 44), (pre, 24), (qadd, 24), (xn, 24), (var, 3), (cs, KT), (yah, KT),
                       (xr, KT), (xch, KT), (ybh, KT), (sig, H), (ath, KT), (root, KT), (mg, 2 * KT), (mh, KT),
                       (gelu, KT), (yaf, KT), (xcf, KT), (m2, H), (hg, KT), (merged, KT), (ya, KT), (mlo, KT), (hid, 44),
                       (xlo, 24), (step, LAYER_STEPS)]

            def scaled_x():
                dve.wait_ge(s_xlo, xlo.now)
                for k in range(KT):
                    last = TS(X[:, k, :], X[:, k, :], ALPHA, None, ALU.mult)
                last.then_inc(s_dve, 1)
                step.up()

            def ln(j):
                c = lambda base: (lambda k: lay[:, base + KT * j + k:base + KT * j + k + 1])
                return dict(g=c(L_LNG), b=c(L_LNB))

            half = lambda k: STT(X[:, k, :], ps[k][:, :], 0.5, X[:, k, :], ALU.mult, ALU.add)
            whole = lambda k: TT(X[:, k, :], X[:, k, :], ps[k][:, :], ALU.add)
            with rounds(dve, LAYERS, *tallies) as l:
                link(CP(lay[:, :], prm[:, bass.ds(l * L_W + C_LAY, L_W)]))
                scaled_x()
                hidden()
                norm(DOWN, half, down_ready, **ln(0))
                scaled_x()

                par = lambda c: lay[:, c:c + 1]
                link(V.memset(mt[1][:, 0:2], 0.0))
                for f in range(KT):
                    b = 3 * (f % 2)
                    dve.wait_ge(s_cs, cs.up())
                    dve.wait_ge(s_done, done.up(2))
                    link(TT(mt[1][:, 2:LAT + 2], mt[0][:, 0:LAT], ps[b + 1][:, :], ALU.mult))
                    y = mt[2][:, 0:LAT]
                    link(TS(y, mt[1][:, 0:LAT], par(L_SC + f), None, ALU.mult))
                    for a in (1, 2):
                        link(STT(y, mt[1][:, a:LAT + a], par(L_SC + KT * a + f), y, ALU.mult, ALU.add))
                    dve.wait_ge(s_done, done.up())
                    dve.wait_ge(s_ya, ya.now)
                    TT(mt[3][:, 0:LAT], y, ps[b + 2][:, :], ALU.mult).then_inc(s_yaf, 1)
                    dve.wait_ge(s_yaf, yaf.up())
                    dve.wait_ge(s_yah, yah.up())
                    TT(acts[:, 8 + f, 1, :], mt[3][:, 0:LAT], f32(acts[:, 8 + f, 0, :]), ALU.subtract).then_inc(s_ya, 1)
                    ya.up()

                for j in range(2):
                    last = V.memset(mt[j][:, 0:3], 0.0)
                link(last)
                for h in range(H + 1):
                    for j in range(2):
                        f = 2 * h + j
                        if h < H:
                            dve.wait_ge(s_xr, xr.up())
                            y = mt[2 + j][:, 0:LAT]
                            link(TS(y, mt[j][:, 0:LAT], par(L_RC + f), par(L_RCB + f), ALU.mult, ALU.add))
                            for a in (1, 2, 3):
                                last = STT(y, mt[j][:, a:LAT + a], par(L_RC + KT * a + f), y, ALU.mult, ALU.add)
                                if a < 3:
                                    link(last)
                            last.then_inc(s_xcf, 1)
                            xcf.up()
                        if h and j == 0:
                            for i in range(2):
                                dve.wait_ge(s_root, root.up())
                                link(V.memset(mt[8 + i][:, 0:1], 1.0))
                                link(TT(mt[6 + i][:, 0:LAT], mt[6 + i][:, 0:LAT], mt[8 + i][:, 0:LAT], ALU.mult))
                                link(V.tensor_tensor_scan(mt[12 + i][:, 0:LAT], mt[10 + i][:, 0:LAT],
                                                          mt[6 + i][:, 0:LAT], 0.0, ALU.mult, ALU.add))
                                dve.wait_ge(s_gelu, gelu.up())
                                TT(mt[4 + i][:, 0:LAT], mt[12 + i][:, 0:LAT], mt[4 + i][:, 0:LAT],
                                   ALU.mult).then_inc(s_hg, 1)
                                hg.up()
                    if h < H:
                        dve.wait_ge(s_xcf, xcf.now)
                        for j in range(2):
                            dve.wait_ge(s_xch, xch.up())
                            TT(acts[:, 32 + j, 1, :], mt[2 + j][:, 0:LAT], f32(acts[:, 32 + j, 0, :]),
                               ALU.subtract).then_inc(s_xc, 1)
                    if h:
                        dve.wait_ge(s_hg, hg.now)
                        for j in range(2):
                            p = 16 + 2 * (h - 1) + j
                            dve.wait_ge(s_ybh, ybh.up())
                            TT(acts[:, p, 1, :], mt[4 + j][:, 0:LAT], f32(acts[:, p, 0, :]),
                               ALU.subtract).then_inc(s_yb, 1)
                    if h < H:
                        dve.wait_ge(s_sig, sig.up())
                        for j in range(2):
                            TT(mt[6 + j][:, 0:LAT], mt[6 + j][:, 0:LAT], mt[2 + j][:, 0:LAT], ALU.mult)
                        dve.wait_ge(s_ath, ath.up(2))
                        for j in range(2):
                            last = TT(mt[8 + j][:, 0:LAT], mt[10 + j][:, 0:LAT], mt[10 + j][:, 0:LAT], ALU.mult)
                        link(last)
                        for j in range(2):
                            last = STT(mt[8 + j][:, 0:LAT], mt[8 + j][:, 0:LAT], 1.0, mt[12 + j][:, 0:LAT],
                                       ALU.add, ALU.mult)
                        last.then_inc(s_m2, 1)
                        dve.wait_ge(s_m2, m2.up())
                done.up(5 * H)

                with rounds(dve, 4, (done, 8), (mg, 4), (merged, 2), (mh, 2), (mlo, 2), (step, 4)) as i:
                    for j in range(2):
                        b = 4 * j
                        dve.wait_ge(s_mg, mg.up())
                        link(TT(tmp[0][:, :], tmp[0][:, :], ps[b][:, :], ALU.mult))
                        dve.wait_ge(s_mg, mg.up())
                        dve.wait_ge(s_done, done.up(4))
                        link(TT(tmp[1][:, :], tmp[1][:, :], ps[b + 2][:, :], ALU.mult))
                        dve.wait_ge(s_mlo, mlo.now)
                        TT(tmp[2][:, :], tmp[0][:, :], tmp[1][:, :], ALU.add).then_inc(s_merge, 1)
                        dve.wait_ge(s_merge, 2 + merged.up())
                        dve.wait_ge(s_mh, mh.up())
                        p = i * 2 + (24 + j)
                        TT(acts[:, bass.ds(p, 1), 1, :], tmp[2][:, :], f32(acts[:, bass.ds(p, 1), 0, :]),
                           ALU.subtract).then_inc(s_mlo, 1)
                        mlo.up()
                norm(range(KT), whole, chunk_ready, **ln(1))
                scaled_x()
                hidden()
                norm(DOWN, half, down_ready, **ln(2))


def program(nc, x_in, stream, ada, params, consts, masks, rope, out):
    build(nc, x_in, stream, ada, params, consts, masks, rope, out)


def _tiles(w):
    k, m = w.shape
    return w.reshape(k // P, P, m // P, P).transpose(2, 1, 0, 3).reshape(m // P, P, -1)


def _rows(w):
    return w.reshape(-1, P, w.shape[1])


def _feature_cols(v):
    return np.moveaxis(v.reshape(-1, P), 1, 0)


def _stream(a):
    out = np.zeros((N_STREAM, P, TILES * P), np.float32)
    at = [0]

    def put(chunks):
        n = len(chunks)
        out[at[0]:at[0] + n] = chunks
        at[0] += n

    def put_ffn(w1, w2):
        n = w1.shape[1] // 2
        put(np.stack([_tiles(w1[:, :n]), _tiles(w1[:, n:])], 1).reshape(2 * FT, P, -1))
        put(_rows(w2))

    w = a["w_in"][0]
    W = H * P
    for c in (W, 2 * W, 4 * W + 16 + W, 4 * W + 16, 0, 3 * W, 4 * W + 16 + 3 * W):
        put(_tiles(w[:, c:c + W]))
    gates = np.zeros((D, P), np.float32)
    gates[:, 0:16] = w[:, 4 * W:4 * W + 16]
    put(_tiles(gates))
    rv = w[:, 4 * W + 16 + 2 * W:4 * W + 16 + 3 * W]
    put(rv.reshape(4, 2, P, W).transpose(0, 2, 1, 3).reshape(4, P, -1))
    put(_tiles(a["w_out"][0]))
    put_ffn(a["w_ffn_in"][0], a["w_ffn_out"][0])
    for l in range(LAYERS):
        put_ffn(a["ffn_w1_2"][l, 0], a["ffn_w2_2"][l, 0])
        b, c, v, xr, yr, ga, gb = (_tiles(a["w_in_2"][l][:, i * D:(i + 1) * D]) for i in range(7))
        put(np.stack([c, v, b], 1).reshape(3 * KT, P, -1))
        for h in range(H):
            put(xr[2 * h:2 * h + 2])
            put(yr[2 * h:2 * h + 2])
            g = a["rg_w_2"][l][:, h].reshape(2, 2, P, 2, P)
            put(g.transpose(2, 0, 3, 1, 4).reshape(1, P, -1))
        put(np.stack([_tiles(a["w_out_conv_2"][l]), ga, _tiles(a["w_out_rnn_2"][l]), gb], 1).reshape(4 * KT, P, -1))
        put(_tiles(a["w_o_2"][l]))
        put_ffn(a["ffn_w1_2"][l, 1], a["ffn_w2_2"][l, 1])
    assert at[0] == N_CHUNKS
    return out


def _params(a):
    p = np.zeros((P, C_W), np.float32)

    def put(at, v):
        p[:, at:at + v.shape[1]] = v

    put(C_COND, np.stack([_feature_cols(a["c"][0]), _feature_cols(a["c_ctx"])], 2).reshape(P, -1))
    put(C_ADAB, _feature_cols(a["ada_b"][0]))
    put(C_GMIX, _feature_cols(a["norm_mix_g"][0]))
    put(C_GFFN, _feature_cols(a["norm_ffn_g"][0]))
    put(C_CONV, a["conv_w"][0].reshape(5, 12, P).transpose(2, 1, 0).reshape(P, -1))
    put(C_GDNG, a["gdn_norm_g"][0][:, None])
    put(C_RETG, a["ret_norm_g"][0][:, None])
    put(C_FING, _feature_cols(a["final_g"]))
    for at, name in ((C_DTB, "gdn_dt_bias"), (C_ALOG, "gdn_a_log"), (C_RETL, "ret_decay_logit")):
        put(at, np.broadcast_to(a[name][0].reshape(1, 8), (P, 8)))
    j = np.arange(P, dtype=np.float32)[:, None]
    put(C_UP, j)
    put(C_DOWN, P - 1 - j)
    for l in range(LAYERS):
        for at, name in ((L_SC, "sc_w_2"), (L_RC, "rc_w_2"), (L_RCB, "rc_b_2"), (L_RGB, "rg_b_2"),
                         (L_BM, "b_merge_2"), (L_LNG, "ln_g_2"), (L_LNB, "ln_b_2"), (L_AP, "a_param_2")):
            put(C_LAY + l * L_W + at, _feature_cols(a[name][l]))
    return p


def _constants():
    i = np.arange(P)
    U = (i[:, None] <= i[None, :]).astype(np.float32)
    rot = np.zeros((P, P), np.float32)
    rot[i[:64] + 64, i[:64]] = -1.0
    rot[i[:64], i[:64] + 64] = 1.0
    diff = (i[None, :] - i[:, None]).astype(np.float32)
    row = np.broadcast_to(i[None, :] + 1.0, (P, P)).astype(np.float32)
    consts = np.concatenate([np.eye(P, dtype=np.float32), np.ones((P, P), np.float32), U, U.T, rot,
                             row, row[:, ::-1], np.maximum(diff, 0), np.maximum(-diff, 0)], 1)
    masks = np.zeros((14, P, P), np.float32)
    for lev in range(7):
        s = 1 << lev
        same = i[:, None] // (2 * s) == i[None, :] // (2 * s)
        low = same & (i[:, None] // s % 2 == 1) & (i[None, :] // s % 2 == 0)
        masks[lev], masks[7 + lev] = low, low.T
    masks = masks.transpose(1, 0, 2).reshape(P, -1)

    def angles(pos, n):
        inv = np.float32(ROPE_THETA) ** (-np.arange(n, dtype=np.float32) / np.float32(n))
        return pos[:, None].astype(np.float32) * inv[None, :].astype(np.float32)

    t = np.arange(LAT)
    zero = np.zeros(CTX)
    ang = np.concatenate([angles(np.concatenate([np.arange(CTX), np.full(LAT, CTX)]), SEQ_PAIRS),
                          angles(np.concatenate([zero, t // GRID_W]), ROW_PAIRS),
                          angles(np.concatenate([zero, t % GRID_W]), COL_PAIRS)], 1)
    cos, sin = (np.tile(f(ang).T, (2, 1)).astype(np.float32) for f in (np.cos, np.sin))
    scale = np.float32(HSCALE)
    rope = np.concatenate([cos, sin, cos[:, CTX:] * scale, sin[:, CTX:] * scale], 1)
    return np.ascontiguousarray(consts), np.ascontiguousarray(masks), np.ascontiguousarray(rope)


def host_arrays(a):
    x = np.concatenate([a["ctx"][0], a["x"][0]], 0)
    consts, masks, rope = _constants()
    return {
        "x_in": np.ascontiguousarray(x.reshape(TOK, KT, P).transpose(2, 1, 0)),
        "stream": _stream(a),
        "ada": np.ascontiguousarray(_tiles(a["ada_w"][0])),
        "params": _params(a),
        "consts": consts,
        "masks": masks,
        "rope": rope,
    }


def kernel(**inputs):
    import concourse.bacc as bacc
    from concourse.bass_utils import run_bass_kernel_spmd

    arrays = host_arrays({k: np.asarray(v) for k, v in inputs.items()})
    nc = bacc.Bacc("TRN2", target_bir_lowering=False, num_devices=1)
    args = [nc.dram_tensor(k, v.shape, mybir.dt.from_np(v.dtype), kind="ExternalInput").ap()
            for k, v in arrays.items()]
    args.append(nc.dram_tensor("out", (P, KT, LAT), F32, kind="ExternalOutput").ap())
    program(nc, *args)
    result = run_bass_kernel_spmd(nc, [arrays], core_ids=[0])
    out = np.asarray(result.results[0]["out"])
    return np.ascontiguousarray(out.transpose(2, 1, 0).reshape(1, LAT, D))
```

```python
from contextlib import ExitStack, contextmanager

import numpy as np

import concourse.bass as bass
from concourse import mybir

F32 = mybir.dt.float32
F32R = mybir.dt.float32r
U8 = mybir.dt.uint8
ALU = mybir.AluOpType
ACT = mybir.ActivationFunctionType

P = 128
D = 1024
KT = D // P
CTX, LAT = 256, 512
TOK = CTX + LAT
H = 4
NC = TOK // P
NCC = CTX // P
FF = 2816
FT = FF // P
LAYERS = 2
GRID_W, ROPE_THETA = 64, 10000.0
SEQ_PAIRS, ROW_PAIRS, COL_PAIRS = 16, 24, 24
EPS, LN_EPS = 1e-6, 1e-5
ALPHA = (2.0 * LAYERS) ** 0.25
LRU_C = 8.0
HSCALE = float(P) ** -0.5

TILES = 8
SLOTS, RAW = 4, 2
N_PROJ = 7 * H + 1 + H
PARTS = 6
N_HEAD = N_PROJ + PARTS * KT
N_B1 = N_HEAD + KT + 2 * FT + FT
N_LAYER = 2 * 3 * FT + 3 * KT + 5 * H + 4 * KT + KT
N_CHUNKS = N_B1 + LAYERS * N_LAYER
N_STREAM = N_CHUNKS + SLOTS
assert N_LAYER % SLOTS == 0
ADA_M = PARTS * KT

_o = 0


def _cols(n):
    global _o
    _o += n
    return _o - n


C_COND, C_ADAB, C_GMIX, C_GFFN = _cols(2 * KT), _cols(ADA_M), _cols(KT), _cols(KT)
C_CONV, C_GDNG, C_RETG, C_FING = _cols(12 * 5), _cols(1), _cols(1), _cols(KT)
C_DTB, C_ALOG, C_RETL = _cols(8), _cols(8), _cols(8)
C_UP, C_DOWN = _cols(1), _cols(1)
C_LAY = _o
L_SC, L_RC, L_RCB, L_RGB, L_BM, L_LNG, L_LNB, L_AP, L_C8, L_N8 = 0, 24, 56, 64, 80, 96, 120, 144, 152, 160
L_W = 168
C_W = C_LAY + LAYERS * L_W
LAYER_STEPS = 157
ITEMS = [(kind, h) for pair in (("k", "rk"), ("v", "rq"), ("q", "z"), ("rg",)) for h in range(H) for kind in pair]
ITEMS += [("ab", 0)]
BEHIND = (2, 1, 1, 1, 2, 1, 0)
N_BEHIND = [BEHIND[i % 7] if i // 7 + 2 < PARTS else 0 for i in range(len(ITEMS))]
TURNS = {i: i // 7 + 2 for i in range(len(ITEMS)) if i % 7 == 6 and i // 7 + 2 < PARTS}
assert sum(N_BEHIND) == (PARTS - 2) * KT
DOWN = (4, 5, 6, 7, 0, 1, 2, 3)
N_SP = NC * 8 + 8 + LAYERS * KT


class Tally:

    def __init__(self, start=0):
        self.base, self.k = start, 0

    def up(self, n=1):
        self.k += n
        return self.base + self.k

    @property
    def now(self):
        return self.base + self.k


@contextmanager
def rounds(engine, count, *pers):
    starts = [(t.base, t.k) for t, _ in pers]
    with engine.Fori(0, count) as i:
        for t, n in pers:
            t.base, t.k = i * n + (t.base + t.k), 0
        yield i
        for t, n in pers:
            assert t.k == n, (t.k, n)
    for (t, n), (base, k) in zip(pers, starts):
        t.base, t.k = base, k + count * n


def f32(ap):
    return ap.bitcast(F32)


def build(nc, x_in, stream, params, consts, masks, rope, out):
    ctx = ExitStack()
    with ctx:
        base = 16512
        KB = 1024

        def at(name, off, shape, dt=F32):
            return nc.alloc_sbuf_tensor_at(name, shape, dt, offset=base + off)

        h1 = at("h1", 0, [P, KT, 2, TOK], F32R)
        acts = at("acts", 0, [P, 34, 2, LAT], F32R)
        ktok = at("ktok", 0, [P, NC, H, P])
        vtok = at("vtok", 12 * KB, [P, NC, H, P])
        rktok = at("rktok", 24 * KB, [P, NC, H, P])
        oret = at("oret", 36 * KB, [P, H, LAT])
        retS = [at(f"retS{d}", (44 + 2 * d) * KB, [P, H, P]) for d in range(2)]
        xin = at("xin", 48 * KB, [P, KT, TOK])
        kT = at("kT", 48 * KB, [P, H, TOK])
        qT = at("qT", 60 * KB, [P, H, LAT])
        vfm = at("vfm", 68 * KB, [P, H, TOK])
        ogdn = at("ogdn", 68 * KB, [P, H, LAT])
        rqT = at("rqT", 80 * KB, [P, H, LAT])
        rkT = at("rkT", 88 * KB, [P, H, TOK])
        rvtok = at("rvtok", 100 * KB, [P, NC, H * P])
        zs = at("zs", 112 * KB, [P, H, LAT])
        rgs = at("rgs", 120 * KB, [P, H, LAT])
        rope_sb = at("rope_sb", 112 * KB, [P, 2 * TOK + 2 * LAT])
        lmask = at("lmask", 128 * KB, [P, 14, P], U8)
        masks_in = at("masks_in", 100 * KB, [P, 14 * P])
        cst1 = at("cst1", 130 * KB, [P, 3, P])
        Dsum = at("Dsum", 132 * KB, [P, H, P])
        tok = at("tok", 134 * KB, [P, 10, NC * 8])
        XO = 136 * KB
        X = at("X", XO, [P, KT, LAT])
        big = [at(f"big{i}", XO + i * 3104, [P, 776]) for i in range(5)]
        WO = XO + 16 * KB
        w_hi = at("w_hi", WO, [P, SLOTS, TILES, P], F32R)
        w_lo = at("w_lo", WO + 16 * KB, [P, SLOTS, TILES, P], F32R)
        raw = at("raw", WO + 32 * KB, [P, RAW, TILES, P])
        MO = WO + 40 * KB
        ident = at("ident", MO, [P, P])
        ones = at("ones", MO + 512, [P, P])
        prm = at("prm", MO + 1024, [P, C_W])
        lay = at("lay", MO + 1024 + 4 * C_W, [P, L_W])
        so = MO + 1024 + 4 * C_W + 4 * L_W
        csil = at("csil", so, [P, 2 * KT])
        mod = at("mod", so + 64, [P, ADA_M, 2])
        coef = at("coef", so + 64 + 8 * ADA_M, [P, 3, KT])
        lgc = at("lgc", so + 64 + 8 * ADA_M + 96, [P, 8])
        gch = at("gch", so + 64 + 8 * ADA_M + 128, [P, 8])
        zeta = at("zeta", so + 64 + 8 * ADA_M + 160, [P, 8])
        epsc = at("epsc", so + 64 + 8 * ADA_M + 192, [P, 8])
        cpart = at("cpart", so + 64 + 8 * ADA_M + 224, [P, 2, 2 * KT], F32R)
        to = (so + 64 + 8 * ADA_M + 224 + 16 * KT + 31) // 32 * 32
        tmp = [at(f"tmp{i}", to + i * 2 * KB, [P, LAT]) for i in range(4)]
        arow = at("arow", to, [P, KT * P])
        spw = at("spw", to + 8 * KB, [P, 6, N_SP])
        assert base + to + 8 * KB + 24 * N_SP <= 229344
        rt = [at(f"rt{i}", XO + i * 2 * KB, [P, H, P]) for i in range(8)]
        gt = [[rt[4 * d + i] for i in range(4)]
              + [at(f"gt{d}{i}", (80 + 16 * d + 2 * i) * KB, [P, H, P]) for i in range(8)] for d in range(2)]
        hq = at("hq", 80 * KB, [P, H, LAT])
        hn = at("hn", 88 * KB, [P, H, LAT])
        hm = at("hm", 96 * KB, [P, H, LAT])
        MT = 96 * KB
        mt = [at(f"mt{i}", MT + i * 2080, [P, LAT + 3]) for i in range(15)]

        sg = at("sg", 128 * KB, [P, 2, LAT])

        ps = [ctx.enter_context(nc.psum_tensor(f"ps{i}", [P, 512], F32)) for i in range(8)]
        pair = lambda j: (acts[:, j, 0, :], acts[:, j, 1, :])

        def sem(name):
            return ctx.enter_context(nc.semaphore(name))


        s_Gc = sem("Gc")
        s_abt = sem("abt")
        s_acc = sem("acc")
        s_act = sem("act")
        s_arow = sem("arow")
        s_acol = sem("acol")
        s_part = sem("part")
        s_ath = sem("ath")
        s_aux_done = sem("aux_done")
        s_squares = sem("squares")
        s_row = sem("row")
        s_aux_read = sem("aux_read")
        s_beta = sem("beta")
        s_cdone = sem("cdone")
        s_cs = sem("cs")
        s_csil = sem("csil")
        s_cst = sem("cst")
        s_cum = sem("cum")
        s_dec = sem("dec")
        s_dexp = sem("dexp")
        s_dm = [sem(f"dm{d}") for d in range(2)]
        s_done = sem("done")
        s_dve = sem("dve")
        s_e = [sem(f"e{d}") for d in range(2)]
        s_eG = sem("eG")
        s_eg = [sem(f"eg{d}") for d in range(2)]
        s_eps = sem("eps")
        s_fin = sem("fin")
        s_g = sem("g")
        s_gS = [sem(f"gS{d}") for d in range(2)]
        s_gelu = sem("gelu")
        s_go = [sem(f"go{d}") for d in range(2)]
        s_god = [sem(f"god{d}") for d in range(2)]
        s_gp = [sem(f"gp{d}") for d in range(2)]
        s_gt = [sem(f"gt{d}") for d in range(2)]
        s_gx = [sem(f"gx{d}") for d in range(2)]
        s_gxt = [sem(f"gxt{d}") for d in range(2)]
        s_gy = [sem(f"gy{d}") for d in range(2)]
        s_gyc = [sem(f"gyc{d}") for d in range(2)]
        s_h1 = sem("h1")
        s_hg = sem("hg")
        s_hh = sem("hh")
        s_hhi = sem("hhi")
        s_hi = sem("hi")
        s_hid = sem("hid")
        s_hm2 = sem("hm2")
        s_hrsq = sem("hrsq")
        s_hsum = sem("hsum")
        s_hm = sem("hm")
        s_hlog = sem("hlog")
        s_hsq = sem("hsq")
        s_hss = sem("hss")
        s_hstd = sem("hstd")
        s_hval = sem("hval")
        s_hvar = sem("hvar")
        s_kg = [sem(f"kg{d}") for d in range(2)]
        s_kv = [sem(f"kv{d}") for d in range(2)]
        s_lg = sem("lg")
        s_lo = sem("lo")
        s_m2 = sem("m2")
        s_merge = sem("merge")
        s_masks = sem("masks")
        s_mg = sem("mg")
        s_mh = sem("mh")
        s_mlo = sem("mlo")
        s_msq = sem("msq")
        s_na = [sem(f"na{d}") for d in range(2)]
        s_nwT = [sem(f"nwT{d}") for d in range(2)]
        s_out = sem("out")
        s_pre = sem("pre")
        s_pread = sem("pread")
        s_prm = sem("prm")
        s_prod = sem("prod")
        s_qadd = sem("qadd")
        s_rS = [sem(f"rS{d}") for d in range(2)]
        s_raw = [sem(f"raw{i}") for i in range(RAW)]
        s_res = sem("res")
        s_rkv = [sem(f"rkv{d}") for d in range(2)]
        s_rkz = [sem(f"rkz{d}") for d in range(2)]
        s_rm = sem("rm")
        s_rm4 = sem("rm4")
        s_ro = [sem(f"ro{d}") for d in range(2)]
        s_rod = [sem(f"rod{d}") for d in range(2)]
        s_root = sem("root")
        s_rope = sem("rope")
        s_rows = [sem(f"rows{d}") for d in range(2)]
        s_rqk = sem("rqk")
        s_rqx = [sem(f"rqx{d}") for d in range(2)]
        s_rv = sem("rv")
        s_sig = sem("sig")
        s_sil = sem("sil")
        s_silu = sem("silu")
        s_spa = sem("spa")
        s_sq = sem("sq")
        s_sqadd = sem("sqadd")
        s_sqx = sem("sqx")
        s_ss = sem("ss")
        s_stat = sem("stat")
        s_sum = sem("sum")
        s_nm = sem("nm")
        s_std = sem("std")
        s_std0 = sem("std0")
        s_turn = sem("turn")
        s_turned = sem("turned")
        s_var = sem("var")
        s_vn = [sem(f"vn{d}") for d in range(2)]
        s_vp = [sem(f"vp{d}") for d in range(2)]
        s_wT = [sem(f"wT{d}") for d in range(2)]
        s_xc = sem("xc")
        s_xcf = sem("xcf")
        s_xch = sem("xch")
        s_xhi = sem("xhi")
        s_xin = sem("xin")
        s_xlo = sem("xlo")
        s_xn = sem("xn")
        s_xr = sem("xr")
        s_xres = sem("xres")
        s_y = sem("y")
        s_ya = sem("ya")
        s_yaf = sem("yaf")
        s_yah = sem("yah")
        s_yb = sem("yb")
        s_ybh = sem("ybh")
        s_yf = sem("yf")
        s_yh = sem("yh")

        items = ITEMS
        WHOLE, CONV, NORMED, ROPED = ("k", "v", "rk", "ab"), ("k", "v", "q"), ("k", "q"), ("rk", "rq")
        count = lambda kinds: [sum(k in kinds for k, _ in items[:i + 1]) for i in range(len(items))]
        n_aux, n_c, n_conv = count(NORMED + ROPED), count(CONV + ROPED), count(CONV)
        n_norm, n_rope = count(NORMED), count(ROPED)
        n_last_rope = max(i for i, (k, _) in enumerate(items) if k in ROPED)
        pbuf = lambda j: big[j % 2]
        cbuf = lambda j: big[2 + j % 2]
        turned = [(kind, c) for kind in ("k", "v", "rk") for c in range(NC)]
        order = (list(range(NC)), list(range(NCC))[::-1] + list(range(NCC, NC))[::-1])
        mats = tmp[3][:, :].rearrange("p (a n) -> p a n", a=4)

        gates = ((tmp[0][:, :], tmp[1][:, :]), (sg[:, 0, :], sg[:, 1, :]))

        block = ctx.enter_context(nc.Block())

        @block.sync
        def _(sp):
            sp.dma_start(prm[:, :], params).then_inc(s_prm, 16)

            def load_chunk(n, slot):
                sp.dma_start(raw[:, slot, :, :].rearrange("p k n -> p (k n)"),
                             stream[bass.ds(n, 1), :, :].rearrange("a p n -> (a p) n")).then_inc(s_raw[slot], 16)

            load_chunk(0, 0)
            load_chunk(1, 1)
            sp.dma_start(ident[:, :], consts[:, 0:P]).then_inc(s_cst, 16)
            sp.dma_start(ones[:, :], consts[:, P:2 * P]).then_inc(s_cst, 16)
            sp.dma_start(cst1[:, :, :].rearrange("p a n -> p (a n)"), consts[:, 2 * P:5 * P]).then_inc(s_cst, 16)
            split = Tally()
            body, early = (N_STREAM - RAW) // RAW, 2 * KT // RAW
            for first, count in ((0, early), (early, body - early)):
                if first:
                    sp.dma_start(rope_sb[:, :], rope).then_inc(s_rope, 16)
                    sp.dma_start(masks_in[:, :], masks).then_inc(s_masks, 16)
                    sp.dma_start(tmp[3][:, :], consts[:, 5 * P:9 * P]).then_inc(s_rm4, 16)
                with rounds(sp, count, (split, RAW)) as i:
                    for s in range(RAW):
                        sp.wait_ge(s_lo, split.up())
                        load_chunk((i + first) * RAW + RAW + s, s)
            for n in range(RAW + body * RAW, N_STREAM):
                sp.wait_ge(s_lo, split.up())
                load_chunk(n, n % RAW)

        @block.gpsimd
        def _(pool):
            hi = Tally()

            def low_part(slot):
                pool.wait_ge(s_hi, hi.up())
                nc.gpsimd.tensor_tensor(w_lo[:, slot, :, :], raw[:, slot % RAW, :, :],
                                        f32(w_hi[:, slot, :, :]), ALU.subtract).then_inc(s_lo, 1)

            with rounds(pool, N_STREAM // SLOTS, (hi, SLOTS)):
                for slot in range(SLOTS):
                    low_part(slot)
            for slot in range(N_STREAM % SLOTS):
                low_part(slot)

        @block.tensor
        def _(pe):
            mm = nc.tensor.matmul
            slot = [0]
            n_hi, n_lo = Tally(), Tally()

            def chunk(outs, ready=None):
                s = slot[0] % SLOTS
                slot[0] += 1
                pe.wait_ge(s_hi, n_hi.up())
                for k in range(TILES):
                    if ready:
                        ready(k)
                    for o, xh, xl, start, stop in outs(k):
                        mm(o, w_hi[:, s, k, :], xh, start=start, stop=False, skip_group_check=True)
                        mm(o, w_hi[:, s, k, :], xl, start=False, stop=False, skip_group_check=True)
                pe.wait_ge(s_lo, n_lo.up())
                for k in range(TILES):
                    for o, xh, xl, start, stop in outs(k):
                        last = mm(o, w_lo[:, s, k, :], xh, start=False, stop=stop, skip_group_check=True)
                last.then_inc(s_done, 1)

            def part_chunk(k, banks):
                sl = slot[0] % SLOTS
                slot[0] += 1
                pe.wait_ge(s_hi, n_hi.up())
                pe.wait_ge(s_lo, n_lo.up())
                ch, cl = (cpart[:, a, 2 * k:2 * k + 2] for a in range(2))
                for half in range(2):
                    o = ps[banks[half]][0:2, :]
                    wh, wl = (w[:, sl, 4 * half:4 * half + 4, :].rearrange("p a n -> p (a n)") for w in (w_hi, w_lo))
                    mm(o, ch, wh, start=(k == 0), stop=False, skip_group_check=True)
                    mm(o, cl, wh, start=False, stop=False, skip_group_check=True)
                    last = mm(o, ch, wl, start=False, stop=(k == KT - 1), skip_group_check=True)
                last.then_inc(s_done, 1)

            def turn_part(part, bank):
                pe.wait_ge(s_arow, part + 1)
                for m in range(KT):
                    last = nc.tensor.transpose(ps[bank][:, 2 * m:2 * m + 2], arow[0:2, m * P:(m + 1) * P],
                                               ident[0:2, 0:2])
                last.then_inc(s_acol, 1)

            pe.wait_ge(s_csil, 3)
            for k in range(KT):
                part_chunk(k, (0, 1))
            for k in range(2):
                part_chunk(k, (2, 3))
            pe.wait_ge(s_cst, 48)
            pe.wait_ge(s_acc, 1)
            mm(ps[4][:, 0:CTX], ones[:, :], big[2][:, 0:CTX], start=True, stop=True)
            mm(ps[5][:, :], ones[:, :], big[2][:, CTX:TOK], start=True, stop=True).then_inc(s_ss, 1)
            turn_part(0, 6)
            for k in range(2, KT):
                part_chunk(k, (2, 3))
            turn_part(1, 7)

            part_k = 2 * KT
            for i, (kind, h) in enumerate(items + [(None, 0)] * 2):
                if kind:
                    if i >= 2:
                        pe.wait_ge(s_pread, i - 1)
                    L, C = ps[2 * (i % 2)], ps[2 * (i % 2) + 1]
                    s = slice(CTX, TOK)

                    def outs(k, whole=kind in WHOLE):
                        r = [(L[:, :], h1[:, k, 0, CTX:TOK], h1[:, k, 1, CTX:TOK], k == 0, k == KT - 1)]
                        if whole:
                            r.append((C[:, 0:CTX], h1[:, k, 0, 0:CTX], h1[:, k, 1, 0:CTX], k == 0, k == KT - 1))
                        return r

                    chunk(outs, ready=(lambda k: pe.wait_ge(s_h1, k + 1)) if i == 0 else None)
                    for _ in range(N_BEHIND[i]):
                        if part_k % KT == 0:
                            pe.wait_ge(s_part, part_k // KT)
                        part_chunk(part_k % KT, (6, 7))
                        part_k += 1
                    if i in TURNS:
                        turn_part(TURNS[i], 6)
                if i >= 2:
                    kind, h = items[i - 2]
                    j = i - 2
                    if kind in NORMED + ROPED:
                        if kind in NORMED:
                            pe.wait_ge(s_squares, n_norm[j])
                        else:
                            pe.wait_ge(s_row, n_rope[j])
                        if n_aux[j] >= 2:
                            pe.wait_ge(s_aux_read, n_aux[j] - 1)
                        w = ones[:, :] if kind in NORMED else cst1[:, 2, :]
                        src = cbuf(j) if kind in NORMED else pbuf(j)
                        if kind == "k":
                            mm(ps[5][:, 0:CTX], w, src[:, 0:CTX], start=True, stop=True)
                            last = mm(ps[4][:, :], w, src[:, CTX + 4:TOK + 4], start=True, stop=True)
                        elif kind == "rk":
                            mm(ps[5][:, 0:CTX], w, src[:, 0:CTX], start=True, stop=True)
                            last = mm(ps[4][:, :], w, src[:, CTX:TOK], start=True, stop=True)
                        else:
                            last = mm(ps[4][:, :], w, src[:, 0:LAT], start=True, stop=True)
                        last.then_inc(s_aux_done, 1)
                    if kind == "ab":
                        pe.wait_ge(s_pread, j + 1)
                        pe.wait_ge(s_part, PARTS)
                        for c in range(NC):
                            last = nc.tensor.transpose(ps[6][:, 16 * c:16 * c + 16],
                                                       pbuf(j)[0:16, c * P:(c + 1) * P], ident[0:16, 0:16])
                        last.then_inc(s_abt, 1)

            pe.wait_ge(s_pread, len(items))
            pe.wait_ge(s_aux_read, n_aux[len(items) - 1])
            for q in range(H):
                sl = slot[0] % SLOTS
                slot[0] += 1
                pe.wait_ge(s_hi, n_hi.up())
                pe.wait_ge(s_lo, n_lo.up())
                for t in range(NC):
                    for kk in range(2):
                        k = 2 * q + kk
                        wh = w_hi[:, sl, 4 * kk:4 * kk + 4, :].rearrange("p a n -> p (a n)")
                        wl = w_lo[:, sl, 4 * kk:4 * kk + 4, :].rearrange("p a n -> p (a n)")
                        xh, xl = (h1[:, k, a, t * P:(t + 1) * P] for a in range(2))
                        mm(ps[t][:, :], xh, wh, start=(k == 0), stop=False, skip_group_check=True)
                        mm(ps[t][:, :], xh, wl, start=False, stop=False, skip_group_check=True)
                        last = mm(ps[t][:, :], xl, wh, start=False, stop=(k == KT - 1), skip_group_check=True)
                last.then_inc(s_done, 1)

            pe.wait_ge(s_g, 1)
            g = tok[:, 0, :]
            mm(ps[7][:, 128:152], cst1[:, 0, :], g[:, 0:24], start=True, stop=True)
            mm(ps[7][:, 152:176], cst1[:, 1, :], g[:, 24:48], start=True, stop=True)
            mm(ps[7][:, 192:240], ones[:, :], g, start=True, stop=True).then_inc(s_cum, 1)

            pe.wait_ge(s_fin, n_aux[-1])
            pe.wait_ge(s_sil, 12)
            for j, (src, c) in enumerate(turned):
                if j >= 2:
                    pe.wait_ge(s_turned, j - 1)
                else:
                    pe.wait_ge(s_rv, 6)
                src = {"k": kT, "v": vfm, "rk": rkT}[src]
                for h in range(H):
                    last = nc.tensor.transpose(ps[j % 2][:, h * P:(h + 1) * P], src[:, h, c * P:(c + 1) * P],
                                               ident[:, :])
                last.then_inc(s_turn, 1)
            pe.wait_ge(s_turned, len(turned))

            for s in range(NC):
                for d in range(2):
                    c, b, n = order[d][s], 4 * d, 2 * s + d
                    cs = slice(c * P, (c + 1) * P)
                    lat = slice(c * P - CTX, (c + 1) * P - CTX)
                    if c >= NCC:
                        if d == 0:
                            if s > NCC:
                                pe.wait_ge(s_rm, s - NCC)
                            for h in range(H):
                                last = mm(ps[b][:, h * P:(h + 1) * P], rkT[:, h, cs], rqT[:, h, lat],
                                          start=True, stop=True)
                            last.then_inc(s_rqk, 1)
                            pe.wait_ge(s_rm, s - NCC + 1)
                        pe.wait_ge(s_rqx[d], s - NCC + 1)
                        if s > NCC:
                            pe.wait_ge(s_ro[d], s - NCC)
                        pe.wait_ge(s_rS[d], s)
                        for h in range(H):
                            o = ps[b + 1][:, h * P:(h + 1) * P]
                            last = mm(o, retS[d][:, h, :], rt[3 + d][:, h, :], start=True, stop=(d == 1))
                            if d == 0:
                                last = mm(o, rvtok[:, c, h * P:(h + 1) * P], rt[2][:, h, :], start=False, stop=True)
                        last.then_inc(s_rod[d], 1)
                    if s < NC - 1:
                        pe.wait_ge(s_rkz[d], s + 1)
                        if s:
                            pe.wait_ge(s_rS[d], s)
                        for h in range(H):
                            last = mm(ps[b + 2][:, h * P:(h + 1) * P], rt[d][:, h, :],
                                      rvtok[:, c, h * P:(h + 1) * P], start=True, stop=True)
                        last.then_inc(s_rkv[d], 1)
            pe.wait_ge(s_ro[1], 4)
            pe.wait_ge(s_ro[0], 4)
            pe.wait_ge(s_rS[0], NC - 1)
            pe.wait_ge(s_rS[1], NC - 1)

            for s in range(NC):
                both = [(d, order[d][s], 4 * d, gt[d]) for d in range(2)]
                for d, c, b, t in both:
                    cs = slice(c * P, (c + 1) * P)
                    U = cst1[:, d, :]
                    if s:
                        pe.wait_ge(s_nwT[d], s)
                        pe.wait_ge(s_gx[d], 7 * s)
                    if s > NCC:
                        pe.wait_ge(s_go[d], s - NCC)
                    for h in range(H):
                        col = 24 * d + 4 * c + h
                        mm(ps[b][:, h * P:(h + 1) * P], tok[:, 0, col:col + 1].to_broadcast([P, P]), U,
                           start=True, stop=True)
                    for h in range(H):
                        last = mm(ps[b + 1][:, h * P:(h + 1) * P], kT[:, h, cs], kT[:, h, cs],
                                  start=True, stop=True)
                    if c >= NCC:
                        for h in range(H):
                            last = mm(ps[b + 2][:, h * P:(h + 1) * P], kT[:, h, cs],
                                      qT[:, h, c * P - CTX:(c + 1) * P - CTX], start=True, stop=True)
                    last.then_inc(s_rows[d], 1)
                for lev in range(7):
                    for d, c, b, t in both:
                        E, NA, Xi, XT, Y = t[0:5]
                        if lev == 0:
                            pe.wait_ge(s_na[d], s + 1)
                            for h in range(H):
                                last = nc.tensor.transpose(ps[b + 1][:, h * P:(h + 1) * P], NA[:, h, :], ident[:, :])
                            last.then_inc(s_gp[d], 1)
                        else:
                            pe.wait_ge(s_gx[d], 7 * s + lev)
                            for h in range(H):
                                last = mm(ps[b][:, h * P:(h + 1) * P], NA[:, h, :], Xi[:, h, :],
                                          start=True, stop=True)
                            last.then_inc(s_gy[d], 1)
                    for d, c, b, t in both:
                        E, NA, Xi, XT, Y = t[0:5]
                        if 0 < lev:
                            pe.wait_ge(s_gyc[d], 6 * s + lev)
                            if lev > 1:
                                pe.wait_ge(s_gxt[d], 5 * s + lev - 1)
                            for h in range(H):
                                if lev < 6:
                                    last = mm(ps[b + 1][:, h * P:(h + 1) * P], XT[:, h, :], Y[:, h, :],
                                              start=True, stop=True)
                                else:
                                    last = mm(ps[b + 1][:, h * P:(h + 1) * P], Y[:, h, :], XT[:, h, :],
                                              start=True, stop=True)
                            last.then_inc(s_gp[d], 1)
                    for d, c, b, t in both:
                        E, NA, Xi, XT, Y = t[0:5]
                        if 0 < lev < 6:
                            pe.wait_ge(s_gx[d], 7 * s + lev + 1)
                            for h in range(H):
                                last = nc.tensor.transpose(ps[b + 2][:, h * P:(h + 1) * P], Xi[:, h, :], ident[:, :])
                            last.then_inc(s_gt[d], 1)
                for d, c, b, t in both:
                    XT, kG = t[3], t[8]
                    pe.wait_ge(s_gx[d], 7 * s + 7)
                    pe.wait_ge(s_kg[d], s + 1)
                    for h in range(H):
                        last = mm(ps[b][:, h * P:(h + 1) * P], kG[:, h, :], XT[:, h, :], start=True, stop=True)
                    last.then_inc(s_wT[d], 1)
                for d, c, b, t in both:
                    XT, nwT, S = t[3], t[7], t[11]
                    if s:
                        pe.wait_ge(s_nwT[d], s + 1)
                        pe.wait_ge(s_gS[d], s)
                    for h in range(H):
                        o = ps[b + 3][:, h * P:(h + 1) * P]
                        last = mm(o, XT[:, h, :], vtok[:, c, h, :], start=True, stop=(s == 0))
                        if s:
                            last = mm(o, nwT[:, h, :], S[:, h, :], start=False, stop=True)
                    last.then_inc(s_vp[d], 1)
                for d, c, b, t in both:
                    QK, qd, kd, vn, S = t[5], t[6], t[9], t[10], t[11]
                    pe.wait_ge(s_vn[d], s + 1)
                    if c >= NCC:
                        for h in range(H):
                            o = ps[b + 2][:, h * P:(h + 1) * P]
                            mm(o, S[:, h, :], qd[:, h, :], start=True, stop=False)
                            last = mm(o, vn[:, h, :], QK[:, h, :], start=False, stop=True)
                        last.then_inc(s_god[d], 1)
                    if s < NC - 1:
                        for h in range(H):
                            last = mm(ps[b + 3][:, h * P:(h + 1) * P], kd[:, h, :], vn[:, h, :],
                                      start=True, stop=True)
                        last.then_inc(s_kv[d], 1)

            pe.wait_ge(s_go[0], 4)
            pe.wait_ge(s_go[1], 4)
            for h in range(H):
                mm(ps[4 + h][:, :], ones[:, :], oret[:, h, :], start=True, stop=True).then_inc(s_hsum, 1)
            for h in range(H):
                pe.wait_ge(s_hrsq, h + 1)
                mm(ps[h][:, :], ones[:, :], tmp[h][:, :], start=True, stop=True).then_inc(s_hss, 1)
            for h in range(H):
                pe.wait_ge(s_hvar, h + 1)
                pe.wait_ge(s_hsq, h + 1)
                mm(ps[h][:, :], ones[:, :], hq[:, h, :], start=True, stop=True).then_inc(s_hss, 1)

            n_pre, n_q, n_x, n_prod, n_hid = Tally(), Tally(), Tally(), Tally(), Tally(1)

            def x_outs(bank, wait=None):
                return lambda k: [(bank[:, :], *pair(k), k == 0, k == KT - 1)]

            def opening(banks, ready, first=0):
                slots = [(slot[0] + j) % SLOTS for j in range(SLOTS)]
                slot[0] += SLOTS
                pe.wait_ge(s_hi, n_hi.up(SLOTS))
                pe.wait_ge(s_lo, n_lo.up(SLOTS))

                def tile(j, k):
                    xh, xl = pair(first + k)
                    o, s = ps[banks[j]][:, :], slots[j]
                    mm(o, w_hi[:, s, k, :], xh, start=(k == 0), stop=False, skip_group_check=True)
                    mm(o, w_hi[:, s, k, :], xl, start=False, stop=False, skip_group_check=True)
                    return mm(o, w_lo[:, s, k, :], xh, start=False, stop=(k == KT - 1), skip_group_check=True)

                for k in range(KT - 2):
                    ready()
                    for j in range(SLOTS):
                        tile(j, k)
                for j in range(SLOTS):
                    for k in (KT - 2, KT - 1):
                        if j == 0:
                            ready()
                        last = tile(j, k)
                    last.then_inc(s_done, 1)

            def x_ready():
                pe.wait_ge(s_xlo, n_x.up())

            def normed(seq, product, mean=True):
                for i in range(KT + 2):
                    if i < KT:
                        product(i, seq[i])
                    if i >= 2:
                        pe.wait_ge(s_pre, n_pre.up())
                        if mean:
                            last = mm(ps[seq[0]][:, :], ones[:, :], X[:, seq[i - 2], :], start=(i == 2),
                                      stop=(i == KT + 1), skip_group_check=True)
                if mean:
                    last.then_inc(s_sum, 1)
                pe.wait_ge(s_qadd, n_q.up(KT))
                mm(ps[seq[1]][:, :], ones[:, :], tmp[2][:, :], start=True, stop=True).then_inc(s_stat, 1)

            def ffn(mean=True):
                pe.wait_ge(s_prod, n_prod.up(2))
                opening((0, 1, 2, 3), x_ready)
                with rounds(pe, FT // 2 - 1, (n_hi, 4), (n_lo, 4), (n_prod, 2)):
                    for j in range(2):
                        pe.wait_ge(s_prod, n_prod.up())
                        chunk(x_outs(ps[2 * j]))
                        chunk(x_outs(ps[2 * j + 1]))

                def down(k, seq, a):
                    s = slot[0] % SLOTS
                    slot[0] += 1
                    hh, hl = acts[:, 8 + k, 0, :] if isinstance(k, int) else acts[:, bass.ds(k + 8, 1), 0, :], \
                        acts[:, 8 + k, 1, :] if isinstance(k, int) else acts[:, bass.ds(k + 8, 1), 1, :]
                    pe.wait_ge(s_hid, n_hid.up())
                    pe.wait_ge(s_hi, n_hi.up())
                    for i, m in enumerate(seq):
                        if a and i == 4:
                            pe.wait_ge(s_prod, n_prod.now + 2)
                        mm(ps[m][:, :], w_hi[:, s, m, :], hh, start=a, stop=False, skip_group_check=True)
                        mm(ps[m][:, :], w_hi[:, s, m, :], hl, start=False, stop=False, skip_group_check=True)
                    pe.wait_ge(s_lo, n_lo.up())
                    for m in seq:
                        last = mm(ps[m][:, :], w_lo[:, s, m, :], hh, start=False, stop=False, skip_group_check=True)
                    last.then_inc(s_done, 1)

                seq = DOWN
                down(0, seq, True)
                down(1, seq, False)
                with rounds(pe, 4, (n_hi, 4), (n_lo, 4), (n_hid, 4)) as i:
                    for j in range(4):
                        down(i * 4 + (2 + j), seq, False)
                for k in range(18, FT - 2):
                    down(k, seq, False)
                slots = [(slot[0] + j) % SLOTS for j in range(2)]
                slot[0] += 2
                pe.wait_ge(s_hid, n_hid.up(2))
                pe.wait_ge(s_hi, n_hi.up(2))
                pe.wait_ge(s_lo, n_lo.up(2))

                def product(i, m):
                    for j, s in enumerate(slots):
                        hh, hl = pair(8 + FT - 2 + j)
                        mm(ps[m][:, :], w_hi[:, s, m, :], hh, start=False, stop=False, skip_group_check=True)
                        mm(ps[m][:, :], w_hi[:, s, m, :], hl, start=False, stop=False, skip_group_check=True)
                        last = mm(ps[m][:, :], w_lo[:, s, m, :], hh, start=False, stop=(j == 1),
                                  skip_group_check=True)
                    if i < KT - 1:
                        last.then_inc(s_out, 1)
                    else:
                        last.then_inc(s_done, 2)

                normed(seq, product, mean)

            n_y = Tally()

            def product(i, m):
                if i == 0:
                    opening(DOWN[:4], lambda: pe.wait_ge(s_y, n_y.up()))
                elif i >= SLOTS:
                    chunk(x_outs(ps[m]))

            normed(DOWN, product, mean=False)
            ffn(mean=False)

            n_mix = {q: Tally() for q in ("xc", "yb", "merge", "half", "gate")}
            n_mix["ya"], n_mix["mlo"] = Tally(1), Tally(1)
            tallies = [(n_hi, N_LAYER), (n_lo, N_LAYER), (n_pre, 24), (n_q, 24), (n_x, 24), (n_prod, 44),
                       (n_hid, 44), (n_mix["ya"], KT), (n_mix["xc"], KT), (n_mix["yb"], KT),
                       (n_mix["merge"], KT), (n_mix["half"], H), (n_mix["gate"], KT), (n_mix["mlo"], KT)]
            with rounds(pe, LAYERS, *tallies):
                ffn()
                opening((0, 1, 2, 3), x_ready)
                for f in range(1, KT):
                    b = 3 * (f % 2)
                    if f >= 2:
                        pe.wait_ge(s_ya, n_mix["ya"].up())
                    for j in range(f == 1, 3):
                        chunk(x_outs(ps[b + j]))
                n_mix["ya"].up(2)
                for h in range(H):
                    if h == 0:
                        pe.wait_ge(s_ya, n_mix["ya"].now)
                    if h:
                        pe.wait_ge(s_gelu, n_mix["gate"].up(2))
                    for j in range(4):
                        chunk(x_outs(ps[j]))
                    if h:
                        pe.wait_ge(s_sig, n_mix["half"].up())
                    pe.wait_ge(s_xc, n_mix["xc"].up(2))

                    def gate_outs(t):
                        g, m, k = t // 4, (t // 2) % 2, t % 2
                        return [(ps[4 + 2 * g + m][:, :], *pair(32 + k), k == 0, k == 1)]

                    chunk(gate_outs)
                n_mix["gate"].up(2)
                n_mix["half"].up(1)
                banks_read = (n_mix["gate"].now, n_mix["half"].now)
                ready = n_mix["yb"].up(KT)
                with rounds(pe, 4, (n_hi, 8), (n_lo, 8), (n_mix["merge"], 2)):
                    for j in range(2):
                        if j == 0:
                            pe.wait_ge(s_ya, n_mix["ya"].now)
                            pe.wait_ge(s_gelu, banks_read[0])
                            pe.wait_ge(s_sig, banks_read[1])
                        pe.wait_ge(s_merge, n_mix["merge"].up())
                        b = 4 * j
                        chunk(lambda k: [(ps[b][:, :], *pair(8 + k), k == 0, k == KT - 1)])
                        chunk(x_outs(ps[b + 1]))
                        chunk(x_outs(ps[b + 3]))
                    for b in (0, 4):
                        if b == 0:
                            pe.wait_ge(s_yb, ready)
                        chunk(lambda k: [(ps[b + 2][:, :], *pair(16 + k), k == 0, k == KT - 1)])
                pe.wait_ge(s_merge, n_mix["merge"].now + 1)

                def product(i, m):
                    if i == 0:
                        opening((0, 1, 2, 3), lambda: pe.wait_ge(s_mlo, n_mix["mlo"].up()), first=24)
                    elif i >= SLOTS:
                        chunk(lambda k: [(ps[m][:, :], *pair(24 + k), k == 0, k == KT - 1)])

                normed(range(KT), product)
                ffn()

        @block.scalar
        def _(act):
            A = nc.scalar.activation
            step = Tally()

            def link(ins):
                ins.then_inc(s_act, 1)
                act.wait_ge(s_act, step.up())

            slot = [0]
            loaded, used = [Tally(), Tally()], Tally()

            def hi_part():
                s = slot[0] % SLOTS
                slot[0] += 1
                act.wait_ge(s_raw[s % RAW], loaded[s % RAW].up(16))
                A(w_hi[:, s, :, :], raw[:, s % RAW, :, :], ACT.Copy).then_inc(s_hi, 1)

            def done():
                act.wait_ge(s_done, used.up())
                hi_part()

            chunks = lambda n: ((used, n), (loaded[0], 8 * n), (loaded[1], 8 * n))

            act.wait_ge(s_prm, 16)
            A(csil[:, :], prm[:, C_COND:C_COND + 2 * KT], ACT.Silu).then_inc(s_csil, 1)
            act.wait_ge(s_csil, 1)
            A(cpart[:, 0, :], csil[:, :], ACT.Copy).then_inc(s_csil, 1)
            for n in range(SLOTS):
                hi_part()
                for k in (2 * n, 2 * n + 1):
                    act.dma_start(xin[:, k, :], x_in[:, k, :]).then_inc(s_xin, 16)
            act.wait_ge(s_xin, 16 * KT)
            for k in range(KT):
                if k >= 2:
                    act.wait_ge(s_sqadd, k - 1)
                A(big[k % 2][:, 0:TOK], xin[:, k, :], ACT.Square).then_inc(s_sq, 1)
                done()
            act.wait_ge(s_ss, 1)
            act.wait_ge(s_eps, 1)
            A(big[3][:, 0:CTX], ps[4][:, 0:CTX], ACT.Sqrt, scale=1.0 / D, bias=epsc[:, 0:1])
            A(big[3][:, CTX:TOK], ps[5][:, :], ACT.Sqrt, scale=1.0 / D, bias=epsc[:, 0:1]).then_inc(s_std0, 1)
            for _ in range(KT):
                done()
            for k in range(KT):
                act.wait_ge(s_hval, k + 1)
                A(h1[:, k, 0, :], big[k % 2][:, 0:TOK], ACT.Copy).then_inc(s_hhi, 1)

            n = len(items)
            for i in range(n + 2):
                if i < n:
                    kind, h = items[i]
                    L, C = ps[2 * (i % 2)], ps[2 * (i % 2) + 1]
                    done()
                    if kind in CONV + ROPED + ("ab",):
                        b = pbuf(i)
                        if i >= 2:
                            act.wait_ge(s_cdone, n_c[i - 2])
                        if i >= 2 and items[i - 2][0] in ROPED:
                            act.wait_ge(s_aux_done, n_aux[i - 2])
                    if kind in CONV:
                        off, o2 = (2, CTX + 6) if kind != "q" else (2, 2)
                        if i == 0 or (kind == "q" and h == 0):
                            z = epsc[:, 2:4]
                            A(b[:, 0:2], z, ACT.Copy)
                            if kind != "q":
                                A(b[:, CTX + 2:CTX + 4], z, ACT.Copy)
                                A(b[:, CTX + 4:CTX + 6], z, ACT.Copy)
                                A(b[:, TOK + 6:TOK + 8], z, ACT.Copy)
                            else:
                                A(b[:, LAT + 2:LAT + 4], z, ACT.Copy)
                        if kind != "q":
                            A(b[:, 2:CTX + 2], C[:, 0:CTX], ACT.Copy)
                        A(b[:, o2:o2 + LAT], L[:, :], ACT.Copy).then_inc(s_pread, 1)
                    elif kind in ROPED:
                        if kind == "rk":
                            A(b[:, 0:CTX], C[:, 0:CTX], ACT.Copy)
                            link(A(b[:, CTX:TOK], L[:, :], ACT.Copy))
                        else:
                            link(A(b[:, 0:LAT], L[:, :], ACT.Copy))
                        act.sem_inc(s_pread, 1)
                        act.sem_inc(s_row, 1)
                    elif kind == "ab":
                        A(b[0:16, 0:CTX], C[0:16, 0:CTX], ACT.Copy)
                        A(b[0:16, CTX:TOK], L[0:16, :], ACT.Copy).then_inc(s_pread, 1)
                    else:
                        if kind == "z" and h == 0:
                            act.wait_ge(s_fin, n_aux[n_last_rope])
                        A((zs if kind == "z" else rgs)[:, h, :], L[:, :], ACT.Silu).then_inc(s_pread, 1)
                    for _ in range(N_BEHIND[i]):
                        done()
                j = i - 1
                if 0 <= j < n and items[j][0] in CONV:
                    kind, h = items[j]
                    act.wait_ge(s_cdone, n_c[j])
                    dst, c = {"k": kT, "q": qT, "v": vfm}[kind], cbuf(j)
                    segs = [(slice(0, LAT), slice(0, LAT))] if kind == "q" else \
                        [(slice(0, CTX), slice(0, CTX)), (slice(CTX, TOK), slice(CTX + 4, TOK + 4))]
                    for a, b in segs:
                        last = A(dst[:, h, a], c[:, b], ACT.Silu)
                    last.then_inc(s_sil, 1)
                    if kind in NORMED:
                        act.wait_ge(s_sil, n_conv[j])
                        for a, b in segs:
                            last = A(c[:, b], dst[:, h, a], ACT.Square)
                        last.then_inc(s_squares, 1)
                j = i - 2
                if 0 <= j < n and items[j][0] in NORMED:
                    kind, h = items[j]
                    act.wait_ge(s_aux_done, n_aux[j])
                    if n_aux[j] > 1:
                        act.wait_ge(s_fin, n_aux[j] - 1)
                    r = big[4]
                    if kind == "k":
                        A(r[:, 0:CTX], ps[5][:, 0:CTX], ACT.Sqrt, bias=epsc[:, 0:1])
                        last = A(r[:, CTX:TOK], ps[4][:, :], ACT.Sqrt, bias=epsc[:, 0:1])
                    else:
                        last = A(r[:, 0:LAT], ps[4][:, :], ACT.Sqrt, scale=float(P), bias=epsc[:, 1:2])
                    last.then_inc(s_aux_read, 1)
            for _ in range(H):
                done()
            for t in range(NC):
                A(rvtok[:, t, :], ps[t][:, :], ACT.Copy).then_inc(s_rv, 1)

            act.wait_ge(s_spa, 1)
            link(A(spw[:, 2, :], spw[:, 1, :], ACT.Exp, scale=-1.0))
            link(A(gch[:, :], prm[:, C_ALOG:C_ALOG + 8], ACT.Exp))
            act.wait_ge(s_abt, 1)
            for d in range(2):
                A(tok[:, 1, 24 * d:24 * d + 24].rearrange("p (c h) -> p c h", h=H),
                  ps[6][:, 0:96].rearrange("p (c h) -> p c h", h=16)[:, :, 8 + 4 * d:12 + 4 * d],
                  ACT.Sigmoid).then_inc(s_beta, 1)
            act.wait_ge(s_lg, 1)
            A(gch[:, :], lgc[:, :], ACT.Exp, scale=float(P))
            A(zeta[:, 0:H], lgc[:, 0:H], ACT.Exp, scale=prm[:, C_DOWN:C_DOWN + 1])
            A(zeta[:, H:2 * H], lgc[:, H:2 * H], ACT.Exp, scale=prm[:, C_UP:C_UP + 1])
            act.wait_ge(s_rm4, 16)
            for d in range(2):
                for h in range(H):
                    A(rt[5 + d][:, h, :], mats[:, d, :], ACT.Exp, scale=lgc[:, 4 * d + h:4 * d + h + 1])
            for d in range(2):
                if d:
                    act.wait_ge(s_dec, 1)
                for h in range(H):
                    last = A(rt[7][:, h, :], mats[:, 2 + d, :], ACT.Exp, scale=lgc[:, 4 * d + h:4 * d + h + 1])
                last.then_inc(s_dexp, 1)
            act.wait_ge(s_Gc, 1)
            A(tok[:, 4, :], tok[:, 3, :], ACT.Exp)
            A(tok[:, 5, :], tok[:, 7, :], ACT.Exp)
            A(tok[:, 6, :], ps[7][:, 192:240], ACT.Exp).then_inc(s_eG, 1)
            act.wait_ge(s_turned, len(turned))

            for s in range(NC - 1):
                for d in range(2):
                    c = order[d][s]
                    if s:
                        act.wait_ge(s_rkv[d], s)
                    for h in range(H):
                        last = A(rt[d][:, h, :], rktok[:, c, h, :], ACT.Copy, scale=zeta[:, 4 * d + h:4 * d + h + 1])
                    last.then_inc(s_rkz[d], 1)

            for d in range(2):
                act.wait_ge(s_ro[d], 4)
            for h in range(H):
                A(tmp[h][:, :], oret[:, h, :], ACT.Square).then_inc(s_hrsq, 1)

            for s in range(NC):
                both = [(d, order[d][s], 4 * d, gt[d]) for d in range(2)]
                for d, c, b, t in both:
                    act.wait_ge(s_dm[d], s + 1)
                    A(t[0][:, :, :], t[0][:, :, :], ACT.Exp).then_inc(s_e[d], 1)
                    if c >= NCC:
                        if s > NCC:
                            act.wait_ge(s_god[d], s - NCC)
                        A(t[6][:, :, :].rearrange("p h n -> p (h n)"), ps[b][:, :], ACT.Exp).then_inc(s_eg[d], 1)
                    if s:
                        act.wait_ge(s_kv[d], s)
                    for h in range(H):
                        col = 24 * d + 4 * c + h
                        A(t[8][:, h, :], ktok[:, c, h, :], ACT.Copy, scale=tok[:, 4, col:col + 1])
                        last = A(t[9][:, h, :], ktok[:, c, h, :], ACT.Copy, scale=tok[:, 5, col:col + 1])
                    last.then_inc(s_kg[d], 1)
                for lev in range(1, 7):
                    for d, c, b, t in both:
                        act.wait_ge(s_gy[d], 6 * s + lev)
                        A(t[4][:, :, :].rearrange("p h n -> p (h n)"), ps[b][:, :], ACT.Copy).then_inc(s_gyc[d], 1)
                    if lev < 6:
                        for d, c, b, t in both:
                            act.wait_ge(s_gt[d], 5 * s + lev)
                            A(t[3][:, :, :].rearrange("p h n -> p (h n)"), ps[b + 2][:, :],
                              ACT.Copy).then_inc(s_gxt[d], 1)
                for d, c, b, t in both:
                    act.wait_ge(s_wT[d], s + 1)
                    A(t[7][:, :, :].rearrange("p h n -> p (h n)"), ps[b][:, :], ACT.Copy,
                      scale=-1.0).then_inc(s_nwT[d], 1)
            for d in range(2):
                act.wait_ge(s_go[d], 4)

            act.dma_start(X[:, :, :], x_in[:, :, CTX:TOK]).then_inc(s_xres, 16)

            for h in range(H):
                A(hq[:, h, :], ogdn[:, h, :], ACT.Square).then_inc(s_hsq, 1)
            for h in range(H):
                act.wait_ge(s_hm, h + 1)
                A(hm[:, h, :], hn[:, h, :], ACT.Square).then_inc(s_hm2, 1)
            for j in range(2 * H):
                factor = tmp[j][:, :] if j < H else hq[:, j - H, :]
                if j < H:
                    act.wait_ge(s_hvar, j + 1)
                    A(factor, factor, ACT.Ln, bias=epsc[:, 0:1]).then_inc(s_hlog, 1)
                else:
                    act.wait_ge(s_hss, j + 1)
                    A(factor, ps[j - H][:, :], ACT.Ln, scale=1.0 / P, bias=epsc[:, 0:1]).then_inc(s_hlog, 1)
                if j % H == H - 1:
                    for i in range(j - H + 1, j + 1):
                        factor = tmp[i][:, :] if i < H else hq[:, i - H, :]
                        act.wait_ge(s_hlog, i + 1)
                        A(factor, factor, ACT.Exp, scale=-0.5).then_inc(s_hstd, 1)
            for j in range(2 * H):
                act.wait_ge(s_yf, j + 1)
                A(acts[:, j, 0, :], (oret if j < H else ogdn)[:, j % H, :], ACT.Copy).then_inc(s_yh, 1)

            pre, qadd, xn = Tally(), Tally(), Tally()
            stat, var, prod, nm = Tally(), Tally(), Tally(), Tally()

            def norm(seq, mean=True, keep=False, chunks_behind=0):
                A(epsc[:, 7:8], epsc[:, 0:1], ACT.Ln)
                for i, k in enumerate(seq):
                    if not chunks_behind:
                        done()
                    act.wait_ge(s_pre, pre.up())
                    if i >= 2:
                        act.wait_ge(s_qadd, qadd.up())
                    A(tmp[i % 2][:, :], X[:, k, :], ACT.Square).then_inc(s_sqx, 1)
                qadd.up(2)
                for _ in range(chunks_behind):
                    done()
                if mean:
                    act.wait_ge(s_nm, nm.up())
                    A(tmp[0][:, :], tmp[3][:, :], ACT.Square).then_inc(s_msq, 1)
                act.wait_ge(s_stat, stat.up())
                if mean:
                    act.wait_ge(s_var, var.up())
                    link(A(tmp[1][:, :], tmp[1][:, :], ACT.Ln, bias=epsc[:, 4:5]))
                else:
                    link(A(tmp[1][:, :], ps[seq[1]][:, :], ACT.Ln, scale=1.0 / D, bias=epsc[:, 0:1]))
                A(tmp[1][:, :], tmp[1][:, :], ACT.Exp, scale=-0.5).then_inc(s_std, 1)
                for k in range(KT):
                    act.wait_ge(s_xn, xn.up())
                    A(acts[:, k, 0, :], (tmp[2 + k % 2][:, :] if keep else X[:, k, :]),
                      ACT.Copy).then_inc(s_xhi, 1)

            def ffn():
                with rounds(act, FT // 2, *chunks(4), (prod, 2)) as i:
                    for j in range(2):
                        done()
                        A(tmp[0][:, :], ps[2 * j][:, :], ACT.Silu).then_inc(s_silu, 1)
                        done()
                        act.wait_ge(s_prod, 2 + prod.up())
                        A(acts[:, bass.ds(i * 2 + (8 + j), 1), 0, :], tmp[1][:, :], ACT.Copy).then_inc(s_hh, 1)
                with rounds(act, FT // SLOTS, *chunks(SLOTS)):
                    for _ in range(SLOTS):
                        done()

            assert FT % SLOTS == 2
            norm(DOWN, mean=False, keep=True)
            ffn()
            norm(DOWN, mean=False, chunks_behind=2)

            yaf, xcf, sig, m2, hg, yb, merge = (Tally() for _ in range(7))
            tallies = [*chunks(N_LAYER), (pre, 24), (qadd, 24), (xn, 24), (stat, 3), (var, 3), (nm, 3), (prod, 44),
                       (yaf, KT), (xcf, KT), (sig, H), (m2, H), (hg, KT), (yb, KT), (merge, KT), (step, 3)]
            with rounds(act, LAYERS, *tallies):
                ffn()
                norm(DOWN, chunks_behind=2)
                for f in range(KT):
                    b = 3 * (f % 2)
                    done()
                    A(mt[0][:, 0:LAT], ps[b][:, :], ACT.Copy).then_inc(s_cs, 1)
                    done()
                    done()
                    act.wait_ge(s_yaf, yaf.up())
                    A(acts[:, 8 + f, 0, :], mt[3][:, 0:LAT], ACT.Copy).then_inc(s_yah, 1)

                def rows(h, j):
                    done()
                    A(mt[j][:, 3:LAT + 3], ps[j][:, :], ACT.Copy).then_inc(s_xr, 1)

                def split_rows():
                    for j in range(2):
                        act.wait_ge(s_xcf, xcf.up())
                        A(acts[:, 32 + j, 0, :], mt[2 + j][:, 0:LAT], ACT.Copy).then_inc(s_xch, 1)

                def split_h(h):
                    for j in range(2):
                        act.wait_ge(s_hg, hg.up())
                        A(acts[:, 16 + 2 * h + j, 0, :], mt[4 + j][:, 0:LAT], ACT.Copy).then_inc(s_ybh, 1)

                def roots():
                    act.wait_ge(s_m2, m2.up())
                    for j in range(2):
                        A(mt[8 + j][:, 0:LAT], mt[8 + j][:, 0:LAT], ACT.Sqrt).then_inc(s_root, 1)

                for h in range(H):
                    rows(h, 0)
                    if h:
                        roots()
                    rows(h, 1)
                    split_rows()
                    for j in range(2):
                        done()
                        if h and j == 0:
                            split_h(h - 1)
                        if h:
                            act.wait_ge(s_yb, yb.up())
                        A(mt[4 + j][:, 0:LAT], ps[2 + j][:, :], ACT.Gelu_apprx_tanh).then_inc(s_gelu, 1)
                    done()
                    for j in range(2):
                        f = 2 * h + j
                        A(mt[6 + j][:, 0:LAT], ps[4 + j][:, :], ACT.Sigmoid, bias=lay[:, L_RGB + f:L_RGB + f + 1])
                        last = A(mt[8 + j][:, 0:LAT], ps[6 + j][:, :], ACT.Sigmoid,
                                 bias=lay[:, L_RGB + KT + f:L_RGB + KT + f + 1])
                    last.then_inc(s_sig, 1)
                    act.wait_ge(s_sig, sig.up())
                    for j in range(2):
                        f = 2 * h + j
                        A(mt[10 + j][:, 0:LAT], mt[8 + j][:, 0:LAT], ACT.Exp, scale=lay[:, L_C8 + f:L_C8 + f + 1])
                        A(mt[12 + j][:, 0:LAT], mt[8 + j][:, 0:LAT], ACT.Tanh,
                          scale=lay[:, L_N8 + f:L_N8 + f + 1]).then_inc(s_ath, 1)
                roots()
                split_h(H - 1)
                yb.up(2)
                with rounds(act, 4, *chunks(8), (merge, 2)) as i:
                    for j in range(2):
                        b, m = 4 * j, i * 2 + j
                        done()
                        done()
                        A(gates[j][0], ps[b + 1][:, :], ACT.Sigmoid,
                          bias=lay[:, bass.ds(m + L_BM, 1)]).then_inc(s_mg, 1)
                        done()
                        A(gates[j][1], ps[b + 3][:, :], ACT.Sigmoid,
                          bias=lay[:, bass.ds(m + (L_BM + KT), 1)]).then_inc(s_mg, 1)
                    for j in range(2):
                        done()
                        act.wait_ge(s_merge, 2 + merge.up())
                        A(acts[:, bass.ds(i * 2 + (24 + j), 1), 0, :], tmp[2 + j][:, :], ACT.Copy).then_inc(s_mh, 1)
                norm(range(KT))
                ffn()
                norm(DOWN, chunks_behind=2)
            act.dma_start(out, X[:, :, :]).then_inc(s_res, 16)
            act.wait_ge(s_res, 16)

        @block.vector
        def _(dve):
            V = nc.vector
            TT, TS, STT, CP = V.tensor_tensor, V.tensor_scalar, V.scalar_tensor_tensor, V.tensor_copy
            step = Tally()

            def link(ins):
                ins.then_inc(s_dve, 1)
                dve.wait_ge(s_dve, step.up())

            flat = lambda t: t[:, :, :].rearrange("p h n -> p (h n)")

            for j, v in ((0, EPS), (1, P * EPS), (2, 0.0), (3, 0.0), (4, LN_EPS)):
                last = V.memset(epsc[:, j:j + 1], v)
            last.then_inc(s_eps, 1)
            dve.sem_inc(s_prod, 2)
            dve.sem_inc(s_merge, 2)
            for free in (s_hid, s_ya, s_mlo):
                dve.sem_inc(free, 1)

            dve.wait_ge(s_csil, 2)
            TT(cpart[:, 1, :], csil[:, :], f32(cpart[:, 0, :]), ALU.subtract).then_inc(s_csil, 1)

            acc = big[2]
            for k in range(KT):
                dve.wait_ge(s_sq, k + 1)
                if k == 0:
                    CP(acc[:, 0:TOK], big[0][:, 0:TOK]).then_inc(s_sqadd, 1)
                else:
                    dve.wait_ge(s_sqadd, k)
                    TT(acc[:, 0:TOK], acc[:, 0:TOK], big[k % 2][:, 0:TOK], ALU.add).then_inc(s_sqadd, 1)
            dve.wait_ge(s_sqadd, KT)
            dve.sem_inc(s_acc, 1)
            def part_rows(part, chunks, banks):
                dve.wait_ge(s_done, chunks)
                for half in range(2):
                    last = CP(arow[0:2, half * 512:(half + 1) * 512], ps[banks[half]][0:2, :])
                last.then_inc(s_arow, 1)

            def part_cols(part, bank):
                dve.wait_ge(s_acol, part + 1)
                m = slice(KT * part, KT * (part + 1))
                TT(mod[:, m, :], ps[bank][:, 0:2 * KT].rearrange("p (m v) -> p m v", v=2),
                   prm[:, C_ADAB + KT * part:C_ADAB + KT * (part + 1)].unsqueeze(2).to_broadcast([P, KT, 2]),
                   ALU.add).then_inc(s_part, 1)
                dve.wait_ge(s_part, part + 1)

            dve.wait_ge(s_prm, 16)
            part_rows(0, KT, (0, 1))
            dve.wait_ge(s_std0, 1)
            link(V.reciprocal(big[3][:, 0:TOK], big[3][:, 0:TOK]))
            for k in range(KT):
                last = TT(xin[:, k, :], xin[:, k, :], big[3][:, 0:TOK], ALU.mult)
            link(last)
            part_cols(0, 6)
            part_rows(1, 2 * KT, (2, 3))
            part_cols(1, 7)
            for j in range(2):
                last = STT(coef[:, j, :], mod[:, KT:2 * KT, j], 1.0, prm[:, C_GMIX:C_GMIX + KT], ALU.add, ALU.mult)
            link(last)
            for k in range(KT + 1):
                b = big[k % 2]
                if k < KT:
                    if k > 1:
                        dve.wait_ge(s_h1, k - 1)
                    TS(b[:, 0:CTX], xin[:, k, 0:CTX], coef[:, 1, k:k + 1], mod[:, k, 1:2], ALU.mult, ALU.add)
                    TS(b[:, CTX:TOK], xin[:, k, CTX:TOK], coef[:, 0, k:k + 1], mod[:, k, 0:1], ALU.mult,
                       ALU.add).then_inc(s_hval, 1)
                if k:
                    dve.wait_ge(s_hval, k)
                    dve.wait_ge(s_hhi, k)
                    TT(h1[:, k - 1, 1, :], big[(k - 1) % 2][:, 0:TOK], f32(h1[:, k - 1, 0, :]),
                       ALU.subtract).then_inc(s_h1, 1)

            n, done_chunks = len(items), 2 * KT
            for i in range(n + 2):
                if i < n:
                    done_chunks += 1
                    if i in TURNS:
                        part_rows(TURNS[i], done_chunks - 1, (6, 7))
                    done_chunks += N_BEHIND[i]
                if i < n and items[i][0] in CONV + ROPED:
                    kind, h = items[i]
                    dve.wait_ge(s_pread, i + 1)
                    b, c = pbuf(i), cbuf(i)
                    if i >= 2 and items[i - 2][0] in NORMED + ROPED:
                        dve.wait_ge(s_aux_done, n_aux[i - 2])
                    if kind in CONV:
                        if i >= 2 and items[i - 2][0] in CONV:
                            dve.wait_ge(s_sil, n_conv[i - 2])
                        ct = {"q": 0, "k": 1, "v": 2}[kind] * H + h
                        w = [prm[:, C_CONV + 5 * ct + a:C_CONV + 5 * ct + a + 1] for a in range(5)]
                        m = LAT if kind == "q" else TOK + 4
                        link(TS(c[:, 0:m], b[:, 0:m], w[0], None, ALU.mult))
                        for a in range(1, 5):
                            last = STT(c[:, 0:m], b[:, a:m + a], w[a], c[:, 0:m], ALU.mult, ALU.add)
                            if a < 4:
                                link(last)
                        last.then_inc(s_cdone, 1)
                    else:
                        if (kind, h) == ("rk", 0):
                            dve.wait_ge(s_rope, 16)
                        dst, o, m = (rkT, 0, TOK) if kind == "rk" else (rqT, 2 * TOK, LAT)
                        TT(dst[:, h, :], b[:, 0:m], rope_sb[:, o:o + m], ALU.mult).then_inc(s_cdone, 1)
                if i == 3:
                    dve.wait_ge(s_masks, 16)
                    CP(lmask[:, :, :].rearrange("p a n -> p (a n)"), masks_in[:, :])
                if i in TURNS:
                    part_cols(TURNS[i], 6)
                    if TURNS[i] == 4:
                        STT(coef[:, 2, :], mod[:, 4 * KT:5 * KT, 0], 1.0, prm[:, C_GFFN:C_GFFN + KT], ALU.add, ALU.mult)
                j = i - 2
                if j >= 0 and n_aux[j] > 1 and items[j][0] in NORMED + ROPED:
                    dve.wait_ge(s_fin, n_aux[j] - 1)
                if j >= 0 and items[j][0] in NORMED:
                    kind, h = items[j]
                    dst, m = (kT, TOK) if kind == "k" else (qT, LAT)
                    dve.wait_ge(s_aux_read, n_aux[j])
                    link(V.reciprocal(big[4][:, 0:m], big[4][:, 0:m]))
                    TT(dst[:, h, :], dst[:, h, :], big[4][:, 0:m], ALU.mult).then_inc(s_fin, 1)
                if j >= 0 and items[j][0] in ROPED:
                    kind, h = items[j]
                    c = big[4]
                    dve.wait_ge(s_aux_done, n_aux[j])
                    if kind == "rk":
                        TT(c[:, 0:CTX], ps[5][:, 0:CTX], rope_sb[:, TOK:TOK + CTX], ALU.mult)
                        TT(c[:, CTX:TOK], ps[4][:, :], rope_sb[:, TOK + CTX:2 * TOK], ALU.mult).then_inc(s_aux_read, 1)
                        dst, m = rkT, TOK
                    else:
                        TT(c[:, 0:LAT], ps[4][:, :], rope_sb[:, 2 * TOK + LAT:], ALU.mult).then_inc(s_aux_read, 1)
                        dst, m = rqT, LAT
                    dve.wait_ge(s_aux_read, n_aux[j])
                    TT(dst[:, h, :], dst[:, h, :], c[:, 0:m], ALU.add).then_inc(s_fin, 1)

            dve.wait_ge(s_abt, 1)
            v = [spw[:, j, :] for j in range(6)]
            ab = ps[6][:, 0:96].rearrange("p (c h) -> p c h", h=16)
            for d in range(2):
                TT(v[0][:, 24 * d:24 * d + 24].rearrange("p (c h) -> p c h", h=H), ab[:, :, 4 * d:4 * d + 4],
                   prm[:, C_DTB + 4 * d:C_DTB + 4 * d + 4].unsqueeze(1).to_broadcast([P, NC, H]), ALU.add)
            TS(v[0][:, 48:56], prm[:, C_RETL:C_RETL + 8], -1.0, None, ALU.mult)
            for l in range(LAYERS):
                a = C_LAY + l * L_W + L_AP
                last = TS(v[0][:, 56 + KT * l:56 + KT * (l + 1)], prm[:, a:a + KT], -1.0, None, ALU.mult)
            link(last)
            STT(v[1], v[0], -1.0, v[0], ALU.mult, ALU.max).then_inc(s_spa, 1)
            dve.wait_ge(s_spa, 1)
            dve.wait_ge(s_act, 8 + 2)
            link(TS(v[3], v[2], 2.0, None, ALU.add))
            link(V.reciprocal(v[3], v[3]))
            link(TT(v[3], v[3], v[2], ALU.mult))
            link(TT(v[4], v[3], v[3], ALU.mult))
            link(TS(v[5], v[4], 1.0 / 17, None, ALU.mult))
            for a in range(15, 1, -2):
                link(STT(v[5], v[5], 1.0 / a, v[4], ALU.add, ALU.mult))
            TS(v[1], v[0], 0.0, None, ALU.max)
            link(STT(v[5], v[5], 1.0, v[3], ALU.add, ALU.mult))
            link(STT(v[5], v[5], 2.0, v[1], ALU.mult, ALU.add))
            for d in range(2):
                last = STT(tok[:, 0, 24 * d:24 * d + 24].rearrange("p (c h) -> p c h", h=H),
                           v[5][:, 24 * d:24 * d + 24].rearrange("p (c h) -> p c h", h=H), -1.0,
                           gch[:, 4 * d:4 * d + 4].unsqueeze(1).to_broadcast([P, NC, H]), ALU.mult, ALU.mult)
            last.then_inc(s_g, 1)
            for l in range(LAYERS):
                a, b = C_LAY + l * L_W, v[5][:, 56 + KT * l:56 + KT * (l + 1)]
                TS(prm[:, a + L_C8:a + L_C8 + KT], b, -LRU_C, None, ALU.mult)
                TS(prm[:, a + L_N8:a + L_N8 + KT], b, LRU_C, None, ALU.mult)
            TS(lgc[:, :], v[5][:, 48:56], -1.0, None, ALU.mult).then_inc(s_lg, 1)
            dve.wait_ge(s_beta, 2)
            TS(tok[:, 2, :], tok[:, 1, :], -1.0, None, ALU.mult)
            for d in range(2):
                dve.wait_ge(s_dexp, d + 1)
                U = cst1[:, d, :].unsqueeze(1).to_broadcast([P, H, P])
                if d == 0:
                    TT(Dsum[:, :, :], rt[7][:, :, :], U, ALU.mult).then_inc(s_dec, 1)
                else:
                    link(TT(rt[7][:, :, :], rt[7][:, :, :], U, ALU.mult))
                    link(TT(Dsum[:, :, :], Dsum[:, :, :], rt[7][:, :, :], ALU.add))
            dve.wait_ge(s_cum, 1)
            link(CP(tok[:, 3, :], ps[7][:, 128:176]))
            TT(tok[:, 7, :], ps[7][:, 192:240], tok[:, 3, :], ALU.subtract).then_inc(s_Gc, 1)

            for j, (src, c) in enumerate(turned):
                dve.wait_ge(s_turn, j + 1)
                dst = {"k": ktok, "v": vtok, "rk": rktok}[src]
                CP(dst[:, c, :, :].rearrange("p h n -> p (h n)"), ps[j % 2][:, :]).then_inc(s_turned, 1)

            def add_rows(s, d, c, dst, bank):
                o = dst[:, :, c * P - CTX:(c + 1) * P - CTX]
                p = bank[:, :].rearrange("p (h n) -> p h n", h=H)
                return CP(o, p) if s < NCC + (NC - NCC) // 2 else TT(o, o, p, ALU.add)

            for s in range(NC):
                for d in range(2):
                    c, b = order[d][s], 4 * d
                    lat = slice(c * P - CTX, (c + 1) * P - CTX)
                    if c >= NCC:
                        if s > NCC:
                            dve.wait_ge(s_rod[d], s - NCC)
                        TT(rt[3 + d][:, :, :], rqT[:, :, lat], rt[5 + d][:, :, :], ALU.mult).then_inc(s_rqx[d], 1)
                        if d == 0:
                            dve.wait_ge(s_rqk, s - NCC + 1)
                            TT(rt[2][:, :, :], ps[b][:, :].rearrange("p (h n) -> p h n", h=H), Dsum[:, :, :],
                               ALU.mult).then_inc(s_rm, 1)
                        dve.wait_ge(s_rod[d], s - NCC + 1)
                        add_rows(s, d, c, oret, ps[b + 1]).then_inc(s_ro[d], 1)
                    if s < NC - 1:
                        dve.wait_ge(s_rkv[d], s + 1)
                        if s == 0:
                            CP(flat(retS[d]), ps[b + 2][:, :]).then_inc(s_rS[d], 1)
                        else:
                            for h in range(H):
                                last = STT(retS[d][:, h, :], retS[d][:, h, :], gch[:, 4 * d + h:4 * d + h + 1],
                                           ps[b + 2][:, h * P:(h + 1) * P], ALU.mult, ALU.add)
                            last.then_inc(s_rS[d], 1)

            I = ident[:, :].unsqueeze(1).to_broadcast([P, H, P])
            bank = lambda b: ps[b][:, :].rearrange("p (h n) -> p h n", h=H)

            def merge(dst, d, rows, lev, src):
                m = lmask[:, lev + 7 * (d ^ rows), :].unsqueeze(1).to_broadcast([P, H, P])
                return V.copy_predicated(dst[:, :, :], m, src)

            for s in range(NC):
                both = [(d, order[d][s], 4 * d, gt[d]) for d in range(2)]
                for d, c, b, t in both:
                    dve.wait_ge(s_rows[d], s + 1)
                    for h in range(H):
                        col = 24 * d + 4 * c + h
                        last = TS(t[0][:, h, :], ps[b][:, h * P:(h + 1) * P], tok[:, 3, col:col + 1], 0.0,
                                  ALU.subtract, ALU.min)
                    last.then_inc(s_dm[d], 1)
                    CP(t[2][:, :, :], I)
                    CP(t[3][:, :, :], I)
                for d, c, b, t in both:
                    dve.wait_ge(s_e[d], s + 1)
                    for h in range(H):
                        col = 24 * d + 4 * c + h
                        last = STT(t[1][:, h, :], ps[b + 1][:, h * P:(h + 1) * P], tok[:, 2, col:col + 1],
                                   t[0][:, h, :], ALU.mult, ALU.mult)
                    last.then_inc(s_na[d], 1)
                    if c >= NCC:
                        dve.wait_ge(s_na[d], s + 1)
                        link(TT(t[0][:, :, :], t[0][:, :, :], cst1[:, d, :].unsqueeze(1).to_broadcast([P, H, P]),
                                ALU.mult))
                        TT(t[5][:, :, :], bank(b + 2), t[0][:, :, :], ALU.mult)
                        dve.wait_ge(s_eg[d], s - NCC + 1)
                        TT(t[6][:, :, :], t[6][:, :, :], qT[:, :, c * P - CTX:(c + 1) * P - CTX], ALU.mult)
                for lev in range(7):
                    for d, c, b, t in both:
                        dve.wait_ge(s_gp[d], 7 * s + lev + 1)
                        if lev == 0:
                            dve.wait_ge(s_na[d], s + 1)
                            merge(t[3], d, 1, 0, t[1][:, :, :])
                        last = merge(t[2], d, 0, lev, bank(b + 1)) if lev < 6 else merge(t[3], d, 1, lev, bank(b + 1))
                        last.then_inc(s_gx[d], 1)
                for d, c, b, t in both:
                    dve.wait_ge(s_vp[d], s + 1)
                    for h in range(H):
                        col = 24 * d + 4 * c + h
                        last = TS(t[10][:, h, :], ps[b + 3][:, h * P:(h + 1) * P], tok[:, 1, col:col + 1], None,
                                  ALU.mult)
                    last.then_inc(s_vn[d], 1)
                for d, c, b, t in both:
                    if c >= NCC:
                        dve.wait_ge(s_god[d], s - NCC + 1)
                        add_rows(s, d, c, ogdn, ps[b + 2]).then_inc(s_go[d], 1)
                    if s < NC - 1:
                        dve.wait_ge(s_kv[d], s + 1)
                        for h in range(H):
                            col = 24 * d + 4 * c + h
                            if s == 0:
                                last = CP(t[11][:, h, :], ps[b + 3][:, h * P:(h + 1) * P])
                            else:
                                last = STT(t[11][:, h, :], t[11][:, h, :], tok[:, 6, col:col + 1],
                                           ps[b + 3][:, h * P:(h + 1) * P], ALU.mult, ALU.add)
                        last.then_inc(s_gS[d], 1)

            for h in range(H):
                dve.wait_ge(s_hsum, h + 1)
                TS(hn[:, h, :], ps[4 + h][:, :], -1.0 / P, None, ALU.mult).then_inc(s_hm, 1)
            for h in range(H):
                dve.wait_ge(s_hss, h + 1)
                dve.wait_ge(s_hm2, h + 1)
                STT(tmp[h][:, :], ps[h][:, :], 1.0 / P, hm[:, h, :], ALU.mult, ALU.subtract).then_inc(s_hvar, 1)
            for h in range(H):
                last = TT(oret[:, h, :], oret[:, h, :], hn[:, h, :], ALU.add)
            link(last)
            for j in range(2 * H + 1):
                if j < 2 * H:
                    src = (oret if j < H else ogdn)[:, j % H, :]
                    factor = tmp[j][:, :] if j < H else hq[:, j - H, :]
                    gate = (rgs if j < H else zs)[:, j % H, :]
                    gn = prm[:, C_RETG:C_RETG + 1] if j < H else prm[:, C_GDNG:C_GDNG + 1]
                    dve.wait_ge(s_hstd, j + 1)
                    link(TT(src, src, factor, ALU.mult))
                    STT(src, src, gn, gate, ALU.mult, ALU.mult).then_inc(s_yf, 1)
                if j:
                    before = (oret if j <= H else ogdn)[:, (j - 1) % H, :]
                    dve.wait_ge(s_yf, j)
                    dve.wait_ge(s_yh, j)
                    TT(acts[:, j - 1, 1, :], before, f32(acts[:, j - 1, 0, :]), ALU.subtract).then_inc(s_y, 1)

            done, sqx, stat, msq = Tally(), Tally(), Tally(), Tally()
            std, xhi, silu, hh, out_t, prod, pre, qadd, xn, var, xlo = (Tally() for _ in range(11))
            hid = Tally(1)

            def norm(seq, residual, ready, mean=True, g=None, b=None, keep=False):
                q = tmp[2][:, :]
                dve.wait_ge(s_dve, step.now)
                for i, k in enumerate([*seq, None]):
                    if k is not None:
                        ready(i)
                        residual(k).then_inc(s_pre, 1)
                        pre.up()
                    if i == 1:
                        dve.wait_ge(s_sqx, sqx.up())
                        CP(q, tmp[0][:, :]).then_inc(s_qadd, 1)
                        qadd.up()
                    elif i > 1:
                        dve.wait_ge(s_sqx, sqx.up())
                        dve.wait_ge(s_qadd, qadd.now)
                        TT(q, q, tmp[(i - 1) % 2][:, :], ALU.add).then_inc(s_qadd, 1)
                        qadd.up()
                r, nm = tmp[1][:, :], tmp[3][:, :]
                if mean:
                    dve.wait_ge(s_sum, msq.now + 1)
                    TS(nm, ps[seq[0]][:, :], -1.0 / D, None, ALU.mult).then_inc(s_nm, 1)
                dve.wait_ge(s_stat, stat.up())
                if mean:
                    dve.wait_ge(s_msq, msq.up())
                    STT(tmp[1][:, :], ps[seq[1]][:, :], 1.0 / D, tmp[0][:, :], ALU.mult, ALU.subtract).then_inc(s_var, 1)
                    var.up()
                dve.wait_ge(s_std, std.up())
                dve.wait_ge(s_pre, pre.now)
                if mean:
                    dve.wait_ge(s_var, var.now)
                    link(TT(nm, nm, r, ALU.mult))
                row = lambda k: tmp[2 + k % 2][:, :] if keep else X[:, k, :]
                for k in range(KT + 1):
                    if k < KT:
                        if keep and k > 1:
                            dve.wait_ge(s_xlo, xlo.now)
                        last = TT(row(k), X[:, k, :], r, ALU.mult)
                    if k:
                        if k < KT:
                            last.then_inc(s_dve, 1)
                        dve.wait_ge(s_xn, xn.now)
                        dve.wait_ge(s_xhi, xhi.up())
                        TT(acts[:, k - 1, 1, :], row(k - 1), f32(acts[:, k - 1, 0, :]), ALU.subtract).then_inc(s_xlo, 1)
                        xlo.up()
                    if k < KT:
                        if k == 0:
                            last.then_inc(s_dve, 1)
                        dve.wait_ge(s_dve, step.up())
                        if mean:
                            link(TT(row(k), row(k), nm, ALU.add))
                        TS(row(k), row(k), g(k), b(k) if b else None, ALU.mult,
                           *([ALU.add] if b else [])).then_inc(s_xn, 1)
                        xn.up()

            def chunk_ready(_):
                dve.wait_ge(s_done, done.up())

            def down_ready(i):
                if i < KT - 1:
                    dve.wait_ge(s_out, out_t.up())
                else:
                    dve.wait_ge(s_done, done.up())

            def hidden():
                with rounds(dve, FT // 2, (done, 4), (silu, 2), (prod, 2), (hh, 2), (hid, 2)) as i:
                    for j in range(2):
                        dve.wait_ge(s_hid, hid.now)
                        dve.wait_ge(s_silu, silu.up())
                        dve.wait_ge(s_done, done.up(2))
                        TT(tmp[1][:, :], tmp[0][:, :], ps[2 * j + 1][:, :], ALU.mult).then_inc(s_prod, 1)
                        dve.wait_ge(s_prod, 2 + prod.up())
                        dve.wait_ge(s_hh, hh.up())
                        TT(acts[:, bass.ds(i * 2 + (8 + j), 1), 1, :], tmp[1][:, :],
                           f32(acts[:, bass.ds(i * 2 + (8 + j), 1), 0, :]), ALU.subtract).then_inc(s_hid, 1)
                        hid.up()
                done.up(FT - 1)

            def modulated(part):
                return lambda k: STT(X[:, k, :], ps[k][:, :], mod[:, KT * part + k, 0:1], X[:, k, :],
                                     ALU.mult, ALU.add)

            done.up(N_HEAD)
            dve.wait_ge(s_xres, 16)
            norm(DOWN, modulated(2), chunk_ready, mean=False, keep=True,
                 g=lambda k: coef[:, 2, k:k + 1], b=lambda k: mod[:, 3 * KT + k, 0:1])
            hidden()
            norm(DOWN, modulated(5), down_ready, mean=False, g=lambda k: prm[:, C_FING + k:C_FING + k + 1])

            cs, yah, xr, xch, ybh, sig, ath, root, mg, mh, gelu = (Tally() for _ in range(11))
            yaf, xcf, m2, hg, merged = (Tally() for _ in range(5))
            ya, mlo = Tally(1), Tally(1)
            tallies = [(done, N_LAYER), (sqx, 24), (stat, 3), (msq, 3), (std, 3), (xhi, 24), (silu, 44), (hh, 44),
                       (out_t, 14), (prod, 44), (pre, 24), (qadd, 24), (xn, 24), (var, 3), (cs, KT), (yah, KT),
                       (xr, KT), (xch, KT), (ybh, KT), (sig, H), (ath, KT), (root, KT), (mg, 2 * KT), (mh, KT),
                       (gelu, KT), (yaf, KT), (xcf, KT), (m2, H), (hg, KT), (merged, KT), (ya, KT), (mlo, KT), (hid, 44),
                       (xlo, 24), (step, LAYER_STEPS)]

            def scaled_x():
                dve.wait_ge(s_xlo, xlo.now)
                for k in range(KT):
                    last = TS(X[:, k, :], X[:, k, :], ALPHA, None, ALU.mult)
                last.then_inc(s_dve, 1)
                step.up()

            def ln(j):
                c = lambda base: (lambda k: lay[:, base + KT * j + k:base + KT * j + k + 1])
                return dict(g=c(L_LNG), b=c(L_LNB))

            half = lambda k: STT(X[:, k, :], ps[k][:, :], 0.5, X[:, k, :], ALU.mult, ALU.add)
            whole = lambda k: TT(X[:, k, :], X[:, k, :], ps[k][:, :], ALU.add)
            with rounds(dve, LAYERS, *tallies) as l:
                link(CP(lay[:, :], prm[:, bass.ds(l * L_W + C_LAY, L_W)]))
                scaled_x()
                hidden()
                norm(DOWN, half, down_ready, **ln(0))
                scaled_x()

                par = lambda c: lay[:, c:c + 1]
                link(V.memset(mt[1][:, 0:2], 0.0))
                for f in range(KT):
                    b = 3 * (f % 2)
                    dve.wait_ge(s_cs, cs.up())
                    dve.wait_ge(s_done, done.up(2))
                    link(TT(mt[1][:, 2:LAT + 2], mt[0][:, 0:LAT], ps[b + 1][:, :], ALU.mult))
                    y = mt[2][:, 0:LAT]
                    link(TS(y, mt[1][:, 0:LAT], par(L_SC + f), None, ALU.mult))
                    for a in (1, 2):
                        link(STT(y, mt[1][:, a:LAT + a], par(L_SC + KT * a + f), y, ALU.mult, ALU.add))
                    dve.wait_ge(s_done, done.up())
                    dve.wait_ge(s_ya, ya.now)
                    TT(mt[3][:, 0:LAT], y, ps[b + 2][:, :], ALU.mult).then_inc(s_yaf, 1)
                    dve.wait_ge(s_yaf, yaf.up())
                    dve.wait_ge(s_yah, yah.up())
                    TT(acts[:, 8 + f, 1, :], mt[3][:, 0:LAT], f32(acts[:, 8 + f, 0, :]), ALU.subtract).then_inc(s_ya, 1)
                    ya.up()

                for j in range(2):
                    last = V.memset(mt[j][:, 0:3], 0.0)
                link(last)
                for h in range(H + 1):
                    for j in range(2):
                        f = 2 * h + j
                        if h < H:
                            dve.wait_ge(s_xr, xr.up())
                            y = mt[2 + j][:, 0:LAT]
                            link(TS(y, mt[j][:, 0:LAT], par(L_RC + f), par(L_RCB + f), ALU.mult, ALU.add))
                            for a in (1, 2, 3):
                                last = STT(y, mt[j][:, a:LAT + a], par(L_RC + KT * a + f), y, ALU.mult, ALU.add)
                                if a < 3:
                                    link(last)
                            last.then_inc(s_xcf, 1)
                            xcf.up()
                        if h and j == 0:
                            for i in range(2):
                                dve.wait_ge(s_root, root.up())
                                link(V.memset(mt[8 + i][:, 0:1], 1.0))
                                link(TT(mt[6 + i][:, 0:LAT], mt[6 + i][:, 0:LAT], mt[8 + i][:, 0:LAT], ALU.mult))
                                link(V.tensor_tensor_scan(mt[12 + i][:, 0:LAT], mt[10 + i][:, 0:LAT],
                                                          mt[6 + i][:, 0:LAT], 0.0, ALU.mult, ALU.add))
                                dve.wait_ge(s_gelu, gelu.up())
                                TT(mt[4 + i][:, 0:LAT], mt[12 + i][:, 0:LAT], mt[4 + i][:, 0:LAT],
                                   ALU.mult).then_inc(s_hg, 1)
                                hg.up()
                    if h < H:
                        dve.wait_ge(s_xcf, xcf.now)
                        for j in range(2):
                            dve.wait_ge(s_xch, xch.up())
                            TT(acts[:, 32 + j, 1, :], mt[2 + j][:, 0:LAT], f32(acts[:, 32 + j, 0, :]),
                               ALU.subtract).then_inc(s_xc, 1)
                    if h:
                        dve.wait_ge(s_hg, hg.now)
                        for j in range(2):
                            p = 16 + 2 * (h - 1) + j
                            dve.wait_ge(s_ybh, ybh.up())
                            TT(acts[:, p, 1, :], mt[4 + j][:, 0:LAT], f32(acts[:, p, 0, :]),
                               ALU.subtract).then_inc(s_yb, 1)
                    if h < H:
                        dve.wait_ge(s_sig, sig.up())
                        for j in range(2):
                            TT(mt[6 + j][:, 0:LAT], mt[6 + j][:, 0:LAT], mt[2 + j][:, 0:LAT], ALU.mult)
                        dve.wait_ge(s_ath, ath.up(2))
                        for j in range(2):
                            last = TT(mt[8 + j][:, 0:LAT], mt[10 + j][:, 0:LAT], mt[10 + j][:, 0:LAT], ALU.mult)
                        link(last)
                        for j in range(2):
                            last = STT(mt[8 + j][:, 0:LAT], mt[8 + j][:, 0:LAT], 1.0, mt[12 + j][:, 0:LAT],
                                       ALU.add, ALU.mult)
                        last.then_inc(s_m2, 1)
                        dve.wait_ge(s_m2, m2.up())
                done.up(5 * H)

                with rounds(dve, 4, (done, 8), (mg, 4), (merged, 2), (mh, 2), (mlo, 2), (step, 4)) as i:
                    for j in range(2):
                        dve.wait_ge(s_mg, mg.up())
                        link(TT(gates[j][0], gates[j][0], ps[4 * j][:, :], ALU.mult))
                        dve.wait_ge(s_mg, mg.up())
                    done.up(6)
                    for j in range(2):
                        dve.wait_ge(s_done, done.up())
                        link(TT(gates[j][1], gates[j][1], ps[4 * j + 2][:, :], ALU.mult))
                        dve.wait_ge(s_mlo, mlo.now)
                        TT(tmp[2 + j][:, :], gates[j][0], gates[j][1], ALU.add).then_inc(s_merge, 1)
                        dve.wait_ge(s_merge, 2 + merged.up())
                        dve.wait_ge(s_mh, mh.up())
                        p = i * 2 + (24 + j)
                        TT(acts[:, bass.ds(p, 1), 1, :], tmp[2 + j][:, :], f32(acts[:, bass.ds(p, 1), 0, :]),
                           ALU.subtract).then_inc(s_mlo, 1)
                        mlo.up()
                norm(range(KT), whole, chunk_ready, **ln(1))
                scaled_x()
                hidden()
                norm(DOWN, half, down_ready, **ln(2))


def program(nc, x_in, stream, params, consts, masks, rope, out):
    build(nc, x_in, stream, params, consts, masks, rope, out)


def _tiles(w):
    k, m = w.shape
    return w.reshape(k // P, P, m // P, P).transpose(2, 1, 0, 3).reshape(m // P, P, -1)


def _rows(w):
    return w.reshape(-1, P, w.shape[1])


def _feature_cols(v):
    return np.moveaxis(v.reshape(-1, P), 1, 0)


def _stream(a):
    out = np.zeros((N_STREAM, P, TILES * P), np.float32)
    at = [0]

    def put(chunks):
        n = len(chunks)
        out[at[0]:at[0] + n] = chunks
        at[0] += n

    def put_ffn(w1, w2):
        n = w1.shape[1] // 2
        put(np.stack([_tiles(w1[:, :n]), _tiles(w1[:, n:])], 1).reshape(2 * FT, P, -1))
        put(_rows(w2))

    parts = a["ada_w"][0].reshape(KT, P, PARTS, D).transpose(2, 0, 1, 3).reshape(PARTS * KT, P, D)
    put(parts[:2 * KT])
    parts = list(parts[2 * KT:])
    w = a["w_in"][0]
    W = H * P
    column = {"q": 0, "k": W, "v": 2 * W, "z": 3 * W}
    column |= {"rq": 4 * W + 16, "rk": 5 * W + 16, "rg": 7 * W + 16}
    for (kind, h), n in zip(ITEMS[:-1], N_BEHIND):
        c = column[kind] + h * P
        put(_tiles(w[:, c:c + P]))
        for _ in range(n):
            put(parts.pop(0)[None])
    gates = np.zeros((D, P), np.float32)
    gates[:, 0:16] = w[:, 4 * W:4 * W + 16]
    put(_tiles(gates))
    rv = w[:, 4 * W + 16 + 2 * W:4 * W + 16 + 3 * W]
    put(rv.reshape(4, 2, P, W).transpose(0, 2, 1, 3).reshape(4, P, -1))
    w = a["w_out"][0]
    put(_tiles(np.concatenate([w[W:], w[:W]]))[list(DOWN)])
    put_ffn(a["w_ffn_in"][0], a["w_ffn_out"][0])
    for l in range(LAYERS):
        put_ffn(a["ffn_w1_2"][l, 0], a["ffn_w2_2"][l, 0])
        b, c, v, xr, yr, ga, gb = (_tiles(a["w_in_2"][l][:, i * D:(i + 1) * D]) for i in range(7))
        put(np.stack([c, v, b], 1).reshape(3 * KT, P, -1))
        for h in range(H):
            put(xr[2 * h:2 * h + 2])
            put(yr[2 * h:2 * h + 2])
            g = a["rg_w_2"][l][:, h].reshape(2, 2, P, 2, P)
            put(g.transpose(2, 0, 3, 1, 4).reshape(1, P, -1))
        conv, rnn = _tiles(a["w_out_conv_2"][l]), _tiles(a["w_out_rnn_2"][l])
        for m in range(0, KT, 2):
            put(np.stack([conv[m], ga[m], gb[m], conv[m + 1], ga[m + 1], gb[m + 1], rnn[m], rnn[m + 1]]))
        put(_tiles(a["w_o_2"][l]))
        put_ffn(a["ffn_w1_2"][l, 1], a["ffn_w2_2"][l, 1])
    assert at[0] == N_CHUNKS
    return out


def _params(a):
    p = np.zeros((P, C_W), np.float32)

    def put(at, v):
        p[:, at:at + v.shape[1]] = v

    put(C_COND, np.stack([_feature_cols(a["c"][0]), _feature_cols(a["c_ctx"])], 2).reshape(P, -1))
    put(C_ADAB, _feature_cols(a["ada_b"][0]))
    put(C_GMIX, _feature_cols(a["norm_mix_g"][0]))
    put(C_GFFN, _feature_cols(a["norm_ffn_g"][0]))
    put(C_CONV, a["conv_w"][0].reshape(5, 12, P).transpose(2, 1, 0).reshape(P, -1))
    put(C_GDNG, a["gdn_norm_g"][0][:, None])
    put(C_RETG, a["ret_norm_g"][0][:, None])
    put(C_FING, _feature_cols(a["final_g"]))
    for at, name in ((C_DTB, "gdn_dt_bias"), (C_ALOG, "gdn_a_log"), (C_RETL, "ret_decay_logit")):
        put(at, np.broadcast_to(a[name][0].reshape(1, 8), (P, 8)))
    j = np.arange(P, dtype=np.float32)[:, None]
    put(C_UP, j)
    put(C_DOWN, P - 1 - j)
    for l in range(LAYERS):
        for at, name in ((L_SC, "sc_w_2"), (L_RC, "rc_w_2"), (L_RCB, "rc_b_2"), (L_RGB, "rg_b_2"),
                         (L_BM, "b_merge_2"), (L_LNG, "ln_g_2"), (L_LNB, "ln_b_2"), (L_AP, "a_param_2")):
            put(C_LAY + l * L_W + at, _feature_cols(a[name][l]))
    return p


def _constants():
    i = np.arange(P)
    U = (i[:, None] <= i[None, :]).astype(np.float32)
    rot = np.zeros((P, P), np.float32)
    rot[i[:64] + 64, i[:64]] = -1.0
    rot[i[:64], i[:64] + 64] = 1.0
    diff = (i[None, :] - i[:, None]).astype(np.float32)
    row = np.broadcast_to(i[None, :] + 1.0, (P, P)).astype(np.float32)
    consts = np.concatenate([np.eye(P, dtype=np.float32), np.ones((P, P), np.float32), U, U.T, rot,
                             row, row[:, ::-1], np.maximum(diff, 0), np.maximum(-diff, 0)], 1)
    masks = np.zeros((14, P, P), np.float32)
    for lev in range(7):
        s = 1 << lev
        same = i[:, None] // (2 * s) == i[None, :] // (2 * s)
        low = same & (i[:, None] // s % 2 == 1) & (i[None, :] // s % 2 == 0)
        masks[lev], masks[7 + lev] = low, low.T
    masks = masks.transpose(1, 0, 2).reshape(P, -1)

    def angles(pos, n):
        inv = np.float32(ROPE_THETA) ** (-np.arange(n, dtype=np.float32) / np.float32(n))
        return pos[:, None].astype(np.float32) * inv[None, :].astype(np.float32)

    t = np.arange(LAT)
    zero = np.zeros(CTX)
    ang = np.concatenate([angles(np.concatenate([np.arange(CTX), np.full(LAT, CTX)]), SEQ_PAIRS),
                          angles(np.concatenate([zero, t // GRID_W]), ROW_PAIRS),
                          angles(np.concatenate([zero, t % GRID_W]), COL_PAIRS)], 1)
    cos, sin = (np.tile(f(ang).T, (2, 1)).astype(np.float32) for f in (np.cos, np.sin))
    scale = np.float32(HSCALE)
    rope = np.concatenate([cos, sin, cos[:, CTX:] * scale, sin[:, CTX:] * scale], 1)
    return np.ascontiguousarray(consts), np.ascontiguousarray(masks), np.ascontiguousarray(rope)


def host_arrays(a):
    x = np.concatenate([a["ctx"][0], a["x"][0]], 0)
    consts, masks, rope = _constants()
    return {
        "x_in": np.ascontiguousarray(x.reshape(TOK, KT, P).transpose(2, 1, 0)),
        "stream": _stream(a),
        "params": _params(a),
        "consts": consts,
        "masks": masks,
        "rope": rope,
    }


def kernel(**inputs):
    import concourse.bacc as bacc
    from concourse.bass_utils import run_bass_kernel_spmd

    arrays = host_arrays({k: np.asarray(v) for k, v in inputs.items()})
    nc = bacc.Bacc("TRN2", target_bir_lowering=False, num_devices=1)
    args = [nc.dram_tensor(k, v.shape, mybir.dt.from_np(v.dtype), kind="ExternalInput").ap()
            for k, v in arrays.items()]
    args.append(nc.dram_tensor("out", (P, KT, LAT), F32, kind="ExternalOutput").ap())
    program(nc, *args)
    result = run_bass_kernel_spmd(nc, [arrays], core_ids=[0])
    out = np.asarray(result.results[0]["out"])
    return np.ascontiguousarray(out.transpose(2, 1, 0).reshape(1, LAT, D))
```

```python
from contextlib import ExitStack, contextmanager

import numpy as np

import concourse.bass as bass
from concourse import mybir

F32 = mybir.dt.float32
F32R = mybir.dt.float32r
U8 = mybir.dt.uint8
ALU = mybir.AluOpType
ACT = mybir.ActivationFunctionType

P = 128
D = 1024
KT = D // P
CTX, LAT = 256, 512
TOK = CTX + LAT
H = 4
NC = TOK // P
NCC = CTX // P
FF = 2816
FT = FF // P
LAYERS = 2
GRID_W, ROPE_THETA = 64, 10000.0
SEQ_PAIRS, ROW_PAIRS, COL_PAIRS = 16, 24, 24
EPS, LN_EPS = 1e-6, 1e-5
ALPHA = (2.0 * LAYERS) ** 0.25
LRU_C = 8.0
HSCALE = float(P) ** -0.5

TILES = 8
SLOTS, RAW = 4, 2
N_PROJ = 7 * H + 1 + H
PARTS = 6
N_HEAD = N_PROJ + PARTS * KT
N_B1 = N_HEAD + KT + 2 * FT + FT
N_LAYER = 2 * 3 * FT + 3 * KT + 5 * H + 4 * KT + KT
N_CHUNKS = N_B1 + LAYERS * N_LAYER
N_STREAM = N_CHUNKS + SLOTS
assert N_LAYER % SLOTS == 0
ADA_M = PARTS * KT

_o = 0


def _cols(n):
    global _o
    _o += n
    return _o - n


C_COND, C_ADAB, C_GMIX, C_GFFN = _cols(2 * KT), _cols(ADA_M), _cols(KT), _cols(KT)
C_CONV, C_GDNG, C_RETG, C_FING = _cols(12 * 5), _cols(1), _cols(1), _cols(KT)
C_DTB, C_ALOG, C_RETL = _cols(8), _cols(8), _cols(8)
C_UP, C_DOWN = _cols(1), _cols(1)
C_LAY = _o
L_SC, L_RC, L_RCB, L_RGB, L_BM, L_LNG, L_LNB, L_AP, L_C8, L_N8 = 0, 24, 56, 64, 80, 96, 120, 144, 152, 160
L_W = 168
C_W = C_LAY + LAYERS * L_W
LAYER_STEPS = 145
ITEMS = [(kind, h) for pair in (("k", "rk"), ("v", "rq"), ("q", "z"), ("rg",)) for h in range(H) for kind in pair]
ITEMS += [("ab", 0)]
BEHIND = (2, 1, 1, 1, 2, 1, 0)
N_BEHIND = [BEHIND[i % 7] if i // 7 + 2 < PARTS else 0 for i in range(len(ITEMS))]
TURNS = {i: i // 7 + 2 for i in range(len(ITEMS)) if i % 7 == 6 and i // 7 + 2 < PARTS}
assert sum(N_BEHIND) == (PARTS - 2) * KT
TAIL = 3
DOWN = (4, 5, 6, 7, 0, 1, 2, 3)
N_SP = NC * 8 + 8 + LAYERS * KT


class Tally:

    def __init__(self, start=0):
        self.base, self.k = start, 0

    def up(self, n=1):
        self.k += n
        return self.base + self.k

    @property
    def now(self):
        return self.base + self.k


@contextmanager
def rounds(engine, count, *pers):
    starts = [(t.base, t.k) for t, _ in pers]
    with engine.Fori(0, count) as i:
        for t, n in pers:
            t.base, t.k = i * n + (t.base + t.k), 0
        yield i
        for t, n in pers:
            assert t.k == n, (t.k, n)
    for (t, n), (base, k) in zip(pers, starts):
        t.base, t.k = base, k + count * n


def f32(ap):
    return ap.bitcast(F32)


def build(nc, x_in, stream, params, consts, masks, rope, out):
    ctx = ExitStack()
    with ctx:
        base = 16512
        KB = 1024

        def at(name, off, shape, dt=F32):
            return nc.alloc_sbuf_tensor_at(name, shape, dt, offset=base + off)

        h1 = at("h1", 0, [P, KT, 2, TOK], F32R)
        acts = at("acts", 0, [P, 34, 2, LAT], F32R)
        ktok = at("ktok", 0, [P, NC, H, P])
        vtok = at("vtok", 12 * KB, [P, NC, H, P])
        rktok = at("rktok", 24 * KB, [P, NC, H, P])
        oret = at("oret", 36 * KB, [P, H, LAT])
        retS = [at(f"retS{d}", (44 + 2 * d) * KB, [P, H, P]) for d in range(2)]
        xin = at("xin", 48 * KB, [P, KT, TOK])
        kT = at("kT", 48 * KB, [P, H, TOK])
        qT = at("qT", 60 * KB, [P, H, LAT])
        vfm = at("vfm", 68 * KB, [P, H, TOK])
        ogdn = at("ogdn", 68 * KB, [P, H, LAT])
        rqT = at("rqT", 80 * KB, [P, H, LAT])
        rkT = at("rkT", 88 * KB, [P, H, TOK])
        rvtok = at("rvtok", 100 * KB, [P, NC, H * P])
        zs = at("zs", 112 * KB, [P, H, LAT])
        rgs = at("rgs", 120 * KB, [P, H, LAT])
        rope_sb = at("rope_sb", 112 * KB, [P, 2 * TOK + 2 * LAT])
        lmask = at("lmask", 128 * KB, [P, 14, P], U8)
        masks_in = at("masks_in", 100 * KB, [P, 14 * P])
        cst1 = at("cst1", 130 * KB, [P, 3, P])
        Dsum = at("Dsum", 132 * KB, [P, H, P])
        tok = at("tok", 134 * KB, [P, 10, NC * 8])
        XO = 136 * KB
        X = at("X", XO, [P, KT, LAT])
        big = [at(f"big{i}", XO + i * 3104, [P, 776]) for i in range(5)]
        WO = XO + 16 * KB
        w_hi = at("w_hi", WO, [P, SLOTS, TILES, P], F32R)
        w_lo = at("w_lo", WO + 16 * KB, [P, SLOTS, TILES, P], F32R)
        raw = at("raw", WO + 32 * KB, [P, RAW, TILES, P])
        MO = WO + 40 * KB
        ident = at("ident", MO, [P, P])
        ones = at("ones", MO + 512, [P, P])
        prm = at("prm", MO + 1024, [P, C_W])
        lay = at("lay", MO + 1024 + 4 * C_W, [P, L_W])
        so = MO + 1024 + 4 * C_W + 4 * L_W
        csil = at("csil", so, [P, 2 * KT])
        mod = at("mod", so + 64, [P, ADA_M, 2])
        coef = at("coef", so + 64 + 8 * ADA_M, [P, 3, KT])
        lgc = at("lgc", so + 64 + 8 * ADA_M + 96, [P, 8])
        gch = at("gch", so + 64 + 8 * ADA_M + 128, [P, 8])
        zeta = at("zeta", so + 64 + 8 * ADA_M + 160, [P, 8])
        epsc = at("epsc", so + 64 + 8 * ADA_M + 192, [P, 8])
        cpart = at("cpart", so + 64 + 8 * ADA_M + 224, [P, 2, 2 * KT], F32R)
        to = (so + 64 + 8 * ADA_M + 224 + 16 * KT + 31) // 32 * 32
        tmp = [at(f"tmp{i}", to + i * 2 * KB, [P, LAT]) for i in range(4)]
        arow = at("arow", to, [P, KT * P])
        spw = at("spw", to + 8 * KB, [P, 6, N_SP])
        assert base + to + 8 * KB + 24 * N_SP <= 229344
        rt = [at(f"rt{i}", XO + i * 2 * KB, [P, H, P]) for i in range(8)]
        zt = [at(f"zt{d}", to + d * 2 * KB, [P, H, P]) for d in range(2)]
        gt = [[rt[4 * d + i] for i in range(4)]
              + [at(f"gt{d}{i}", (80 + 16 * d + 2 * i) * KB, [P, H, P]) for i in range(8)] for d in range(2)]
        second = [[at(f"second{d}{i}", (24 + 6 * d + 2 * i) * KB, [P, H, P]) for i in range(3)] for d in range(2)]
        gts = [gt, [[g[0], z[0], g[2], z[1], *g[4:6], z[2], *g[7:]] for g, z in zip(gt, second)]]
        hq = at("hq", 80 * KB, [P, H, LAT])
        hn = at("hn", 88 * KB, [P, H, LAT])
        hm = at("hm", 96 * KB, [P, H, LAT])
        MT = 96 * KB
        mt = [at(f"mt{i}", MT + i * 2080, [P, LAT + 3]) for i in range(15)]

        sg = at("sg", 128 * KB, [P, 2, LAT])

        ps = [ctx.enter_context(nc.psum_tensor(f"ps{i}", [P, 512], F32)) for i in range(8)]
        pair = lambda j: (acts[:, j, 0, :], acts[:, j, 1, :])

        def sem(name):
            return ctx.enter_context(nc.semaphore(name))


        s_Gc = sem("Gc")
        s_abt = sem("abt")
        s_acc = sem("acc")
        s_act = sem("act")
        s_arow = sem("arow")
        s_acol = sem("acol")
        s_part = sem("part")
        s_ath = sem("ath")
        s_aux_done = sem("aux_done")
        s_squares = sem("squares")
        s_row = sem("row")
        s_aux_read = sem("aux_read")
        s_beta = sem("beta")
        s_cdone = sem("cdone")
        s_cs = sem("cs")
        s_csil = sem("csil")
        s_cst = sem("cst")
        s_cum = sem("cum")
        s_dec = sem("dec")
        s_dexp = sem("dexp")
        s_dm = [sem(f"dm{d}") for d in range(2)]
        s_done = sem("done")
        s_dve = sem("dve")
        s_e = [sem(f"e{d}") for d in range(2)]
        s_eG = sem("eG")
        s_eg = [sem(f"eg{d}") for d in range(2)]
        s_eps = sem("eps")
        s_fin = sem("fin")
        s_g = sem("g")
        s_gS = [sem(f"gS{d}") for d in range(2)]
        s_gelu = sem("gelu")
        s_go = [sem(f"go{d}") for d in range(2)]
        s_god = [sem(f"god{d}") for d in range(2)]
        s_gp = [sem(f"gp{d}") for d in range(2)]
        s_gt = [sem(f"gt{d}") for d in range(2)]
        s_gx = [sem(f"gx{d}") for d in range(2)]
        s_gxt = [sem(f"gxt{d}") for d in range(2)]
        s_gy = [sem(f"gy{d}") for d in range(2)]
        s_gyc = [sem(f"gyc{d}") for d in range(2)]
        s_h1 = sem("h1")
        s_hg = sem("hg")
        s_hh = sem("hh")
        s_hhi = sem("hhi")
        s_hi = sem("hi")
        s_half = sem("half")
        s_hid = sem("hid")
        s_hm2 = sem("hm2")
        s_hrsq = sem("hrsq")
        s_hsum = sem("hsum")
        s_hm = sem("hm")
        s_hlog = sem("hlog")
        s_hsq = sem("hsq")
        s_hss = sem("hss")
        s_hstd = sem("hstd")
        s_hval = sem("hval")
        s_hvar = sem("hvar")
        s_kg = [sem(f"kg{d}") for d in range(2)]
        s_kv = [sem(f"kv{d}") for d in range(2)]
        s_lg = sem("lg")
        s_lo = sem("lo")
        s_m2 = sem("m2")
        s_merge = sem("merge")
        s_masks = sem("masks")
        s_mg = sem("mg")
        s_mh = sem("mh")
        s_mlo = sem("mlo")
        s_msq = sem("msq")
        s_na = [sem(f"na{d}") for d in range(2)]
        s_nwT = [sem(f"nwT{d}") for d in range(2)]
        s_out = sem("out")
        s_pre = sem("pre")
        s_pread = sem("pread")
        s_prm = sem("prm")
        s_prod = sem("prod")
        s_qadd = sem("qadd")
        s_rS = [sem(f"rS{d}") for d in range(2)]
        s_raw = [sem(f"raw{i}") for i in range(RAW)]
        s_res = sem("res")
        s_rkv = [sem(f"rkv{d}") for d in range(2)]
        s_rkz = [sem(f"rkz{d}") for d in range(2)]
        s_rm = sem("rm")
        s_ro = [sem(f"ro{d}") for d in range(2)]
        s_rod = [sem(f"rod{d}") for d in range(2)]
        s_root = sem("root")
        s_rope = sem("rope")
        s_qk = [sem(f"qk{d}") for d in range(2)]
        s_kk = [sem(f"kk{d}") for d in range(2)]
        s_rows = [sem(f"rows{d}") for d in range(2)]
        s_rqk = sem("rqk")
        s_rqx = [sem(f"rqx{d}") for d in range(2)]
        s_rv = sem("rv")
        s_sig = sem("sig")
        s_sil = sem("sil")
        s_silu = sem("silu")
        s_spa = sem("spa")
        s_sq = sem("sq")
        s_sqadd = sem("sqadd")
        s_sqx = sem("sqx")
        s_ss = sem("ss")
        s_stat = sem("stat")
        s_sum = sem("sum")
        s_sadd = sem("sadd")
        s_nm = sem("nm")
        s_std = sem("std")
        s_std0 = sem("std0")
        s_turn = sem("turn")
        s_turned = sem("turned")
        s_var = sem("var")
        s_vn = [sem(f"vn{d}") for d in range(2)]
        s_vp = [sem(f"vp{d}") for d in range(2)]
        s_wT = [sem(f"wT{d}") for d in range(2)]
        s_xc = sem("xc")
        s_xcf = sem("xcf")
        s_xch = sem("xch")
        s_xhi = sem("xhi")
        s_xin = sem("xin")
        s_xlo = sem("xlo")
        s_xn = sem("xn")
        s_xr = sem("xr")
        s_xres = sem("xres")
        s_y = sem("y")
        s_ya = sem("ya")
        s_yaf = sem("yaf")
        s_yah = sem("yah")
        s_yb = sem("yb")
        s_ybh = sem("ybh")
        s_yf = sem("yf")
        s_yh = sem("yh")

        items = ITEMS
        WHOLE, CONV, NORMED, ROPED = ("k", "v", "rk", "ab"), ("k", "v", "q"), ("k", "q"), ("rk", "rq")
        count = lambda kinds: [sum(k in kinds for k, _ in items[:i + 1]) for i in range(len(items))]
        n_aux, n_c, n_conv = count(NORMED + ROPED), count(CONV + ROPED), count(CONV)
        n_norm, n_rope = count(NORMED), count(ROPED)
        n_last_rope = max(i for i, (k, _) in enumerate(items) if k in ROPED)
        pbuf = lambda j: big[j % 2]
        cbuf = lambda j: big[2 + j % 2]
        turned = [(kind, c) for kind in ("v", "rk", "k") for c in range(NC)]
        zbuf = lambda d, s: rt[d] if s % 2 == 0 else zt[d]
        turn_bank = lambda j: (6, 7)[j % 2] if j < 2 * NC else (3, 7)[j % 2]
        order = (list(range(NC)), list(range(NCC))[::-1] + list(range(NCC, NC))[::-1])
        mats = tmp[3][:, :].rearrange("p (a n) -> p a n", a=4)

        gates = ((tmp[0][:, :], tmp[1][:, :]), (sg[:, 0, :], sg[:, 1, :]))

        block = ctx.enter_context(nc.Block())

        @block.sync
        def _(sp):
            sp.dma_start(prm[:, :], params).then_inc(s_prm, 16)

            def load_chunk(n, slot):
                sp.dma_start(raw[:, slot, :, :].rearrange("p k n -> p (k n)"),
                             stream[bass.ds(n, 1), :, :].rearrange("a p n -> (a p) n")).then_inc(s_raw[slot], 16)

            load_chunk(0, 0)
            load_chunk(1, 1)
            sp.dma_start(ident[:, :], consts[:, 0:P]).then_inc(s_cst, 16)
            sp.dma_start(ones[:, :], consts[:, P:2 * P]).then_inc(s_cst, 16)
            sp.dma_start(cst1[:, :, :].rearrange("p a n -> p (a n)"), consts[:, 2 * P:5 * P]).then_inc(s_cst, 16)
            split = Tally()
            body, shared = (N_STREAM - RAW) // RAW, 2 * KT // RAW
            for first, count in ((0, shared), (shared, 2), (shared + 2, body - shared - 2)):
                if first == shared + 2:
                    sp.dma_start(rope_sb[:, :], rope).then_inc(s_rope, 16)
                    sp.dma_start(masks_in[:, :], masks).then_inc(s_masks, 16)
                    sp.dma_start(tmp[3][:, :], consts[:, 5 * P:9 * P]).then_inc(s_masks, 16)
                with rounds(sp, count, (split, RAW)) as i:
                    for s in range(RAW):
                        sp.wait_ge(s_lo, split.up())
                        if first == 0:
                            sp.wait_ge(s_half, split.now)
                        load_chunk((i + first) * RAW + RAW + s, s)
            for n in range(RAW + body * RAW, N_STREAM):
                sp.wait_ge(s_lo, split.up())
                load_chunk(n, n % RAW)
            for k in range(KT):
                sp.wait_ge(s_xn, KT * (2 + 3 * LAYERS - 1) + k + 1)
                sp.dma_start(out[:, k, :], X[:, k, :]).then_inc(s_res, 16)
            sp.wait_ge(s_res, 16 * KT)

        @block.gpsimd
        def _(pool):
            hi = Tally()

            def low_part(slot, tiles=TILES):
                pool.wait_ge(s_hi, hi.up())
                nc.gpsimd.tensor_tensor(w_lo[:, slot, 0:tiles, :], raw[:, slot % RAW, 0:tiles, :],
                                        f32(w_hi[:, slot, 0:tiles, :]), ALU.subtract).then_inc(s_lo, 1)

            shared = 2 * KT // SLOTS
            with rounds(pool, shared, (hi, SLOTS)):
                for slot in range(SLOTS):
                    low_part(slot, TILES // 2)
            with rounds(pool, N_STREAM // SLOTS - shared, (hi, SLOTS)):
                for slot in range(SLOTS):
                    low_part(slot)
            for slot in range(N_STREAM % SLOTS):
                low_part(slot)

        @block.tensor
        def _(pe):
            mm = nc.tensor.matmul
            slot = [0]
            n_hi, n_lo = Tally(), Tally()

            def chunk(outs, ready=None):
                s = slot[0] % SLOTS
                slot[0] += 1
                pe.wait_ge(s_hi, n_hi.up())
                for k in range(TILES):
                    if ready:
                        ready(k)
                    for o, xh, xl, start, stop in outs(k):
                        mm(o, w_hi[:, s, k, :], xh, start=start, stop=False, skip_group_check=True)
                        mm(o, w_hi[:, s, k, :], xl, start=False, stop=False, skip_group_check=True)
                pe.wait_ge(s_lo, n_lo.up())
                for k in range(TILES):
                    for o, xh, xl, start, stop in outs(k):
                        last = mm(o, w_lo[:, s, k, :], xh, start=False, stop=stop, skip_group_check=True)
                last.then_inc(s_done, 1)

            def part_chunk(k, banks):
                sl = slot[0] % SLOTS
                slot[0] += 1
                pe.wait_ge(s_hi, n_hi.up())
                pe.wait_ge(s_lo, n_lo.up())
                if n_lo.now <= 2 * KT:
                    pe.wait_ge(s_half, n_lo.now)
                ch, cl = (cpart[:, a, 2 * k:2 * k + 2] for a in range(2))
                for half in range(2):
                    o = ps[banks[half]][0:2, :]
                    wh, wl = (w[:, sl, 4 * half:4 * half + 4, :].rearrange("p a n -> p (a n)") for w in (w_hi, w_lo))
                    mm(o, ch, wh, start=(k == 0), stop=False, skip_group_check=True)
                    mm(o, cl, wh, start=False, stop=False, skip_group_check=True)
                    last = mm(o, ch, wl, start=False, stop=(k == KT - 1), skip_group_check=True)
                last.then_inc(s_done, 1)

            def turn_part(part, bank):
                pe.wait_ge(s_arow, part + 1)
                for m in range(KT):
                    last = nc.tensor.transpose(ps[bank][:, 2 * m:2 * m + 2], arow[0:2, m * P:(m + 1) * P],
                                               ident[0:2, 0:2])
                last.then_inc(s_acol, 1)

            pe.wait_ge(s_csil, 3)
            for k in range(KT):
                part_chunk(k, (0, 1))
            for k in range(2):
                part_chunk(k, (2, 3))
            pe.wait_ge(s_cst, 48)
            pe.wait_ge(s_acc, 1)
            mm(ps[4][:, 0:CTX], ones[:, :], big[2][:, 0:CTX], start=True, stop=True)
            mm(ps[5][:, :], ones[:, :], big[2][:, CTX:TOK], start=True, stop=True).then_inc(s_ss, 1)
            turn_part(0, 6)
            for k in range(2, KT):
                part_chunk(k, (2, 3))
            turn_part(1, 7)

            part_k = 2 * KT
            for i, (kind, h) in enumerate(items + [(None, 0)] * 2):
                if kind:
                    if i >= 2:
                        pe.wait_ge(s_pread, i - 1)
                    L, C = ps[2 * (i % 2)], ps[2 * (i % 2) + 1]
                    s = slice(CTX, TOK)

                    def outs(k, whole=kind in WHOLE):
                        r = [(L[:, :], h1[:, k, 0, CTX:TOK], h1[:, k, 1, CTX:TOK], k == 0, k == KT - 1)]
                        if whole:
                            r.append((C[:, 0:CTX], h1[:, k, 0, 0:CTX], h1[:, k, 1, 0:CTX], k == 0, k == KT - 1))
                        return r

                    chunk(outs, ready=(lambda k: pe.wait_ge(s_h1, k + 1)) if i == 0 else None)
                    for _ in range(N_BEHIND[i]):
                        if part_k % KT == 0:
                            pe.wait_ge(s_part, part_k // KT)
                        part_chunk(part_k % KT, (6, 7))
                        part_k += 1
                    if i in TURNS:
                        turn_part(TURNS[i], 6)
                if i >= 2:
                    kind, h = items[i - 2]
                    j = i - 2
                    if kind in NORMED + ROPED:
                        if kind in NORMED:
                            pe.wait_ge(s_squares, n_norm[j])
                        else:
                            pe.wait_ge(s_row, n_rope[j])
                        if n_aux[j] >= 2:
                            pe.wait_ge(s_aux_read, n_aux[j] - 1)
                        w = ones[:, :] if kind in NORMED else cst1[:, 2, :]
                        src = cbuf(j) if kind in NORMED else pbuf(j)
                        if kind == "k":
                            mm(ps[5][:, 0:CTX], w, src[:, 0:CTX], start=True, stop=True)
                            last = mm(ps[4][:, :], w, src[:, CTX + 4:TOK + 4], start=True, stop=True)
                        elif kind == "rk":
                            mm(ps[5][:, 0:CTX], w, src[:, 0:CTX], start=True, stop=True)
                            last = mm(ps[4][:, :], w, src[:, CTX:TOK], start=True, stop=True)
                        else:
                            last = mm(ps[4][:, :], w, src[:, 0:LAT], start=True, stop=True)
                        last.then_inc(s_aux_done, 1)
                    if kind == "ab":
                        pe.wait_ge(s_pread, j + 1)
                        pe.wait_ge(s_part, PARTS)
                        for c in range(NC):
                            last = nc.tensor.transpose(ps[6][:, 16 * c:16 * c + 16],
                                                       pbuf(j)[0:16, c * P:(c + 1) * P], ident[0:16, 0:16])
                        last.then_inc(s_abt, 1)

            def turn(j):
                if j >= 2:
                    pe.wait_ge(s_turned, j - 1)
                src, c = turned[j]
                src = {"k": kT, "v": vfm, "rk": rkT}[src]
                for h in range(H):
                    last = nc.tensor.transpose(ps[turn_bank(j)][:, h * P:(h + 1) * P],
                                               src[:, h, c * P:(c + 1) * P], ident[:, :])
                last.then_inc(s_turn, 1)

            pe.wait_ge(s_pread, len(items))
            pe.wait_ge(s_aux_read, n_aux[len(items) - 1])
            for q in range(H):
                sl = slot[0] % SLOTS
                slot[0] += 1
                pe.wait_ge(s_hi, n_hi.up())
                pe.wait_ge(s_lo, n_lo.up())
                for t in range(NC):
                    for kk in range(2):
                        k = 2 * q + kk
                        wh = w_hi[:, sl, 4 * kk:4 * kk + 4, :].rearrange("p a n -> p (a n)")
                        wl = w_lo[:, sl, 4 * kk:4 * kk + 4, :].rearrange("p a n -> p (a n)")
                        xh, xl = (h1[:, k, a, t * P:(t + 1) * P] for a in range(2))
                        mm(ps[t][:, :], xh, wh, start=(k == 0), stop=False, skip_group_check=True)
                        mm(ps[t][:, :], xh, wl, start=False, stop=False, skip_group_check=True)
                        last = mm(ps[t][:, :], xl, wh, start=False, stop=(k == KT - 1), skip_group_check=True)
                    if t == NC - 1:
                        last.then_inc(s_done, 1)
                    if (q, t) == (1, 3):
                        pe.wait_ge(s_g, 1)
                        g = tok[:, 0, :]
                        mm(ps[7][:, 128:152], cst1[:, 0, :], g[:, 0:24], start=True, stop=True)
                        mm(ps[7][:, 152:176], cst1[:, 1, :], g[:, 24:48], start=True, stop=True)
                        mm(ps[7][:, 192:240], ones[:, :], g, start=True, stop=True).then_inc(s_cum, 1)
                    if q >= 2:
                        if (q, t) == (2, 0):
                            pe.wait_ge(s_fin, n_aux[-1])
                            pe.wait_ge(s_sil, 3 * H)
                            pe.wait_ge(s_eG, 1)
                        turn(NC * (q - 2) + t)
            pe.wait_ge(s_rv, NC)
            pe.wait_ge(s_turned, 2 * NC)


            for s in range(NC):
                for d in range(2):
                    c, b, n = order[d][s], 4 * d, 2 * s + d
                    cs = slice(c * P, (c + 1) * P)
                    lat = slice(c * P - CTX, (c + 1) * P - CTX)
                    if c >= NCC:
                        if d == 0:
                            if s > NCC:
                                pe.wait_ge(s_rm, s - NCC)
                            for h in range(H):
                                last = mm(ps[b][:, h * P:(h + 1) * P], rkT[:, h, cs], rqT[:, h, lat],
                                          start=True, stop=True)
                            last.then_inc(s_rqk, 1)
                            pe.wait_ge(s_rm, s - NCC + 1)
                        pe.wait_ge(s_rqx[d], s - NCC + 1)
                        if s > NCC:
                            pe.wait_ge(s_ro[d], s - NCC)
                        pe.wait_ge(s_rS[d], s)
                        for h in range(H):
                            o = ps[b + 1][:, h * P:(h + 1) * P]
                            last = mm(o, retS[d][:, h, :], rt[3 + d][:, h, :], start=True, stop=(d == 1))
                            if d == 0:
                                last = mm(o, rvtok[:, c, h * P:(h + 1) * P], rt[2][:, h, :], start=False, stop=True)
                        last.then_inc(s_rod[d], 1)
                    if s < NC - 1:
                        pe.wait_ge(s_rkz[d], s + 1)
                        if s:
                            pe.wait_ge(s_rS[d], s)
                        for h in range(H):
                            last = mm(ps[b + 2][:, h * P:(h + 1) * P], zbuf(d, s)[:, h, :],
                                      rvtok[:, c, h * P:(h + 1) * P], start=True, stop=True)
                        last.then_inc(s_rkv[d], 1)
                if s < NC // 2:
                    turn(2 * NC + 2 * s)
                    turn(2 * NC + 2 * s + 1)
            pe.wait_ge(s_turned, len(turned))
            pe.wait_ge(s_ro[1], 4)
            pe.wait_ge(s_ro[0], 4)
            pe.wait_ge(s_rS[0], NC - 1)
            pe.wait_ge(s_rS[1], NC - 1)

            def decay_rows(s):
                for d in range(2):
                    for h in range(H):
                        col = 24 * d + 4 * order[d][s] + h
                        last = mm(ps[4 * d + 3][:, h * P:(h + 1) * P], tok[:, 0, col:col + 1].to_broadcast([P, P]),
                                  cst1[:, d, :], start=True, stop=True)
                    last.then_inc(s_rows[d], 1)

            def key_products(s):
                for d in range(2):
                    c = order[d][s]
                    pe.wait_ge(s_dm[d], s + 1)
                    if c >= NCC:
                        pe.wait_ge(s_eg[d], s - NCC + 1)
                    for h in range(H):
                        keys = kT[:, h, c * P:(c + 1) * P]
                        last = mm(ps[4 * d + 3][:, h * P:(h + 1) * P], keys, keys, start=True, stop=True)
                    last.then_inc(s_kk[d], 1)

            def first_turn(s):
                for d in range(2):
                    pe.wait_ge(s_na[d], s + 1)
                    for h in range(H):
                        last = nc.tensor.transpose(ps[4 * d + 1][:, h * P:(h + 1) * P], gts[s % 2][d][1][:, h, :],
                                                   ident[:, :])
                    last.then_inc(s_gp[d], 1)

            decay_rows(0)
            key_products(0)
            first_turn(0)
            for s in range(NC):
                both = [(d, order[d][s], 4 * d, gts[s % 2][d]) for d in range(2)]
                for lev in range(1, 7):
                    for d, c, b, t in both:
                        E, NA, Xi, XT, Y = t[0:5]
                        pe.wait_ge(s_gx[d], 7 * s + lev)
                        for h in range(H):
                            last = mm(ps[b][:, h * P:(h + 1) * P], NA[:, h, :], Xi[:, h, :],
                                      start=True, stop=True)
                        last.then_inc(s_gy[d], 1)
                        if lev > 1:
                            if lev == 2 and s > NCC:
                                pe.wait_ge(s_go[d], s - NCC)
                            for h in range(H):
                                last = nc.tensor.transpose(ps[b + 2][:, h * P:(h + 1) * P], Xi[:, h, :],
                                                           ident[:, :])
                            last.then_inc(s_gt[d], 1)
                    if lev == 4 and s < NC - 1:
                        decay_rows(s + 1)
                    if lev == 5 and s < NC - 1:
                        key_products(s + 1)
                    for d, c, b, t in both:
                        if lev == 1 and c >= NCC:
                            pe.wait_ge(s_gS[d], s)
                            for h in range(H):
                                last = mm(ps[b + 3][:, h * P:(h + 1) * P], kT[:, h, c * P:(c + 1) * P],
                                          qT[:, h, c * P - CTX:(c + 1) * P - CTX], start=True, stop=True)
                            last.then_inc(s_qk[d], 1)
                    for d, c, b, t in both:
                        E, NA, Xi, XT, Y = t[0:5]
                        pe.wait_ge(s_gyc[d], 6 * s + lev)
                        if lev > 1:
                            pe.wait_ge(s_gxt[d], 5 * s + lev - 1)
                        for h in range(H):
                            if lev < 6:
                                last = mm(ps[b + 1][:, h * P:(h + 1) * P], XT[:, h, :], Y[:, h, :],
                                          start=True, stop=True)
                            else:
                                last = mm(ps[b + 1][:, h * P:(h + 1) * P], Y[:, h, :], XT[:, h, :],
                                          start=True, stop=True)
                        last.then_inc(s_gp[d], 1)
                for d, c, b, t in both:
                    XT, kG = t[3], t[8]
                    pe.wait_ge(s_gx[d], 7 * s + 7)
                    pe.wait_ge(s_kg[d], s + 1)
                    for h in range(H):
                        last = mm(ps[b][:, h * P:(h + 1) * P], kG[:, h, :], XT[:, h, :], start=True, stop=True)
                    last.then_inc(s_wT[d], 1)
                if s < NC - 1:
                    first_turn(s + 1)
                for d, c, b, t in both:
                    XT, nwT, S = t[3], t[7], t[11]
                    pe.wait_ge(s_nwT[d], s + 1)
                    if s:
                        pe.wait_ge(s_gS[d], s)
                    for h in range(H):
                        o = ps[b + 3][:, h * P:(h + 1) * P]
                        last = mm(o, XT[:, h, :], vtok[:, c, h, :], start=True, stop=(s == 0))
                        if s:
                            last = mm(o, nwT[:, h, :], S[:, h, :], start=False, stop=True)
                    last.then_inc(s_vp[d], 1)
                for d, c, b, t in both:
                    QK, qd, kd, vn, S = t[5], t[6], t[9], t[10], t[11]
                    pe.wait_ge(s_vn[d], s + 1)
                    if c >= NCC:
                        for h in range(H):
                            o = ps[b + 2][:, h * P:(h + 1) * P]
                            mm(o, S[:, h, :], qd[:, h, :], start=True, stop=False)
                            last = mm(o, vn[:, h, :], QK[:, h, :], start=False, stop=True)
                        last.then_inc(s_god[d], 1)
                    if s < NC - 1:
                        for h in range(H):
                            last = mm(ps[b + 3][:, h * P:(h + 1) * P], kd[:, h, :], vn[:, h, :],
                                      start=True, stop=True)
                        last.then_inc(s_kv[d], 1)

            pe.wait_ge(s_go[0], 4)
            pe.wait_ge(s_go[1], 4)
            for h in range(H):
                mm(ps[4 + h][:, :], ones[:, :], oret[:, h, :], start=True, stop=True).then_inc(s_hsum, 1)
            for h in range(H):
                pe.wait_ge(s_hrsq, h + 1)
                mm(ps[h][:, :], ones[:, :], tmp[h][:, :], start=True, stop=True).then_inc(s_hss, 1)
            for h in range(H):
                pe.wait_ge(s_hvar, h + 1)
                pe.wait_ge(s_hsq, h + 1)
                mm(ps[h][:, :], ones[:, :], hq[:, h, :], start=True, stop=True).then_inc(s_hss, 1)

            n_pre, n_q, n_x, n_prod, n_hid = Tally(), Tally(), Tally(), Tally(), Tally(1)
            n_s, n_sq = Tally(), Tally()

            def x_outs(bank, wait=None):
                return lambda k: [(bank[:, :], *pair(k), k == 0, k == KT - 1)]

            def opening(banks, high, low, n, first=0):
                slots = [(slot[0] + j) % SLOTS for j in range(SLOTS)]
                slot[0] += SLOTS
                part = lambda w, x: (lambda j, k: mm(
                    ps[banks[j]][:, :], w[:, slots[j], k, :], pair(first + k)[x],
                    start=(k == 0 and w is w_hi and x == 0), stop=(k == KT - 1 and x == 1), skip_group_check=True))
                high_high, high_low, low_high = part(w_hi, 0), part(w_hi, 1), part(w_lo, 0)
                late = 3
                for k in range(KT - 2):
                    pe.wait_ge(high, n.up())
                    for j in range(SLOTS):
                        if k == 0:
                            pe.wait_ge(s_hi, n_hi.up())
                        high_high(j, k)
                    if k >= late:
                        for j in range(SLOTS):
                            low_high(j, k)
                    pe.wait_ge(low, n.now)
                    for j in range(SLOTS):
                        high_low(j, k)
                    if k == late - 1:
                        for j in range(SLOTS):
                            pe.wait_ge(s_lo, n_lo.up())
                            for i in range(late):
                                low_high(j, i)
                for j in range(SLOTS):
                    for k in (KT - 2, KT - 1):
                        if j == 0:
                            pe.wait_ge(high, n.up())
                        high_high(j, k)
                        low_high(j, k)
                        if j == 0:
                            pe.wait_ge(low, n.now)
                        last = high_low(j, k)
                    last.then_inc(s_done, 1)

            def normed(seq, product, mean=True):
                for i in range(KT):
                    product(i, seq[i])
                    if i:
                        pe.wait_ge(s_pre, n_pre.up())
                pe.wait_ge(s_pre, n_pre.up())
                if mean:
                    mm(ps[seq[0]][:, :], ones[:, :], X[:, seq[KT - 1], :], start=True, stop=False,
                       skip_group_check=True)
                    pe.wait_ge(s_sadd, n_s.up(KT - 2))
                    mm(ps[seq[0]][:, :], ones[:, :], tmp[3][:, :], start=False, stop=True,
                       skip_group_check=True).then_inc(s_sum, 1)
                pe.wait_ge(s_sqx, n_sq.up(KT))
                mm(ps[seq[1]][:, :], ones[:, :], tmp[1][:, :], start=True, stop=False, skip_group_check=True)
                pe.wait_ge(s_qadd, n_q.up(KT - 1))
                mm(ps[seq[1]][:, :], ones[:, :], tmp[2][:, :], start=False, stop=True,
                   skip_group_check=True).then_inc(s_stat, 1)

            def ffn(mean=True):
                pe.wait_ge(s_prod, n_prod.up(2))
                opening((0, 1, 2, 3), s_xhi, s_xlo, n_x)
                with rounds(pe, FT // 2 - 1, (n_hi, 4), (n_lo, 4), (n_prod, 2)):
                    for j in range(2):
                        pe.wait_ge(s_prod, n_prod.up())
                        chunk(x_outs(ps[2 * j]))
                        chunk(x_outs(ps[2 * j + 1]))

                def down(k, seq, a):
                    s = slot[0] % SLOTS
                    slot[0] += 1
                    hh, hl = acts[:, 8 + k, 0, :] if isinstance(k, int) else acts[:, bass.ds(k + 8, 1), 0, :], \
                        acts[:, 8 + k, 1, :] if isinstance(k, int) else acts[:, bass.ds(k + 8, 1), 1, :]
                    pe.wait_ge(s_hid, n_hid.up())
                    pe.wait_ge(s_hi, n_hi.up())
                    for i, m in enumerate(seq):
                        if a and i == 4:
                            pe.wait_ge(s_prod, n_prod.now + 2)
                        mm(ps[m][:, :], w_hi[:, s, m, :], hh, start=a, stop=False, skip_group_check=True)
                        mm(ps[m][:, :], w_hi[:, s, m, :], hl, start=False, stop=False, skip_group_check=True)
                    pe.wait_ge(s_lo, n_lo.up())
                    for m in seq:
                        last = mm(ps[m][:, :], w_lo[:, s, m, :], hh, start=False, stop=False, skip_group_check=True)
                    last.then_inc(s_done, 1)

                seq = DOWN
                down(0, seq, True)
                down(1, seq, False)
                with rounds(pe, 4, (n_hi, 4), (n_lo, 4), (n_hid, 4)) as i:
                    for j in range(4):
                        down(i * 4 + (2 + j), seq, False)
                for k in range(18, FT - TAIL):
                    down(k, seq, False)
                slots = [(slot[0] + j) % SLOTS for j in range(TAIL)]
                slot[0] += TAIL
                pe.wait_ge(s_hid, n_hid.up(TAIL))
                pe.wait_ge(s_hi, n_hi.up(TAIL))
                pe.wait_ge(s_lo, n_lo.up(TAIL))

                def product(i, m):
                    for j, s in enumerate(slots):
                        hh, hl = pair(8 + FT - TAIL + j)
                        mm(ps[m][:, :], w_hi[:, s, m, :], hh, start=False, stop=False, skip_group_check=True)
                        mm(ps[m][:, :], w_hi[:, s, m, :], hl, start=False, stop=False, skip_group_check=True)
                        last = mm(ps[m][:, :], w_lo[:, s, m, :], hh, start=False, stop=(j == TAIL - 1),
                                  skip_group_check=True)
                    if i < KT - 1:
                        last.then_inc(s_out, 1)
                    else:
                        last.then_inc(s_done, TAIL)

                normed(seq, product, mean)

            n_y = Tally()

            def product(i, m):
                if i == 0:
                    opening(DOWN[:4], s_yh, s_y, n_y)
                elif i >= SLOTS:
                    chunk(x_outs(ps[m]))

            normed(DOWN, product, mean=False)
            ffn(mean=False)

            n_mix = {q: Tally() for q in ("xc", "yb", "merge", "half", "gate")}
            n_mix["ya"], n_mix["mlo"] = Tally(1), Tally(1)
            tallies = [(n_hi, N_LAYER), (n_lo, N_LAYER), (n_pre, 24), (n_q, 21), (n_s, 18), (n_sq, 24), (n_x, 24), (n_prod, 44),
                       (n_hid, 44), (n_mix["ya"], KT), (n_mix["xc"], KT), (n_mix["yb"], KT),
                       (n_mix["merge"], KT), (n_mix["half"], H), (n_mix["gate"], KT), (n_mix["mlo"], KT)]
            with rounds(pe, LAYERS, *tallies):
                ffn()
                opening((0, 1, 2, 3), s_xhi, s_xlo, n_x)
                for f in range(1, KT):
                    b = 3 * (f % 2)
                    if f >= 2:
                        pe.wait_ge(s_ya, n_mix["ya"].up())
                    for j in range(f == 1, 3):
                        chunk(x_outs(ps[b + j]))
                n_mix["ya"].up(2)
                for h in range(H):
                    if h == 0:
                        pe.wait_ge(s_ya, n_mix["ya"].now)
                    if h:
                        pe.wait_ge(s_gelu, n_mix["gate"].up(2))
                    for j in range(4):
                        chunk(x_outs(ps[j]))
                    if h:
                        pe.wait_ge(s_sig, n_mix["half"].up())
                    pe.wait_ge(s_xc, n_mix["xc"].up(2))

                    def gate_outs(t):
                        g, m, k = t // 4, (t // 2) % 2, t % 2
                        return [(ps[4 + 2 * g + m][:, :], *pair(32 + k), k == 0, k == 1)]

                    chunk(gate_outs)
                n_mix["gate"].up(2)
                n_mix["half"].up(1)
                banks_read = (n_mix["gate"].now, n_mix["half"].now)
                ready = n_mix["yb"].up(KT)
                with rounds(pe, 4, (n_hi, 8), (n_lo, 8), (n_mix["merge"], 2)):
                    for j in range(2):
                        if j == 0:
                            pe.wait_ge(s_ya, n_mix["ya"].now)
                            pe.wait_ge(s_gelu, banks_read[0])
                            pe.wait_ge(s_sig, banks_read[1])
                        pe.wait_ge(s_merge, n_mix["merge"].up())
                        b = 4 * j
                        chunk(lambda k: [(ps[b][:, :], *pair(8 + k), k == 0, k == KT - 1)])
                        chunk(x_outs(ps[b + 1]))
                        chunk(x_outs(ps[b + 3]))
                    for b in (0, 4):
                        if b == 0:
                            pe.wait_ge(s_yb, ready)
                        chunk(lambda k: [(ps[b + 2][:, :], *pair(16 + k), k == 0, k == KT - 1)])
                pe.wait_ge(s_merge, n_mix["merge"].now + 1)

                def product(i, m):
                    if i == 0:
                        opening((0, 1, 2, 3), s_mh, s_mlo, n_mix["mlo"], first=24)
                    elif i >= SLOTS:
                        chunk(lambda k: [(ps[m][:, :], *pair(24 + k), k == 0, k == KT - 1)])

                normed(range(KT), product)
                ffn()

        @block.scalar
        def _(act):
            A = nc.scalar.activation
            step = Tally()

            def link(ins):
                ins.then_inc(s_act, 1)
                act.wait_ge(s_act, step.up())

            slot = [0]
            loaded, used = [Tally(), Tally()], Tally()

            def hi_part():
                s = slot[0] % SLOTS
                slot[0] += 1
                act.wait_ge(s_raw[s % RAW], loaded[s % RAW].up(16))
                A(w_hi[:, s, :, :], raw[:, s % RAW, :, :], ACT.Copy).then_inc(s_hi, 1)

            def done():
                act.wait_ge(s_done, used.up())
                hi_part()

            chunks = lambda n: ((used, n), (loaded[0], 8 * n), (loaded[1], 8 * n))

            act.wait_ge(s_prm, 16)
            A(csil[:, :], prm[:, C_COND:C_COND + 2 * KT], ACT.Silu).then_inc(s_csil, 1)
            act.wait_ge(s_csil, 1)
            A(cpart[:, 0, :], csil[:, :], ACT.Copy).then_inc(s_csil, 1)
            for n in range(SLOTS):
                hi_part()
                for k in (2 * n, 2 * n + 1):
                    act.dma_start(xin[:, k, :], x_in[:, k, :]).then_inc(s_xin, 16)
            act.wait_ge(s_xin, 16 * KT)
            for k in range(KT):
                if k >= 2:
                    act.wait_ge(s_sqadd, k - 1)
                A(big[k % 2][:, 0:TOK], xin[:, k, :], ACT.Square).then_inc(s_sq, 1)
                done()
            act.wait_ge(s_ss, 1)
            act.wait_ge(s_eps, 1)
            A(big[3][:, 0:CTX], ps[4][:, 0:CTX], ACT.Sqrt, scale=1.0 / D, bias=epsc[:, 0:1])
            A(big[3][:, CTX:TOK], ps[5][:, :], ACT.Sqrt, scale=1.0 / D, bias=epsc[:, 0:1]).then_inc(s_std0, 1)
            for _ in range(SLOTS + 1):
                done()
            for k in range(KT):
                if k in (2, 4, 6):
                    done()
                act.wait_ge(s_hval, k + 1)
                A(h1[:, k, 0, :], big[k % 2][:, 0:TOK], ACT.Copy).then_inc(s_hhi, 1)

            n = len(items)
            for i in range(n + 2):
                if i < n:
                    kind, h = items[i]
                    L, C = ps[2 * (i % 2)], ps[2 * (i % 2) + 1]
                    done()
                    if kind in CONV + ROPED + ("ab",):
                        b = pbuf(i)
                        if i >= 2:
                            act.wait_ge(s_cdone, n_c[i - 2])
                        if i >= 2 and items[i - 2][0] in ROPED:
                            act.wait_ge(s_aux_done, n_aux[i - 2])
                    if kind in CONV:
                        off, o2 = (2, CTX + 6) if kind != "q" else (2, 2)
                        if i == 0 or (kind == "q" and h == 0):
                            z = epsc[:, 2:4]
                            A(b[:, 0:2], z, ACT.Copy)
                            if kind != "q":
                                A(b[:, CTX + 2:CTX + 4], z, ACT.Copy)
                                A(b[:, CTX + 4:CTX + 6], z, ACT.Copy)
                                A(b[:, TOK + 6:TOK + 8], z, ACT.Copy)
                            else:
                                A(b[:, LAT + 2:LAT + 4], z, ACT.Copy)
                        if kind != "q":
                            A(b[:, 2:CTX + 2], C[:, 0:CTX], ACT.Copy)
                        A(b[:, o2:o2 + LAT], L[:, :], ACT.Copy).then_inc(s_pread, 1)
                    elif kind in ROPED:
                        if kind == "rk":
                            A(b[:, 0:CTX], C[:, 0:CTX], ACT.Copy)
                            link(A(b[:, CTX:TOK], L[:, :], ACT.Copy))
                        else:
                            link(A(b[:, 0:LAT], L[:, :], ACT.Copy))
                        act.sem_inc(s_pread, 1)
                        act.sem_inc(s_row, 1)
                    elif kind == "ab":
                        A(b[0:16, 0:CTX], C[0:16, 0:CTX], ACT.Copy)
                        A(b[0:16, CTX:TOK], L[0:16, :], ACT.Copy).then_inc(s_pread, 1)
                    else:
                        if kind == "z" and h == 0:
                            act.wait_ge(s_fin, n_aux[n_last_rope])
                        A((zs if kind == "z" else rgs)[:, h, :], L[:, :], ACT.Silu).then_inc(s_pread, 1)
                    for _ in range(N_BEHIND[i]):
                        done()
                j = i - 1
                if 0 <= j < n and items[j][0] in CONV:
                    kind, h = items[j]
                    act.wait_ge(s_cdone, n_c[j])
                    dst, c = {"k": kT, "q": qT, "v": vfm}[kind], cbuf(j)
                    segs = [(slice(0, LAT), slice(0, LAT))] if kind == "q" else \
                        [(slice(0, CTX), slice(0, CTX)), (slice(CTX, TOK), slice(CTX + 4, TOK + 4))]
                    for a, b in segs:
                        last = A(dst[:, h, a], c[:, b], ACT.Silu)
                    last.then_inc(s_sil, 1)
                    if kind in NORMED:
                        act.wait_ge(s_sil, n_conv[j])
                        for a, b in segs:
                            last = A(c[:, b], dst[:, h, a], ACT.Square)
                        last.then_inc(s_squares, 1)
                j = i - 2
                if 0 <= j < n and items[j][0] in NORMED:
                    kind, h = items[j]
                    act.wait_ge(s_aux_done, n_aux[j])
                    if n_aux[j] > 1:
                        act.wait_ge(s_fin, n_aux[j] - 1)
                    r = big[4]
                    if kind == "k":
                        A(r[:, 0:CTX], ps[5][:, 0:CTX], ACT.Sqrt, bias=epsc[:, 0:1])
                        last = A(r[:, CTX:TOK], ps[4][:, :], ACT.Sqrt, bias=epsc[:, 0:1])
                    else:
                        last = A(r[:, 0:LAT], ps[4][:, :], ACT.Sqrt, scale=float(P), bias=epsc[:, 1:2])
                    last.then_inc(s_aux_read, 1)
            act.wait_ge(s_spa, 1)
            link(A(spw[:, 2, :], spw[:, 1, :], ACT.Exp, scale=-1.0))
            link(A(gch[:, :], prm[:, C_ALOG:C_ALOG + 8], ACT.Exp))
            act.wait_ge(s_abt, 1)
            for d in range(2):
                A(tok[:, 1, 24 * d:24 * d + 24].rearrange("p (c h) -> p c h", h=H),
                  ps[6][:, 0:96].rearrange("p (c h) -> p c h", h=16)[:, :, 8 + 4 * d:12 + 4 * d],
                  ACT.Sigmoid).then_inc(s_beta, 1)
            act.wait_ge(s_lg, 1)
            A(gch[:, :], lgc[:, :], ACT.Exp, scale=float(P))
            A(zeta[:, 0:H], lgc[:, 0:H], ACT.Exp, scale=prm[:, C_DOWN:C_DOWN + 1])
            A(zeta[:, H:2 * H], lgc[:, H:2 * H], ACT.Exp, scale=prm[:, C_UP:C_UP + 1])
            act.wait_ge(s_masks, 32)
            for d in range(2):
                for h in range(H):
                    A(rt[5 + d][:, h, :], mats[:, d, :], ACT.Exp, scale=lgc[:, 4 * d + h:4 * d + h + 1])
            for d in range(2):
                if d:
                    act.wait_ge(s_dec, 1)
                for h in range(H):
                    last = A(rt[7][:, h, :], mats[:, 2 + d, :], ACT.Exp, scale=lgc[:, 4 * d + h:4 * d + h + 1])
                last.then_inc(s_dexp, 1)
            act.wait_ge(s_Gc, 1)
            A(tok[:, 4, :], tok[:, 3, :], ACT.Exp)
            A(tok[:, 5, :], tok[:, 7, :], ACT.Exp)
            A(tok[:, 6, :], ps[7][:, 192:240], ACT.Exp).then_inc(s_eG, 1)
            for _ in range(H):
                done()
            for t in range(NC):
                A(rvtok[:, t, :], ps[t][:, :], ACT.Copy).then_inc(s_rv, 1)
            act.wait_ge(s_turned, 2 * NC)

            for s in range(NC - 1):
                for d in range(2):
                    c = order[d][s]
                    if s > 1:
                        act.wait_ge(s_rkv[d], s - 1)
                    for h in range(H):
                        last = A(zbuf(d, s)[:, h, :], rktok[:, c, h, :], ACT.Copy, scale=zeta[:, 4 * d + h:4 * d + h + 1])
                    last.then_inc(s_rkz[d], 1)

            for d in range(2):
                act.wait_ge(s_ro[d], 4)
            act.wait_ge(s_turned, len(turned))
            for h in range(H):
                A(tmp[h][:, :], oret[:, h, :], ACT.Square).then_inc(s_hrsq, 1)

            def decays(s):
                for d in range(2):
                    t = gts[s % 2][d]
                    act.wait_ge(s_dm[d], s + 1)
                    A(t[0][:, :, :], t[0][:, :, :], ACT.Exp).then_inc(s_e[d], 1)
                for d in range(2):
                    t = gts[s % 2][d]
                    if order[d][s] >= NCC:
                        if s - 2 >= NCC:
                            act.wait_ge(s_god[d], s - 2 - NCC + 1)
                        A(t[6][:, :, :].rearrange("p h n -> p (h n)"), ps[4 * d + 3][:, :],
                          ACT.Exp).then_inc(s_eg[d], 1)

            decays(0)
            for s in range(NC):
                both = [(d, order[d][s], 4 * d, gts[s % 2][d]) for d in range(2)]
                for lev in range(1, 7):
                    if lev == 5 and s < NC - 1:
                        decays(s + 1)
                    for d, c, b, t in both:
                        act.wait_ge(s_gy[d], 6 * s + lev)
                        A(t[4][:, :, :].rearrange("p h n -> p (h n)"), ps[b][:, :], ACT.Copy).then_inc(s_gyc[d], 1)
                        if lev > 1:
                            act.wait_ge(s_gt[d], 5 * s + lev - 1)
                            A(t[3][:, :, :].rearrange("p h n -> p (h n)"), ps[b + 2][:, :],
                              ACT.Copy).then_inc(s_gxt[d], 1)
                    if lev < 5:
                        d, c, b, t = both[(lev - 1) // 2]
                        dst, factor = ((t[8], 4), (t[9], 5))[(lev - 1) % 2]
                        if s and lev % 2:
                            act.wait_ge(s_kv[d], s)
                        for h in range(H):
                            col = 24 * d + 4 * c + h
                            last = A(dst[:, h, :], ktok[:, c, h, :], ACT.Copy, scale=tok[:, factor, col:col + 1])
                        if lev % 2 == 0:
                            last.then_inc(s_kg[d], 1)
                for d, c, b, t in both:
                    act.wait_ge(s_wT[d], s + 1)
                    A(t[7][:, :, :].rearrange("p h n -> p (h n)"), ps[b][:, :], ACT.Copy,
                      scale=-1.0).then_inc(s_nwT[d], 1)
            for d in range(2):
                act.wait_ge(s_go[d], 4)

            act.dma_start(X[:, :, :], x_in[:, :, CTX:TOK]).then_inc(s_xres, 16)

            for h in range(H):
                A(hq[:, h, :], ogdn[:, h, :], ACT.Square).then_inc(s_hsq, 1)
            for h in range(H):
                act.wait_ge(s_hm, h + 1)
                A(hm[:, h, :], hn[:, h, :], ACT.Square).then_inc(s_hm2, 1)
            for j in range(2 * H):
                factor = tmp[j][:, :] if j < H else hq[:, j - H, :]
                if j < H:
                    act.wait_ge(s_hvar, j + 1)
                    A(factor, factor, ACT.Ln, bias=epsc[:, 0:1]).then_inc(s_hlog, 1)
                else:
                    act.wait_ge(s_hss, j + 1)
                    A(factor, ps[j - H][:, :], ACT.Ln, scale=1.0 / P, bias=epsc[:, 0:1]).then_inc(s_hlog, 1)
                if j % H == H - 1:
                    for i in range(j - H + 1, j + 1):
                        factor = tmp[i][:, :] if i < H else hq[:, i - H, :]
                        act.wait_ge(s_hlog, i + 1)
                        A(factor, factor, ACT.Exp, scale=-0.5).then_inc(s_hstd, 1)
            for j in range(2 * H):
                act.wait_ge(s_yf, j + 1)
                A(acts[:, j, 0, :], (oret if j < H else ogdn)[:, j % H, :], ACT.Copy).then_inc(s_yh, 1)

            pre, qadd, xn = Tally(), Tally(), Tally()
            stat, var, prod, nm = Tally(), Tally(), Tally(), Tally()

            def norm(seq, mean=True, keep=False, chunks_behind=0):
                A(epsc[:, 7:8], epsc[:, 0:1], ACT.Ln)
                for i, k in enumerate(seq):
                    if not chunks_behind:
                        done()
                    act.wait_ge(s_pre, pre.up())
                    if i >= 2:
                        act.wait_ge(s_qadd, qadd.up())
                    A(tmp[i % 2][:, :], X[:, k, :], ACT.Square).then_inc(s_sqx, 1)
                qadd.up(1)
                for _ in range(min(chunks_behind, RAW)):
                    done()
                if mean:
                    act.wait_ge(s_nm, nm.up())
                    A(tmp[0][:, :], tmp[3][:, :], ACT.Square).then_inc(s_msq, 1)
                act.wait_ge(s_stat, stat.up())
                if mean:
                    act.wait_ge(s_var, var.up())
                    link(A(tmp[1][:, :], tmp[1][:, :], ACT.Ln, bias=epsc[:, 4:5]))
                else:
                    link(A(tmp[1][:, :], ps[seq[1]][:, :], ACT.Ln, scale=1.0 / D, bias=epsc[:, 0:1]))
                A(tmp[1][:, :], tmp[1][:, :], ACT.Exp, scale=-0.5).then_inc(s_std, 1)
                for _ in range(chunks_behind - RAW):
                    done()
                for k in range(KT):
                    act.wait_ge(s_xn, xn.up())
                    A(acts[:, k, 0, :], (tmp[2 + k % 2][:, :] if keep else X[:, k, :]),
                      ACT.Copy).then_inc(s_xhi, 1)

            def ffn():
                with rounds(act, FT // 2, *chunks(4), (prod, 2)) as i:
                    for j in range(2):
                        done()
                        A(tmp[0][:, :], ps[2 * j][:, :], ACT.Silu).then_inc(s_silu, 1)
                        done()
                        act.wait_ge(s_prod, 2 + prod.up())
                        A(acts[:, bass.ds(i * 2 + (8 + j), 1), 0, :], tmp[1][:, :], ACT.Copy).then_inc(s_hh, 1)
                with rounds(act, 4, *chunks(SLOTS)):
                    for _ in range(SLOTS):
                        done()
                for _ in range(FT - TAIL - 4 * SLOTS):
                    done()

            norm(DOWN, mean=False, keep=True)
            ffn()
            norm(DOWN, mean=False, chunks_behind=TAIL)

            yaf, xcf, sig, m2, hg, yb, merge = (Tally() for _ in range(7))
            tallies = [*chunks(N_LAYER), (pre, 24), (qadd, 21), (xn, 24), (stat, 3), (var, 3), (nm, 3), (prod, 44),
                       (yaf, KT), (xcf, KT), (sig, H), (m2, H), (hg, KT), (yb, KT), (merge, KT), (step, 3)]
            with rounds(act, LAYERS, *tallies):
                ffn()
                norm(DOWN, chunks_behind=TAIL)
                for f in range(KT):
                    b = 3 * (f % 2)
                    done()
                    A(mt[0][:, 0:LAT], ps[b][:, :], ACT.Copy).then_inc(s_cs, 1)
                    done()
                    done()
                    act.wait_ge(s_yaf, yaf.up())
                    A(acts[:, 8 + f, 0, :], mt[3][:, 0:LAT], ACT.Copy).then_inc(s_yah, 1)

                def rows(h, j):
                    done()
                    A(mt[j][:, 3:LAT + 3], ps[j][:, :], ACT.Copy).then_inc(s_xr, 1)

                def split_rows():
                    for j in range(2):
                        act.wait_ge(s_xcf, xcf.up())
                        A(acts[:, 32 + j, 0, :], mt[2 + j][:, 0:LAT], ACT.Copy).then_inc(s_xch, 1)

                def split_h(h):
                    for j in range(2):
                        act.wait_ge(s_hg, hg.up())
                        A(acts[:, 16 + 2 * h + j, 0, :], mt[4 + j][:, 0:LAT], ACT.Copy).then_inc(s_ybh, 1)

                def roots():
                    act.wait_ge(s_m2, m2.up())
                    for j in range(2):
                        A(mt[8 + j][:, 0:LAT], mt[8 + j][:, 0:LAT], ACT.Sqrt).then_inc(s_root, 1)

                for h in range(H):
                    rows(h, 0)
                    if h:
                        roots()
                    rows(h, 1)
                    split_rows()
                    for j in range(2):
                        done()
                        if h and j == 0:
                            split_h(h - 1)
                        if h:
                            act.wait_ge(s_yb, yb.up())
                        A(mt[4 + j][:, 0:LAT], ps[2 + j][:, :], ACT.Gelu_apprx_tanh).then_inc(s_gelu, 1)
                    done()
                    for j in range(2):
                        f = 2 * h + j
                        A(mt[6 + j][:, 0:LAT], ps[4 + j][:, :], ACT.Sigmoid, bias=lay[:, L_RGB + f:L_RGB + f + 1])
                        last = A(mt[8 + j][:, 0:LAT], ps[6 + j][:, :], ACT.Sigmoid,
                                 bias=lay[:, L_RGB + KT + f:L_RGB + KT + f + 1])
                    last.then_inc(s_sig, 1)
                    act.wait_ge(s_sig, sig.up())
                    for j in range(2):
                        f = 2 * h + j
                        A(mt[10 + j][:, 0:LAT], mt[8 + j][:, 0:LAT], ACT.Exp, scale=lay[:, L_C8 + f:L_C8 + f + 1])
                        A(mt[12 + j][:, 0:LAT], mt[8 + j][:, 0:LAT], ACT.Tanh,
                          scale=lay[:, L_N8 + f:L_N8 + f + 1]).then_inc(s_ath, 1)
                roots()
                split_h(H - 1)
                yb.up(2)
                with rounds(act, 4, *chunks(8), (merge, 2)) as i:
                    for j in range(2):
                        b, m = 4 * j, i * 2 + j
                        done()
                        done()
                        A(gates[j][0], ps[b + 1][:, :], ACT.Sigmoid,
                          bias=lay[:, bass.ds(m + L_BM, 1)]).then_inc(s_mg, 1)
                        done()
                        A(gates[j][1], ps[b + 3][:, :], ACT.Sigmoid,
                          bias=lay[:, bass.ds(m + (L_BM + KT), 1)]).then_inc(s_mg, 1)
                    for j in range(2):
                        done()
                        act.wait_ge(s_merge, 2 + merge.up())
                        A(acts[:, bass.ds(i * 2 + (24 + j), 1), 0, :], tmp[2 + j][:, :], ACT.Copy).then_inc(s_mh, 1)
                norm(range(KT))
                ffn()
                norm(DOWN, chunks_behind=TAIL)

        @block.vector
        def _(dve):
            V = nc.vector
            TT, TS, STT, CP = V.tensor_tensor, V.tensor_scalar, V.scalar_tensor_tensor, V.tensor_copy
            step = Tally()

            def link(ins):
                ins.then_inc(s_dve, 1)
                dve.wait_ge(s_dve, step.up())

            flat = lambda t: t[:, :, :].rearrange("p h n -> p (h n)")

            for j, v in ((0, EPS), (1, P * EPS), (2, 0.0), (3, 0.0), (4, LN_EPS)):
                last = V.memset(epsc[:, j:j + 1], v)
            last.then_inc(s_eps, 1)
            dve.sem_inc(s_prod, 2)
            dve.sem_inc(s_merge, 2)
            for free in (s_hid, s_ya, s_mlo, s_mh):
                dve.sem_inc(free, 1)

            dve.wait_ge(s_csil, 2)
            TT(cpart[:, 1, :], csil[:, :], f32(cpart[:, 0, :]), ALU.subtract).then_inc(s_csil, 1)

            def half_low_part(n):
                dve.wait_ge(s_hi, n + 1)
                TT(w_lo[:, n % SLOTS, TILES // 2:, :], raw[:, n % RAW, TILES // 2:, :],
                   f32(w_hi[:, n % SLOTS, TILES // 2:, :]), ALU.subtract).then_inc(s_half, 1)

            for n in range(SLOTS):
                half_low_part(n)

            acc = big[2]
            for k in range(KT):
                dve.wait_ge(s_sq, k + 1)
                if k == 0:
                    CP(acc[:, 0:TOK], big[0][:, 0:TOK]).then_inc(s_sqadd, 1)
                else:
                    dve.wait_ge(s_sqadd, k)
                    TT(acc[:, 0:TOK], acc[:, 0:TOK], big[k % 2][:, 0:TOK], ALU.add).then_inc(s_sqadd, 1)
                half_low_part(SLOTS + k)
            dve.wait_ge(s_sqadd, KT)
            dve.sem_inc(s_acc, 1)
            def part_rows(part, chunks, banks):
                dve.wait_ge(s_done, chunks)
                for half in range(2):
                    last = CP(arow[0:2, half * 512:(half + 1) * 512], ps[banks[half]][0:2, :])
                last.then_inc(s_arow, 1)

            def part_cols(part, bank):
                dve.wait_ge(s_acol, part + 1)
                m = slice(KT * part, KT * (part + 1))
                TT(mod[:, m, :], ps[bank][:, 0:2 * KT].rearrange("p (m v) -> p m v", v=2),
                   prm[:, C_ADAB + KT * part:C_ADAB + KT * (part + 1)].unsqueeze(2).to_broadcast([P, KT, 2]),
                   ALU.add).then_inc(s_part, 1)
                dve.wait_ge(s_part, part + 1)

            dve.wait_ge(s_prm, 16)
            part_rows(0, KT, (0, 1))
            for n in range(2):
                half_low_part(SLOTS + KT + n)
            dve.wait_ge(s_std0, 1)
            link(V.reciprocal(big[3][:, 0:TOK], big[3][:, 0:TOK]))
            for n in range(2, 4):
                half_low_part(SLOTS + KT + n)
            for k in range(KT):
                if k == KT // 2:
                    part_cols(0, 6)
                    part_rows(1, 2 * KT, (2, 3))
                last = TT(xin[:, k, :], xin[:, k, :], big[3][:, 0:TOK], ALU.mult)
            link(last)
            part_cols(1, 7)
            for j in range(2):
                last = STT(coef[:, j, :], mod[:, KT:2 * KT, j], 1.0, prm[:, C_GMIX:C_GMIX + KT], ALU.add, ALU.mult)
            link(last)
            for k in range(KT + 1):
                b = big[k % 2]
                if k < KT:
                    if k > 1:
                        dve.wait_ge(s_h1, k - 1)
                    TS(b[:, 0:CTX], xin[:, k, 0:CTX], coef[:, 1, k:k + 1], mod[:, k, 1:2], ALU.mult, ALU.add)
                    TS(b[:, CTX:TOK], xin[:, k, CTX:TOK], coef[:, 0, k:k + 1], mod[:, k, 0:1], ALU.mult,
                       ALU.add).then_inc(s_hval, 1)
                if k:
                    dve.wait_ge(s_hval, k)
                    dve.wait_ge(s_hhi, k)
                    TT(h1[:, k - 1, 1, :], big[(k - 1) % 2][:, 0:TOK], f32(h1[:, k - 1, 0, :]),
                       ALU.subtract).then_inc(s_h1, 1)

            n, done_chunks = len(items), 2 * KT
            for i in range(n + 2):
                if i < n:
                    done_chunks += 1
                    if i in TURNS:
                        part_rows(TURNS[i], done_chunks - 1, (6, 7))
                    done_chunks += N_BEHIND[i]
                if i < n and items[i][0] in CONV + ROPED:
                    kind, h = items[i]
                    dve.wait_ge(s_pread, i + 1)
                    b, c = pbuf(i), cbuf(i)
                    if i >= 2 and items[i - 2][0] in NORMED + ROPED:
                        dve.wait_ge(s_aux_done, n_aux[i - 2])
                    if kind in CONV:
                        if i >= 2 and items[i - 2][0] in CONV:
                            dve.wait_ge(s_sil, n_conv[i - 2])
                        ct = {"q": 0, "k": 1, "v": 2}[kind] * H + h
                        w = [prm[:, C_CONV + 5 * ct + a:C_CONV + 5 * ct + a + 1] for a in range(5)]
                        m = LAT if kind == "q" else TOK + 4
                        link(TS(c[:, 0:m], b[:, 0:m], w[0], None, ALU.mult))
                        for a in range(1, 5):
                            last = STT(c[:, 0:m], b[:, a:m + a], w[a], c[:, 0:m], ALU.mult, ALU.add)
                            if a < 4:
                                link(last)
                        last.then_inc(s_cdone, 1)
                    else:
                        if (kind, h) == ("rk", 0):
                            dve.wait_ge(s_rope, 16)
                        dst, o, m = (rkT, 0, TOK) if kind == "rk" else (rqT, 2 * TOK, LAT)
                        TT(dst[:, h, :], b[:, 0:m], rope_sb[:, o:o + m], ALU.mult).then_inc(s_cdone, 1)
                if i == 3:
                    dve.wait_ge(s_masks, 32)
                    CP(lmask[:, :, :].rearrange("p a n -> p (a n)"), masks_in[:, :])
                if i in TURNS:
                    part_cols(TURNS[i], 6)
                    if TURNS[i] == 4:
                        STT(coef[:, 2, :], mod[:, 4 * KT:5 * KT, 0], 1.0, prm[:, C_GFFN:C_GFFN + KT], ALU.add, ALU.mult)
                j = i - 2
                if j >= 0 and n_aux[j] > 1 and items[j][0] in NORMED + ROPED:
                    dve.wait_ge(s_fin, n_aux[j] - 1)
                if j >= 0 and items[j][0] in NORMED:
                    kind, h = items[j]
                    dst, m = (kT, TOK) if kind == "k" else (qT, LAT)
                    dve.wait_ge(s_aux_read, n_aux[j])
                    link(V.reciprocal(big[4][:, 0:m], big[4][:, 0:m]))
                    TT(dst[:, h, :], dst[:, h, :], big[4][:, 0:m], ALU.mult).then_inc(s_fin, 1)
                if j >= 0 and items[j][0] in ROPED:
                    kind, h = items[j]
                    c = big[4]
                    dve.wait_ge(s_aux_done, n_aux[j])
                    if kind == "rk":
                        TT(c[:, 0:CTX], ps[5][:, 0:CTX], rope_sb[:, TOK:TOK + CTX], ALU.mult)
                        TT(c[:, CTX:TOK], ps[4][:, :], rope_sb[:, TOK + CTX:2 * TOK], ALU.mult).then_inc(s_aux_read, 1)
                        dst, m = rkT, TOK
                    else:
                        TT(c[:, 0:LAT], ps[4][:, :], rope_sb[:, 2 * TOK + LAT:], ALU.mult).then_inc(s_aux_read, 1)
                        dst, m = rqT, LAT
                    dve.wait_ge(s_aux_read, n_aux[j])
                    TT(dst[:, h, :], dst[:, h, :], c[:, 0:m], ALU.add).then_inc(s_fin, 1)

            dve.wait_ge(s_abt, 1)
            v = [spw[:, j, :] for j in range(6)]
            ab = ps[6][:, 0:96].rearrange("p (c h) -> p c h", h=16)
            for d in range(2):
                TT(v[0][:, 24 * d:24 * d + 24].rearrange("p (c h) -> p c h", h=H), ab[:, :, 4 * d:4 * d + 4],
                   prm[:, C_DTB + 4 * d:C_DTB + 4 * d + 4].unsqueeze(1).to_broadcast([P, NC, H]), ALU.add)
            TS(v[0][:, 48:56], prm[:, C_RETL:C_RETL + 8], -1.0, None, ALU.mult)
            for l in range(LAYERS):
                a = C_LAY + l * L_W + L_AP
                last = TS(v[0][:, 56 + KT * l:56 + KT * (l + 1)], prm[:, a:a + KT], -1.0, None, ALU.mult)
            link(last)
            STT(v[1], v[0], -1.0, v[0], ALU.mult, ALU.max).then_inc(s_spa, 1)
            dve.wait_ge(s_spa, 1)
            dve.wait_ge(s_act, 8 + 2)
            link(TS(v[3], v[2], 2.0, None, ALU.add))
            link(V.reciprocal(v[3], v[3]))
            link(TT(v[3], v[3], v[2], ALU.mult))
            link(TT(v[4], v[3], v[3], ALU.mult))
            link(TS(v[5], v[4], 1.0 / 17, None, ALU.mult))
            for a in range(15, 1, -2):
                link(STT(v[5], v[5], 1.0 / a, v[4], ALU.add, ALU.mult))
            TS(v[1], v[0], 0.0, None, ALU.max)
            link(STT(v[5], v[5], 1.0, v[3], ALU.add, ALU.mult))
            link(STT(v[5], v[5], 2.0, v[1], ALU.mult, ALU.add))
            for d in range(2):
                last = STT(tok[:, 0, 24 * d:24 * d + 24].rearrange("p (c h) -> p c h", h=H),
                           v[5][:, 24 * d:24 * d + 24].rearrange("p (c h) -> p c h", h=H), -1.0,
                           gch[:, 4 * d:4 * d + 4].unsqueeze(1).to_broadcast([P, NC, H]), ALU.mult, ALU.mult)
            last.then_inc(s_g, 1)
            for l in range(LAYERS):
                a, b = C_LAY + l * L_W, v[5][:, 56 + KT * l:56 + KT * (l + 1)]
                TS(prm[:, a + L_C8:a + L_C8 + KT], b, -LRU_C, None, ALU.mult)
                TS(prm[:, a + L_N8:a + L_N8 + KT], b, LRU_C, None, ALU.mult)
            TS(lgc[:, :], v[5][:, 48:56], -1.0, None, ALU.mult).then_inc(s_lg, 1)
            dve.wait_ge(s_beta, 2)
            TS(tok[:, 2, :], tok[:, 1, :], -1.0, None, ALU.mult)
            for d in range(2):
                dve.wait_ge(s_dexp, d + 1)
                U = cst1[:, d, :].unsqueeze(1).to_broadcast([P, H, P])
                if d == 0:
                    TT(Dsum[:, :, :], rt[7][:, :, :], U, ALU.mult).then_inc(s_dec, 1)
                else:
                    link(TT(rt[7][:, :, :], rt[7][:, :, :], U, ALU.mult))
                    link(TT(Dsum[:, :, :], Dsum[:, :, :], rt[7][:, :, :], ALU.add))
            dve.wait_ge(s_cum, 1)
            link(CP(tok[:, 3, :], ps[7][:, 128:176]))
            TT(tok[:, 7, :], ps[7][:, 192:240], tok[:, 3, :], ALU.subtract).then_inc(s_Gc, 1)

            def copy_turn(j):
                src, c = turned[j]
                dve.wait_ge(s_turn, j + 1)
                dst = {"k": ktok, "v": vtok, "rk": rktok}[src]
                CP(dst[:, c, :, :].rearrange("p h n -> p (h n)"), ps[turn_bank(j)][:, :]).then_inc(s_turned, 1)

            for j in range(2 * NC):
                copy_turn(j)

            def add_rows(s, d, c, dst, bank):
                o = dst[:, :, c * P - CTX:(c + 1) * P - CTX]
                p = bank[:, :].rearrange("p (h n) -> p h n", h=H)
                return CP(o, p) if s < NCC + (NC - NCC) // 2 else TT(o, o, p, ALU.add)

            for s in range(NC):
                for d in range(2):
                    c, b = order[d][s], 4 * d
                    lat = slice(c * P - CTX, (c + 1) * P - CTX)
                    if c >= NCC:
                        if s > NCC:
                            dve.wait_ge(s_rod[d], s - NCC)
                        TT(rt[3 + d][:, :, :], rqT[:, :, lat], rt[5 + d][:, :, :], ALU.mult).then_inc(s_rqx[d], 1)
                        if d == 0:
                            dve.wait_ge(s_rqk, s - NCC + 1)
                            TT(rt[2][:, :, :], ps[b][:, :].rearrange("p (h n) -> p h n", h=H), Dsum[:, :, :],
                               ALU.mult).then_inc(s_rm, 1)
                        dve.wait_ge(s_rod[d], s - NCC + 1)
                        add_rows(s, d, c, oret, ps[b + 1]).then_inc(s_ro[d], 1)
                    if s < NC - 1:
                        dve.wait_ge(s_rkv[d], s + 1)
                        if s == 0:
                            CP(flat(retS[d]), ps[b + 2][:, :]).then_inc(s_rS[d], 1)
                        else:
                            for h in range(H):
                                last = STT(retS[d][:, h, :], retS[d][:, h, :], gch[:, 4 * d + h:4 * d + h + 1],
                                           ps[b + 2][:, h * P:(h + 1) * P], ALU.mult, ALU.add)
                            last.then_inc(s_rS[d], 1)
                if s < NC // 2:
                    copy_turn(2 * NC + 2 * s)
                    copy_turn(2 * NC + 2 * s + 1)

            I = ident[:, :].unsqueeze(1).to_broadcast([P, H, P])
            bank = lambda b: ps[b][:, :].rearrange("p (h n) -> p h n", h=H)

            def merge(dst, d, rows, lev, src):
                m = lmask[:, lev + 7 * (d ^ rows), :].unsqueeze(1).to_broadcast([P, H, P])
                return V.copy_predicated(dst[:, :, :], m, src)

            def differences(s):
                for d in range(2):
                    dve.wait_ge(s_rows[d], s + 1)
                    for h in range(H):
                        col = 24 * d + 4 * order[d][s] + h
                        last = TS(gt[d][0][:, h, :], ps[4 * d + 3][:, h * P:(h + 1) * P], tok[:, 3, col:col + 1], 0.0,
                                  ALU.subtract, ALU.min)
                    last.then_inc(s_dm[d], 1)

            def negative_matrix(s):
                for d in range(2):
                    t = gts[s % 2][d]
                    CP(t[3][:, :, :], I)
                    dve.wait_ge(s_kk[d], s + 1)
                    dve.wait_ge(s_e[d], s + 1)
                    for h in range(H):
                        col = 24 * d + 4 * order[d][s] + h
                        last = STT(t[1][:, h, :], ps[4 * d + 3][:, h * P:(h + 1) * P], tok[:, 2, col:col + 1],
                                   t[0][:, h, :], ALU.mult, ALU.mult)
                    last.then_inc(s_na[d], 1)

            def first_level(s):
                for d in range(2):
                    t = gts[s % 2][d]
                    last = CP(t[2][:, :, :], I)
                    if d == 1:
                        link(last)
                for d in range(2):
                    t = gts[s % 2][d]
                    dve.wait_ge(s_gp[d], 7 * s + 1)
                    dve.wait_ge(s_na[d], s + 1)
                    merge(t[3], d, 1, 0, t[1][:, :, :])
                    merge(t[2], d, 0, 0, bank(4 * d + 1)).then_inc(s_gx[d], 1)

            differences(0)
            negative_matrix(0)
            first_level(0)
            for s in range(NC):
                both = [(d, order[d][s], 4 * d, gts[s % 2][d]) for d in range(2)]
                for lev in range(1, 7):
                    if lev == 4 and s < NC - 1:
                        differences(s + 1)
                    if lev == 5 and s < NC - 1:
                        negative_matrix(s + 1)
                    for d, c, b, t in both:
                        dve.wait_ge(s_gp[d], 7 * s + lev + 1)
                        last = merge(t[2], d, 0, lev, bank(b + 1)) if lev < 6 else merge(t[3], d, 1, lev, bank(b + 1))
                        last.then_inc(s_gx[d], 1)
                    for d, c, b, t in both:
                        if c >= NCC and lev == 1:
                            last = TT(t[0][:, :, :], t[0][:, :, :],
                                      cst1[:, d, :].unsqueeze(1).to_broadcast([P, H, P]), ALU.mult)
                            if d == 1:
                                link(last)
                        if c >= NCC and lev == 2:
                            dve.wait_ge(s_qk[d], s - NCC + 1)
                            TT(t[5][:, :, :], bank(b + 3), t[0][:, :, :], ALU.mult)
                        if c >= NCC and lev == 3:
                            dve.wait_ge(s_eg[d], s - NCC + 1)
                            TT(t[6][:, :, :], t[6][:, :, :], qT[:, :, c * P - CTX:(c + 1) * P - CTX], ALU.mult)
                if s < NC - 1:
                    first_level(s + 1)
                for d, c, b, t in both:
                    dve.wait_ge(s_vp[d], s + 1)
                    for h in range(H):
                        col = 24 * d + 4 * c + h
                        last = TS(t[10][:, h, :], ps[b + 3][:, h * P:(h + 1) * P], tok[:, 1, col:col + 1], None,
                                  ALU.mult)
                    last.then_inc(s_vn[d], 1)
                for d, c, b, t in both:
                    if c >= NCC:
                        dve.wait_ge(s_god[d], s - NCC + 1)
                        add_rows(s, d, c, ogdn, ps[b + 2]).then_inc(s_go[d], 1)
                    if s < NC - 1:
                        dve.wait_ge(s_kv[d], s + 1)
                        for h in range(H):
                            col = 24 * d + 4 * c + h
                            if s == 0:
                                last = CP(t[11][:, h, :], ps[b + 3][:, h * P:(h + 1) * P])
                            else:
                                last = STT(t[11][:, h, :], t[11][:, h, :], tok[:, 6, col:col + 1],
                                           ps[b + 3][:, h * P:(h + 1) * P], ALU.mult, ALU.add)
                        last.then_inc(s_gS[d], 1)

            for h in range(H):
                dve.wait_ge(s_hsum, h + 1)
                TS(hn[:, h, :], ps[4 + h][:, :], -1.0 / P, None, ALU.mult).then_inc(s_hm, 1)
            for h in range(H):
                dve.wait_ge(s_hss, h + 1)
                dve.wait_ge(s_hm2, h + 1)
                STT(tmp[h][:, :], ps[h][:, :], 1.0 / P, hm[:, h, :], ALU.mult, ALU.subtract).then_inc(s_hvar, 1)
            for h in range(H):
                last = TT(oret[:, h, :], oret[:, h, :], hn[:, h, :], ALU.add)
            link(last)
            for j in range(2 * H + 1):
                if j < 2 * H:
                    src = (oret if j < H else ogdn)[:, j % H, :]
                    factor = tmp[j][:, :] if j < H else hq[:, j - H, :]
                    gate = (rgs if j < H else zs)[:, j % H, :]
                    gn = prm[:, C_RETG:C_RETG + 1] if j < H else prm[:, C_GDNG:C_GDNG + 1]
                    dve.wait_ge(s_hstd, j + 1)
                    link(TT(src, src, factor, ALU.mult))
                    STT(src, src, gn, gate, ALU.mult, ALU.mult).then_inc(s_yf, 1)
                if j:
                    before = (oret if j <= H else ogdn)[:, (j - 1) % H, :]
                    dve.wait_ge(s_yf, j)
                    dve.wait_ge(s_yh, j)
                    TT(acts[:, j - 1, 1, :], before, f32(acts[:, j - 1, 0, :]), ALU.subtract).then_inc(s_y, 1)

            done, sqx, stat, msq = Tally(), Tally(), Tally(), Tally()
            std, xhi, silu, hh, out_t, prod, pre, qadd, sadd, xn, var, xlo = (Tally() for _ in range(12))
            hid = Tally(1)

            def norm(seq, residual, ready, mean=True, g=None, b=None, keep=False):
                q = tmp[2][:, :]
                dve.wait_ge(s_dve, step.now)
                for i, k in enumerate(seq):
                    ready(i)
                    residual(k).then_inc(s_pre, 1)
                    pre.up()
                    if i:
                        dve.wait_ge(s_sqx, sqx.up())
                        if i > 1:
                            dve.wait_ge(s_qadd, qadd.now)
                        (CP(q, tmp[0][:, :]) if i == 1 else
                         TT(q, q, tmp[(i - 1) % 2][:, :], ALU.add)).then_inc(s_qadd, 1)
                        qadd.up()
                    if mean:
                        if i > 1:
                            n = i - 1
                            if n > 1:
                                dve.wait_ge(s_sadd, sadd.now)
                            dve.wait_ge(s_pre, pre.now - 1)
                            (TT(tmp[3][:, :], X[:, seq[0], :], X[:, seq[1], :], ALU.add) if n == 1 else
                             TT(tmp[3][:, :], tmp[3][:, :], X[:, seq[n], :], ALU.add)).then_inc(s_sadd, 1)
                            sadd.up()
                sqx.up()
                r, nm = tmp[1][:, :], tmp[3][:, :]
                if mean:
                    dve.wait_ge(s_sum, msq.now + 1)
                    TS(nm, ps[seq[0]][:, :], -1.0 / D, None, ALU.mult).then_inc(s_nm, 1)
                dve.wait_ge(s_stat, stat.up())
                if mean:
                    dve.wait_ge(s_msq, msq.up())
                    STT(tmp[1][:, :], ps[seq[1]][:, :], 1.0 / D, tmp[0][:, :], ALU.mult, ALU.subtract).then_inc(s_var, 1)
                    var.up()
                centred = 0
                if mean:
                    dve.wait_ge(s_var, var.now)
                    centred = 4
                    for k in range(centred):
                        last = TT(X[:, k, :], X[:, k, :], nm, ALU.add)
                    link(last)
                dve.wait_ge(s_std, std.up())
                dve.wait_ge(s_pre, pre.now)
                row = lambda k: tmp[2 + k % 2][:, :] if keep else X[:, k, :]
                for k in range(KT + 1):
                    if k < KT:
                        if keep and k > 1:
                            dve.wait_ge(s_xlo, xlo.now)
                        if mean and k >= centred:
                            link(TT(X[:, k, :], X[:, k, :], nm, ALU.add))
                        last = TT(row(k), X[:, k, :], r, ALU.mult)
                    if k:
                        if k < KT:
                            last.then_inc(s_dve, 1)
                        dve.wait_ge(s_xn, xn.now)
                        dve.wait_ge(s_xhi, xhi.up())
                        TT(acts[:, k - 1, 1, :], row(k - 1), f32(acts[:, k - 1, 0, :]), ALU.subtract).then_inc(s_xlo, 1)
                        xlo.up()
                    if k < KT:
                        if k == 0:
                            last.then_inc(s_dve, 1)
                        dve.wait_ge(s_dve, step.up())
                        TS(row(k), row(k), g(k), b(k) if b else None, ALU.mult,
                           *([ALU.add] if b else [])).then_inc(s_xn, 1)
                        xn.up()

            def chunk_ready(_):
                dve.wait_ge(s_done, done.up())

            def down_ready(i):
                if i < KT - 1:
                    dve.wait_ge(s_out, out_t.up())
                else:
                    dve.wait_ge(s_done, done.up())

            def hidden():
                with rounds(dve, FT // 2, (done, 4), (silu, 2), (prod, 2), (hh, 2), (hid, 2)) as i:
                    for j in range(2):
                        dve.wait_ge(s_hid, hid.now)
                        dve.wait_ge(s_silu, silu.up())
                        dve.wait_ge(s_done, done.up(2))
                        TT(tmp[1][:, :], tmp[0][:, :], ps[2 * j + 1][:, :], ALU.mult).then_inc(s_prod, 1)
                        dve.wait_ge(s_prod, 2 + prod.up())
                        dve.wait_ge(s_hh, hh.up())
                        TT(acts[:, bass.ds(i * 2 + (8 + j), 1), 1, :], tmp[1][:, :],
                           f32(acts[:, bass.ds(i * 2 + (8 + j), 1), 0, :]), ALU.subtract).then_inc(s_hid, 1)
                        hid.up()
                done.up(FT - 1)

            def modulated(part):
                return lambda k: STT(X[:, k, :], ps[k][:, :], mod[:, KT * part + k, 0:1], X[:, k, :],
                                     ALU.mult, ALU.add)

            done.up(N_HEAD)
            dve.wait_ge(s_xres, 16)
            norm(DOWN, modulated(2), chunk_ready, mean=False, keep=True,
                 g=lambda k: coef[:, 2, k:k + 1], b=lambda k: mod[:, 3 * KT + k, 0:1])
            hidden()
            norm(DOWN, modulated(5), down_ready, mean=False, g=lambda k: prm[:, C_FING + k:C_FING + k + 1])

            cs, yah, xr, xch, ybh, sig, ath, root, mg, gelu = (Tally() for _ in range(10))
            yaf, xcf, m2, hg, merged = (Tally() for _ in range(5))
            ya, mlo, mh = Tally(1), Tally(1), Tally(1)
            tallies = [(done, N_LAYER), (sqx, 24), (stat, 3), (msq, 3), (std, 3), (xhi, 24), (silu, 44), (hh, 44),
                       (out_t, 14), (prod, 44), (pre, 24), (qadd, 21), (sadd, 18), (xn, 24), (var, 3), (cs, KT), (yah, KT),
                       (xr, KT), (xch, KT), (ybh, KT), (sig, H), (ath, KT), (root, KT), (mg, 2 * KT), (mh, KT),
                       (gelu, KT), (yaf, KT), (xcf, KT), (m2, H), (hg, KT), (merged, KT), (ya, KT), (mlo, KT), (hid, 44),
                       (xlo, 24), (step, LAYER_STEPS)]

            def scaled_x():
                dve.wait_ge(s_xlo, xlo.now)
                for k in range(KT):
                    last = TS(X[:, k, :], X[:, k, :], ALPHA, None, ALU.mult)
                last.then_inc(s_dve, 1)
                step.up()

            def ln(j):
                c = lambda base: (lambda k: lay[:, base + KT * j + k:base + KT * j + k + 1])
                return dict(g=c(L_LNG), b=c(L_LNB))

            half = lambda k: STT(X[:, k, :], ps[k][:, :], 0.5, X[:, k, :], ALU.mult, ALU.add)
            whole = lambda k: TT(X[:, k, :], X[:, k, :], ps[k][:, :], ALU.add)
            with rounds(dve, LAYERS, *tallies) as l:
                link(CP(lay[:, :], prm[:, bass.ds(l * L_W + C_LAY, L_W)]))
                scaled_x()
                hidden()
                norm(DOWN, half, down_ready, **ln(0))
                scaled_x()

                par = lambda c: lay[:, c:c + 1]
                link(V.memset(mt[1][:, 0:2], 0.0))
                for f in range(KT):
                    b = 3 * (f % 2)
                    dve.wait_ge(s_cs, cs.up())
                    dve.wait_ge(s_done, done.up(2))
                    link(TT(mt[1][:, 2:LAT + 2], mt[0][:, 0:LAT], ps[b + 1][:, :], ALU.mult))
                    y = mt[2][:, 0:LAT]
                    link(TS(y, mt[1][:, 0:LAT], par(L_SC + f), None, ALU.mult))
                    for a in (1, 2):
                        link(STT(y, mt[1][:, a:LAT + a], par(L_SC + KT * a + f), y, ALU.mult, ALU.add))
                    dve.wait_ge(s_done, done.up())
                    dve.wait_ge(s_ya, ya.now)
                    TT(mt[3][:, 0:LAT], y, ps[b + 2][:, :], ALU.mult).then_inc(s_yaf, 1)
                    dve.wait_ge(s_yaf, yaf.up())
                    dve.wait_ge(s_yah, yah.up())
                    TT(acts[:, 8 + f, 1, :], mt[3][:, 0:LAT], f32(acts[:, 8 + f, 0, :]), ALU.subtract).then_inc(s_ya, 1)
                    ya.up()

                for j in range(2):
                    last = V.memset(mt[j][:, 0:3], 0.0)
                link(last)
                for h in range(H + 1):
                    for j in range(2):
                        f = 2 * h + j
                        if h < H:
                            dve.wait_ge(s_xr, xr.up())
                            y = mt[2 + j][:, 0:LAT]
                            link(TS(y, mt[j][:, 0:LAT], par(L_RC + f), par(L_RCB + f), ALU.mult, ALU.add))
                            for a in (1, 2, 3):
                                last = STT(y, mt[j][:, a:LAT + a], par(L_RC + KT * a + f), y, ALU.mult, ALU.add)
                                if a < 3:
                                    link(last)
                            last.then_inc(s_xcf, 1)
                            xcf.up()
                        if h and j == 0:
                            for i in range(2):
                                dve.wait_ge(s_root, root.up())
                                link(V.memset(mt[8 + i][:, 0:1], 1.0))
                                link(TT(mt[6 + i][:, 0:LAT], mt[6 + i][:, 0:LAT], mt[8 + i][:, 0:LAT], ALU.mult))
                                link(V.tensor_tensor_scan(mt[12 + i][:, 0:LAT], mt[10 + i][:, 0:LAT],
                                                          mt[6 + i][:, 0:LAT], 0.0, ALU.mult, ALU.add))
                                dve.wait_ge(s_gelu, gelu.up())
                                TT(mt[4 + i][:, 0:LAT], mt[12 + i][:, 0:LAT], mt[4 + i][:, 0:LAT],
                                   ALU.mult).then_inc(s_hg, 1)
                                hg.up()
                    if h < H:
                        dve.wait_ge(s_xcf, xcf.now)
                        for j in range(2):
                            dve.wait_ge(s_xch, xch.up())
                            TT(acts[:, 32 + j, 1, :], mt[2 + j][:, 0:LAT], f32(acts[:, 32 + j, 0, :]),
                               ALU.subtract).then_inc(s_xc, 1)
                    if h:
                        dve.wait_ge(s_hg, hg.now)
                        for j in range(2):
                            p = 16 + 2 * (h - 1) + j
                            dve.wait_ge(s_ybh, ybh.up())
                            TT(acts[:, p, 1, :], mt[4 + j][:, 0:LAT], f32(acts[:, p, 0, :]),
                               ALU.subtract).then_inc(s_yb, 1)
                    if h < H:
                        dve.wait_ge(s_sig, sig.up())
                        for j in range(2):
                            TT(mt[6 + j][:, 0:LAT], mt[6 + j][:, 0:LAT], mt[2 + j][:, 0:LAT], ALU.mult)
                        dve.wait_ge(s_ath, ath.up(2))
                        for j in range(2):
                            last = TT(mt[8 + j][:, 0:LAT], mt[10 + j][:, 0:LAT], mt[10 + j][:, 0:LAT], ALU.mult)
                        link(last)
                        for j in range(2):
                            last = STT(mt[8 + j][:, 0:LAT], mt[8 + j][:, 0:LAT], 1.0, mt[12 + j][:, 0:LAT],
                                       ALU.add, ALU.mult)
                        last.then_inc(s_m2, 1)
                        dve.wait_ge(s_m2, m2.up())
                done.up(5 * H)

                with rounds(dve, 4, (done, 8), (mg, 4), (merged, 2), (mh, 2), (mlo, 2), (step, 4)) as i:
                    for j in range(2):
                        dve.wait_ge(s_mg, mg.up())
                        link(TT(gates[j][0], gates[j][0], ps[4 * j][:, :], ALU.mult))
                        dve.wait_ge(s_mg, mg.up())
                    done.up(6)
                    for j in range(2):
                        dve.wait_ge(s_done, done.up())
                        link(TT(gates[j][1], gates[j][1], ps[4 * j + 2][:, :], ALU.mult))
                        dve.wait_ge(s_mlo, mlo.now)
                        TT(tmp[2 + j][:, :], gates[j][0], gates[j][1], ALU.add).then_inc(s_merge, 1)
                        dve.wait_ge(s_merge, 2 + merged.up())
                        dve.wait_ge(s_mh, mh.up())
                        p = i * 2 + (24 + j)
                        TT(acts[:, bass.ds(p, 1), 1, :], tmp[2 + j][:, :], f32(acts[:, bass.ds(p, 1), 0, :]),
                           ALU.subtract).then_inc(s_mlo, 1)
                        mlo.up()
                norm(range(KT), whole, chunk_ready, **ln(1))
                scaled_x()
                hidden()
                norm(DOWN, half, down_ready, **ln(2))


def program(nc, x_in, stream, params, consts, masks, rope, out):
    build(nc, x_in, stream, params, consts, masks, rope, out)


def _tiles(w):
    k, m = w.shape
    return w.reshape(k // P, P, m // P, P).transpose(2, 1, 0, 3).reshape(m // P, P, -1)


def _rows(w):
    return w.reshape(-1, P, w.shape[1])


def _feature_cols(v):
    return np.moveaxis(v.reshape(-1, P), 1, 0)


def _stream(a):
    out = np.zeros((N_STREAM, P, TILES * P), np.float32)
    at = [0]

    def put(chunks):
        n = len(chunks)
        out[at[0]:at[0] + n] = chunks
        at[0] += n

    def put_ffn(w1, w2):
        n = w1.shape[1] // 2
        put(np.stack([_tiles(w1[:, :n]), _tiles(w1[:, n:])], 1).reshape(2 * FT, P, -1))
        put(_rows(w2))

    parts = a["ada_w"][0].reshape(KT, P, PARTS, D).transpose(2, 0, 1, 3).reshape(PARTS * KT, P, D)
    put(parts[:2 * KT])
    parts = list(parts[2 * KT:])
    w = a["w_in"][0]
    W = H * P
    column = {"q": 0, "k": W, "v": 2 * W, "z": 3 * W}
    column |= {"rq": 4 * W + 16, "rk": 5 * W + 16, "rg": 7 * W + 16}
    for (kind, h), n in zip(ITEMS[:-1], N_BEHIND):
        c = column[kind] + h * P
        put(_tiles(w[:, c:c + P]))
        for _ in range(n):
            put(parts.pop(0)[None])
    gates = np.zeros((D, P), np.float32)
    gates[:, 0:16] = w[:, 4 * W:4 * W + 16]
    put(_tiles(gates))
    rv = w[:, 4 * W + 16 + 2 * W:4 * W + 16 + 3 * W]
    put(rv.reshape(4, 2, P, W).transpose(0, 2, 1, 3).reshape(4, P, -1))
    w = a["w_out"][0]
    put(_tiles(np.concatenate([w[W:], w[:W]]))[list(DOWN)])
    put_ffn(a["w_ffn_in"][0], a["w_ffn_out"][0])
    for l in range(LAYERS):
        put_ffn(a["ffn_w1_2"][l, 0], a["ffn_w2_2"][l, 0])
        b, c, v, xr, yr, ga, gb = (_tiles(a["w_in_2"][l][:, i * D:(i + 1) * D]) for i in range(7))
        put(np.stack([c, v, b], 1).reshape(3 * KT, P, -1))
        for h in range(H):
            put(xr[2 * h:2 * h + 2])
            put(yr[2 * h:2 * h + 2])
            g = a["rg_w_2"][l][:, h].reshape(2, 2, P, 2, P)
            put(g.transpose(2, 0, 3, 1, 4).reshape(1, P, -1))
        conv, rnn = _tiles(a["w_out_conv_2"][l]), _tiles(a["w_out_rnn_2"][l])
        for m in range(0, KT, 2):
            put(np.stack([conv[m], ga[m], gb[m], conv[m + 1], ga[m + 1], gb[m + 1], rnn[m], rnn[m + 1]]))
        put(_tiles(a["w_o_2"][l]))
        put_ffn(a["ffn_w1_2"][l, 1], a["ffn_w2_2"][l, 1])
    assert at[0] == N_CHUNKS
    return out


def _params(a):
    p = np.zeros((P, C_W), np.float32)

    def put(at, v):
        p[:, at:at + v.shape[1]] = v

    put(C_COND, np.stack([_feature_cols(a["c"][0]), _feature_cols(a["c_ctx"])], 2).reshape(P, -1))
    put(C_ADAB, _feature_cols(a["ada_b"][0]))
    put(C_GMIX, _feature_cols(a["norm_mix_g"][0]))
    put(C_GFFN, _feature_cols(a["norm_ffn_g"][0]))
    put(C_CONV, a["conv_w"][0].reshape(5, 12, P).transpose(2, 1, 0).reshape(P, -1))
    put(C_GDNG, a["gdn_norm_g"][0][:, None])
    put(C_RETG, a["ret_norm_g"][0][:, None])
    put(C_FING, _feature_cols(a["final_g"]))
    for at, name in ((C_DTB, "gdn_dt_bias"), (C_ALOG, "gdn_a_log"), (C_RETL, "ret_decay_logit")):
        put(at, np.broadcast_to(a[name][0].reshape(1, 8), (P, 8)))
    j = np.arange(P, dtype=np.float32)[:, None]
    put(C_UP, j)
    put(C_DOWN, P - 1 - j)
    for l in range(LAYERS):
        for at, name in ((L_SC, "sc_w_2"), (L_RC, "rc_w_2"), (L_RCB, "rc_b_2"), (L_RGB, "rg_b_2"),
                         (L_BM, "b_merge_2"), (L_LNG, "ln_g_2"), (L_LNB, "ln_b_2"), (L_AP, "a_param_2")):
            put(C_LAY + l * L_W + at, _feature_cols(a[name][l]))
    return p


def _constants():
    i = np.arange(P)
    U = (i[:, None] <= i[None, :]).astype(np.float32)
    rot = np.zeros((P, P), np.float32)
    rot[i[:64] + 64, i[:64]] = -1.0
    rot[i[:64], i[:64] + 64] = 1.0
    diff = (i[None, :] - i[:, None]).astype(np.float32)
    row = np.broadcast_to(i[None, :] + 1.0, (P, P)).astype(np.float32)
    consts = np.concatenate([np.eye(P, dtype=np.float32), np.ones((P, P), np.float32), U, U.T, rot,
                             row, row[:, ::-1], np.maximum(diff, 0), np.maximum(-diff, 0)], 1)
    masks = np.zeros((14, P, P), np.float32)
    for lev in range(7):
        s = 1 << lev
        same = i[:, None] // (2 * s) == i[None, :] // (2 * s)
        low = same & (i[:, None] // s % 2 == 1) & (i[None, :] // s % 2 == 0)
        masks[lev], masks[7 + lev] = low, low.T
    masks = masks.transpose(1, 0, 2).reshape(P, -1)

    def angles(pos, n):
        inv = np.float32(ROPE_THETA) ** (-np.arange(n, dtype=np.float32) / np.float32(n))
        return pos[:, None].astype(np.float32) * inv[None, :].astype(np.float32)

    t = np.arange(LAT)
    zero = np.zeros(CTX)
    ang = np.concatenate([angles(np.concatenate([np.arange(CTX), np.full(LAT, CTX)]), SEQ_PAIRS),
                          angles(np.concatenate([zero, t // GRID_W]), ROW_PAIRS),
                          angles(np.concatenate([zero, t % GRID_W]), COL_PAIRS)], 1)
    cos, sin = (np.tile(f(ang).T, (2, 1)).astype(np.float32) for f in (np.cos, np.sin))
    scale = np.float32(HSCALE)
    rope = np.concatenate([cos, sin, cos[:, CTX:] * scale, sin[:, CTX:] * scale], 1)
    return np.ascontiguousarray(consts), np.ascontiguousarray(masks), np.ascontiguousarray(rope)


def host_arrays(a):
    x = np.concatenate([a["ctx"][0], a["x"][0]], 0)
    consts, masks, rope = _constants()
    return {
        "x_in": np.ascontiguousarray(x.reshape(TOK, KT, P).transpose(2, 1, 0)),
        "stream": _stream(a),
        "params": _params(a),
        "consts": consts,
        "masks": masks,
        "rope": rope,
    }


def kernel(**inputs):
    import concourse.bacc as bacc
    from concourse.bass_utils import run_bass_kernel_spmd

    arrays = host_arrays({k: np.asarray(v) for k, v in inputs.items()})
    nc = bacc.Bacc("TRN2", target_bir_lowering=False, num_devices=1)
    args = [nc.dram_tensor(k, v.shape, mybir.dt.from_np(v.dtype), kind="ExternalInput").ap()
            for k, v in arrays.items()]
    args.append(nc.dram_tensor("out", (P, KT, LAT), F32, kind="ExternalOutput").ap())
    program(nc, *args)
    result = run_bass_kernel_spmd(nc, [arrays], core_ids=[0])
    out = np.asarray(result.results[0]["out"])
    return np.ascontiguousarray(out.transpose(2, 1, 0).reshape(1, LAT, D))
```
